# Optimizing a Trainium2 kernel written in Bass

```python
import jax, jax.numpy as jnp
from jax import lax
import numpy as np

D_MODEL = 1024
BATCH = 1
SEQ = 512
DEPTH = 1
DEC_BATCH = 8
DEC_SEQ = 1
PAST_LEN = 2048
PAGE_SIZE = 128

SSD_EXPAND = 2
D_SSD = SSD_EXPAND * D_MODEL
SSD_HEAD_DIM = 64
SSD_HEADS = D_SSD // SSD_HEAD_DIM
SSD_GROUPS = 4
SSD_STATE = 128
CONV_WIDTH = 4
SSD_CHUNK = 128
D_XBC = D_SSD + 2 * SSD_GROUPS * SSD_STATE

ATT_HEAD_DIM = 64
ATT_SLOTS = 8
ATT_GROUPS = ((128, 1), (512, 4), (2048, 16))
N_ATT_GROUPS = 3
ATT_HEADS = ATT_SLOTS * N_ATT_GROUPS
D_ATT_QK = ATT_HEADS * ATT_HEAD_DIM
D_ATT = ATT_SLOTS * ATT_HEAD_DIM
ATT_SCALE = ATT_HEAD_DIM ** -0.5
ROPE_THETA = 10000.0
EPS = 1e-6

N_IN = D_SSD + D_XBC + SSD_HEADS + 3 * D_ATT_QK + D_ATT + 2 * D_MODEL

kernel_name = 'ssd_dilated_swa_gated_hybrid_step'

F32 = jnp.float32

def _split_points():
    sizes = [D_SSD, D_XBC, SSD_HEADS, D_ATT_QK, D_ATT_QK, D_ATT_QK, D_ATT, D_MODEL, D_MODEL]
    return [int(v) for v in np.cumsum(sizes)[:-1]]

def _rmsnorm(x, w):
    xf = x.astype(F32)
    y = xf * lax.rsqrt(jnp.mean(xf * xf, axis=-1, keepdims=True) + EPS)
    return (y * w.astype(F32)).astype(x.dtype)

def _rope(x, pos):
    half = x.shape[-1] // 2
    inv = ROPE_THETA ** (-jnp.arange(half, dtype=F32) / half)
    ang = pos.astype(F32)[:, None] * inv[None, :]
    cos = jnp.cos(ang)[None, :, None, :]
    sin = jnp.sin(ang)[None, :, None, :]
    xf = x.astype(F32)
    x1, x2 = xf[..., :half], xf[..., half:]
    return jnp.concatenate([x1 * cos - x2 * sin, x2 * cos + x1 * sin], axis=-1).astype(x.dtype)

def _causal_conv(xbc, conv_state, w, b):
    xp = jnp.concatenate([conv_state.astype(xbc.dtype), xbc], axis=1)
    out = lax.conv_general_dilated(xp, w[:, None, :].astype(xp.dtype), (1,), 'VALID',
                                   dimension_numbers=('NWC', 'WIO', 'NWC'),
                                   feature_group_count=xp.shape[-1])
    out = jax.nn.silu(out + b.astype(out.dtype))
    return out, xp[:, -(CONV_WIDTH - 1):]

def _ssd_chunked(x, dt, A, Bm, Cm, h0):
    b, T, H, P = x.shape
    G, N, Q = SSD_GROUPS, SSD_STATE, SSD_CHUNK
    E = H // G
    pad = (-T) % Q
    Tp = T + pad
    nc = Tp // Q
    xf = jnp.pad(x.astype(F32), ((0, 0), (0, pad), (0, 0), (0, 0)))
    dtp = jnp.pad(dt, ((0, 0), (0, pad), (0, 0)))
    Bc = jnp.pad(Bm.astype(F32), ((0, 0), (0, pad), (0, 0), (0, 0))).reshape(b, nc, Q, G, N)
    Cc = jnp.pad(Cm.astype(F32), ((0, 0), (0, pad), (0, 0), (0, 0))).reshape(b, nc, Q, G, N)
    xdt = (xf * dtp[..., None]).reshape(b, nc, Q, G, E, P)
    a = (dtp * A).reshape(b, nc, Q, G, E)
    acum = jnp.cumsum(a, axis=2)
    seg = acum[:, :, :, None] - acum[:, :, None, :]
    causal = jnp.tril(jnp.ones((Q, Q), dtype=bool))
    Lmat = jnp.exp(jnp.where(causal[:, :, None, None], seg, -jnp.inf))
    CB = jnp.einsum('bclgn,bcsgn->bclsg', Cc, Bc)
    y_diag = jnp.einsum('bclsg,bclsge,bcsgep->bclgep', CB, Lmat, xdt)
    decay_states = jnp.exp(acum[:, :, -1:] - acum)
    states = jnp.einsum('bclgn,bclge,bclgep->bcgepn', Bc, decay_states, xdt)
    chunk_decay = jnp.exp(acum[:, :, -1])

    def step(h, inp):
        s, dec = inp
        return dec[..., None, None] * h + s, h

    h_init = h0.astype(F32).reshape(b, G, E, P, N)
    h_final, h_prev = lax.scan(step, h_init, (jnp.moveaxis(states, 1, 0), jnp.moveaxis(chunk_decay, 1, 0)))
    h_prev = jnp.moveaxis(h_prev, 0, 1)
    y_off = jnp.einsum('bclgn,bcgepn,bclge->bclgep', Cc, h_prev, jnp.exp(acum))
    y = (y_diag + y_off).reshape(b, Tp, H, P)[:, :T]
    return y, h_final.reshape(b, H, P, N)

def _dilated_attn_prompt(q, k, v, window, dil):
    b, S, h, hd = q.shape
    wk = window // dil
    L = S // dil
    nb = -(-L // wk)
    Lp = nb * wk

    def blocks(t):
        t = t.reshape(b, L, dil, h, hd).transpose(0, 2, 1, 3, 4)
        t = jnp.pad(t, ((0, 0), (0, 0), (0, Lp - L), (0, 0), (0, 0)))
        return t.reshape(b, dil, nb, wk, h, hd)

    def with_prev(t):
        prev = jnp.pad(t[:, :, :-1], ((0, 0), (0, 0), (1, 0), (0, 0), (0, 0), (0, 0)))
        return jnp.concatenate([prev, t], axis=3)

    qb = blocks(q)
    kc, vc = with_prev(blocks(k)), with_prev(blocks(v))
    s = jnp.einsum('brnqhd,brnkhd->brnhqk', qb, kc).astype(F32) * ATT_SCALE
    qi = jnp.arange(wk)[:, None]
    ki = jnp.arange(2 * wk)[None, :]
    dist = wk + qi - ki
    band = (dist >= 0) & (dist <= wk)
    first = jnp.arange(nb)[:, None, None] == 0
    mask = band[None] & (jnp.logical_not(first) | (ki >= wk)[None])
    s = jnp.where(mask[None, None, :, None], s, -jnp.inf)
    lse = jax.nn.logsumexp(s, axis=-1)
    p = jnp.exp(s - lse[..., None])
    o = jnp.einsum('brnhqk,brnkhd->brnqhd', p.astype(v.dtype), vc)
    o = o.reshape(b, dil, Lp, h, hd)[:, :, :L].transpose(0, 2, 1, 3, 4).reshape(b, S, h, hd)
    lse = lse.transpose(0, 1, 2, 4, 3).reshape(b, dil, Lp, h)[:, :, :L].transpose(0, 2, 1, 3).reshape(b, S, h)
    return o, lse

def _dilated_attn_sample(q, k, v, buf, window, dil):
    b, T, h, hd = q.shape
    Wb = buf.shape[1]
    kv_all = jnp.concatenate([buf.astype(k.dtype), jnp.stack([k, v], axis=2)], axis=1)
    nk = window // dil + 1
    idx = Wb + jnp.arange(T)[:, None] - dil * jnp.arange(nk)[None, :]
    valid = idx >= 0
    kvg = kv_all[:, jnp.maximum(idx, 0)]
    s = jnp.einsum('bthd,btkhd->bthk', q, kvg[:, :, :, 0]).astype(F32) * ATT_SCALE
    s = jnp.where(valid[None, :, None, :], s, -jnp.inf)
    lse = jax.nn.logsumexp(s, axis=-1)
    p = jnp.exp(s - lse[..., None])
    o = jnp.einsum('bthk,btkhd->bthd', p.astype(v.dtype), kvg[:, :, :, 1])
    return o, lse, kv_all

def _layer(x, pos, conv_state, ssm_state, kv_bufs, norm_w, w_in, conv_w, conv_b, dt_bias, a_log,
           d_skip, ssd_norm_w, q_norm_w, k_norm_w, w_ssd_br, w_att_br, w_out):
    b, t, _ = x.shape
    hn = _rmsnorm(x, norm_w)
    u = hn @ w_in
    z_ssd, xbc, dt_raw, q, k, v, z_att, g_ssd, g_att = jnp.split(u, _split_points(), axis=-1)

    xbc, new_conv = _causal_conv(xbc, conv_state, conv_w, conv_b)
    xs, Bm, Cm = jnp.split(xbc, [D_SSD, D_SSD + SSD_GROUPS * SSD_STATE], axis=-1)
    xh = xs.reshape(b, t, SSD_HEADS, SSD_HEAD_DIM)
    dt = jax.nn.softplus(dt_raw.astype(F32) + dt_bias.astype(F32))
    A = -jnp.exp(a_log.astype(F32))
    y, new_ssm = _ssd_chunked(xh, dt, A, Bm.reshape(b, t, SSD_GROUPS, SSD_STATE),
                              Cm.reshape(b, t, SSD_GROUPS, SSD_STATE), ssm_state)
    y = y + d_skip.astype(F32)[:, None] * xh.astype(F32)
    yg = (y.reshape(b, t, D_SSD) * jax.nn.silu(z_ssd.astype(F32))).reshape(b, t, SSD_GROUPS, D_SSD // SSD_GROUPS)
    yg = yg * lax.rsqrt(jnp.mean(yg * yg, axis=-1, keepdims=True) + EPS)
    y = yg.reshape(b, t, D_SSD) * ssd_norm_w.astype(F32)
    br_ssd = (y.astype(x.dtype) @ w_ssd_br).astype(F32)

    q = _rope(_rmsnorm(q.reshape(b, t, ATT_HEADS, ATT_HEAD_DIM), q_norm_w), pos)
    k = _rope(_rmsnorm(k.reshape(b, t, ATT_HEADS, ATT_HEAD_DIM), k_norm_w), pos)
    v = v.reshape(b, t, ATT_HEADS, ATT_HEAD_DIM)
    outs, lses, new_bufs = [], [], []
    for g, (win, dil) in enumerate(ATT_GROUPS):
        sl = slice(g * ATT_SLOTS, (g + 1) * ATT_SLOTS)
        qg, kg, vg = q[:, :, sl], k[:, :, sl], v[:, :, sl]
        if kv_bufs is None:
            o, lse = _dilated_attn_prompt(qg, kg, vg, win, dil)
            kv_all = jnp.stack([kg, vg], axis=2)
        else:
            o, lse, kv_all = _dilated_attn_sample(qg, kg, vg, kv_bufs[g], win, dil)
        outs.append(o)
        lses.append(lse)
        new_bufs.append(kv_all[:, -min(win, kv_all.shape[1]):])
    alpha = jax.nn.softmax(jnp.stack(lses, axis=-1), axis=-1)
    o = jnp.einsum('bthdg,bthg->bthd', jnp.stack(outs, axis=-1).astype(F32), alpha)
    o = o.reshape(b, t, D_ATT) * jax.nn.silu(z_att.astype(F32))
    br_att = (o.astype(x.dtype) @ w_att_br).astype(F32)

    mix = jax.nn.sigmoid(g_ssd.astype(F32)) * br_ssd + jax.nn.sigmoid(g_att.astype(F32)) * br_att
    out = x + mix.astype(x.dtype) @ w_out
    return out, new_conv, new_ssm, new_bufs

def setup_inputs(seed: int = 0) -> dict:
    key = jax.random.key(seed)
    ks = jax.random.split(key, 24)
    nrm = jax.random.normal
    win_rows = [min(w, PAST_LEN) for (w, _) in ATT_GROUPS]
    dt0 = jnp.exp(jax.random.uniform(ks[0], (DEPTH, SSD_HEADS)) * (np.log(0.1) - np.log(0.001)) + np.log(0.001))
    return {
        'x_prompt': nrm(ks[1], (BATCH, SEQ, D_MODEL), F32),
        'x_sample': nrm(ks[2], (DEC_BATCH, DEC_SEQ, D_MODEL), F32),
        'state_conv': nrm(ks[3], (DEPTH, DEC_BATCH, CONV_WIDTH - 1, D_XBC), F32),
        'state_ssm': 0.1 * nrm(ks[4], (DEPTH, DEC_BATCH, SSD_HEADS, SSD_HEAD_DIM, SSD_STATE), F32),
        'cache_kv_w128': nrm(ks[5], (DEPTH, DEC_BATCH, win_rows[0], 2, ATT_SLOTS, ATT_HEAD_DIM), F32),
        'cache_kv_w512': nrm(ks[6], (DEPTH, DEC_BATCH, win_rows[1], 2, ATT_SLOTS, ATT_HEAD_DIM), F32),
        'cache_kv_w2048': nrm(ks[7], (DEPTH, DEC_BATCH, win_rows[2], 2, ATT_SLOTS, ATT_HEAD_DIM), F32),
        'norm_w': 1.0 + 0.02 * nrm(ks[8], (DEPTH, D_MODEL), F32),
        'w_in': nrm(ks[9], (DEPTH, D_MODEL, N_IN), F32) * D_MODEL ** -0.5,
        'conv_w': nrm(ks[10], (DEPTH, CONV_WIDTH, D_XBC), F32) * CONV_WIDTH ** -0.5,
        'conv_b': 0.01 * nrm(ks[11], (DEPTH, D_XBC), F32),
        'dt_bias': dt0 + jnp.log(-jnp.expm1(-dt0)),
        'a_log': jnp.log(jax.random.uniform(ks[12], (DEPTH, SSD_HEADS), F32, 1.0, 16.0)),
        'd_skip': 1.0 + 0.1 * nrm(ks[13], (DEPTH, SSD_HEADS), F32),
        'ssd_norm_w': 1.0 + 0.02 * nrm(ks[14], (DEPTH, D_SSD), F32),
        'q_norm_w': 1.0 + 0.02 * nrm(ks[15], (DEPTH, ATT_HEAD_DIM), F32),
        'k_norm_w': 1.0 + 0.02 * nrm(ks[16], (DEPTH, ATT_HEAD_DIM), F32),
        'w_ssd_br': nrm(ks[17], (DEPTH, D_SSD, D_MODEL), F32) * D_SSD ** -0.5,
        'w_att_br': nrm(ks[18], (DEPTH, D_ATT, D_MODEL), F32) * D_ATT ** -0.5,
        'w_out': nrm(ks[19], (DEPTH, D_MODEL, D_MODEL), F32) * D_MODEL ** -0.5,
    }

def reference(x_prompt, x_sample, state_conv, state_ssm, cache_kv_w128, cache_kv_w512, cache_kv_w2048,
              norm_w, w_in, conv_w, conv_b, dt_bias, a_log, d_skip, ssd_norm_w, q_norm_w, k_norm_w,
              w_ssd_br, w_att_br, w_out):
    yp, ys = x_prompt, x_sample
    bp, sp = x_prompt.shape[0], x_prompt.shape[1]
    pos_p = jnp.arange(sp, dtype=jnp.int32)
    pos_s = PAST_LEN + jnp.arange(x_sample.shape[1], dtype=jnp.int32)
    conv_p, ssm_p, kv128_p, kv512_p, kv2048_p = [], [], [], [], []
    conv_s, ssm_s, kv128_s, kv512_s, kv2048_s = [], [], [], [], []
    for l in range(DEPTH):
        wl = (norm_w[l], w_in[l], conv_w[l], conv_b[l], dt_bias[l], a_log[l], d_skip[l], ssd_norm_w[l],
              q_norm_w[l], k_norm_w[l], w_ssd_br[l], w_att_br[l], w_out[l])
        conv0 = jnp.zeros((bp, CONV_WIDTH - 1, D_XBC), yp.dtype)
        ssm0 = jnp.zeros((bp, SSD_HEADS, SSD_HEAD_DIM, SSD_STATE), F32)
        yp, c, s, kv = _layer(yp, pos_p, conv0, ssm0, None, *wl)
        conv_p.append(c); ssm_p.append(s)
        kv128_p.append(kv[0]); kv512_p.append(kv[1]); kv2048_p.append(kv[2])
        ys, c, s, kv = _layer(ys, pos_s, state_conv[l], state_ssm[l],
                              [cache_kv_w128[l], cache_kv_w512[l], cache_kv_w2048[l]], *wl)
        conv_s.append(c); ssm_s.append(s)
        kv128_s.append(kv[0]); kv512_s.append(kv[1]); kv2048_s.append(kv[2])
    return (yp, ys,
            jnp.stack(conv_p), jnp.stack(ssm_p), jnp.stack(kv128_p), jnp.stack(kv512_p), jnp.stack(kv2048_p),
            jnp.stack(conv_s), jnp.stack(ssm_s), jnp.stack(kv128_s), jnp.stack(kv512_s), jnp.stack(kv2048_s))


_drawn_inputs = setup_inputs


def setup_inputs(seed=0):
    import zlib

    import numpy as np

    out = dict(_drawn_inputs(seed))
    spreads = {}
    factors = {'conv_b': 3.33, 'ssd_norm_w': 5.87, 'q_norm_w': 8.0, 'k_norm_w': 3.327}
    for name, (base, spread) in spreads.items():
        noise = np.random.default_rng([zlib.crc32(name.encode()), seed]).standard_normal(out[name].shape)
        drawn = base * np.exp(spread * noise) if base else spread * noise
        out[name] = __import__('jax').numpy.asarray(drawn.astype(out[name].dtype))
    for name, factor in factors.items():
        out[name] = (out[name] * factor).astype(out[name].dtype)
    return out
```

```python
from contextlib import ExitStack

import numpy as np
import concourse.bass as bass
from concourse import mybir

F32 = mybir.dt.float32
F32R = mybir.dt.float32r
ALU = mybir.AluOpType
ACT = mybir.ActivationFunctionType
AX = mybir.AxisListType

P = 128
D = 1024
T = 512
B = 8
R = B + T
HALF = R // 2
KD = D // P
SLOT = 2048
NT = T // P
DSSD, GROUPS, NSTATE, HEADS = 2048, 4, 128, 32
DXBC = DSSD + 2 * GROUPS * NSTATE
UNITS = DSSD // P
PER_GROUP = UNITS // GROUPS
SLOTS, HD, NG = 8, 64, 3
DATT = SLOTS * HD
HP = SLOTS // 2
WINDOWS = (128, 512, 2048)
DILATIONS = (1, 4, 16)
EPS = 1e-6
SCALE = HD ** -0.5
TAPS = 4
XU = DXBC // P
S0 = TAPS - 1 + T
BUF = S0 + TAPS * B
CONV = BUF - (TAPS - 1)
CS = T + TAPS - 1
TAIL = (TAPS - 1) * (1 + B)
NKEYS = P

_SIZES = [DSSD, DXBC, HEADS, NG * DATT, NG * DATT, NG * DATT, DATT, D, D]
OFF = dict(zip(["z", "xbc", "dt", "q", "k", "v", "za", "gs", "ga"], np.cumsum([0] + _SIZES[:-1]).tolist()))
OFF_X, OFF_B, OFF_C = OFF["xbc"], OFF["xbc"] + DSSD, OFF["xbc"] + DSSD + GROUPS * NSTATE


def weight_items():
    items = [("rm", g, s, half) for g in range(NG) for s in "qkv" for half in range(2)]
    items += [("za", 0), ("za", 1), ("dt", 0)]
    for g in range(GROUPS):
        items.append(("bc", g))
        for j in range(2 * g, 2 * g + 2):
            items += [("x", j), ("z", j)]
    for j in range(4):
        items += [("gs", j), ("bs", 2 * j), ("bs", 2 * j + 1)]
    for j in range(2):
        items += [("ga", 2 * j), ("ga", 2 * j + 1), ("ba", j)]
    items += [("wo", j) for j in range(4)]
    return items


ITEMS = weight_items()
ITEM_AT = {it: i for i, it in enumerate(ITEMS)}
SHAPES = {"rm": (4, 512), "dt": (KD, P), "bs": (UNITS, P), "ba": (4, 512)}


def plan():
    out = [("init",), ("split", 0)]

    def proj(*item):
        i = ITEM_AT[item]
        if i + 1 < len(ITEMS):
            out.append(("split", i + 1))
        out.append(("proj", i))

    for g in range(NG):
        for s in "qkv":
            proj("rm", g, s, 0)
            proj("rm", g, s, 1)
            if s == "k":
                out.append(("turn", g, 0))
        out.append(("turn", g, 1))
        for h in range(SLOTS + 2):
            if h < SLOTS:
                out.append(("scores", g, h))
            if 1 <= h <= SLOTS:
                out.append(("probs", g, h - 1))
            if h >= 2:
                out.append(("values", g, h - 2))
    out += [("barrier",), ("merge",), ("sample",)]
    proj("za", 0)
    proj("za", 1)
    out.append(("barrier",))
    proj("dt", 0)
    out.append(("dt",))
    for g in range(GROUPS):
        proj("bc", g)
        if g > 0:
            out.append(("ssdB", 4 * g - 1))
        out.append(("bc", g))
        for j in range(2 * g, 2 * g + 2):
            proj("x", j)
            if j > 2 * g:
                out.append(("ssdB", 2 * j - 1))
            elif g > 0:
                out.append(("gnorm", g - 1))
            out.append(("ssdA", 2 * j))
            proj("z", j)
            out.append(("ssdB", 2 * j))
            out.append(("ssdA", 2 * j + 1))
    out += [("ssdB", UNITS - 1), ("gnorm", GROUPS - 1)]
    out += [("barrier",), ("parts",)]
    for j in range(4):
        proj("gs", j)
        proj("bs", 2 * j)
        proj("bs", 2 * j + 1)
    for j in range(2):
        proj("ga", 2 * j)
        proj("ga", 2 * j + 1)
        proj("ba", j)
        out += [("mix", 2 * j), ("mix", 2 * j + 1)]
    for j in range(4):
        proj("wo", j)
    return out


PLAN = plan()

PW_NORM, PW_CONV = 0, KD
PW_CONVB = PW_CONV + XU * TAPS
PW_SNORM = PW_CONVB + XU
PW_D = PW_SNORM + UNITS
PW_DTB, PW_ALOG = PW_D + UNITS, PW_D + UNITS + 1
PW_QW = PW_ALOG + 1
PW_KW = PW_QW + HD
NPARAM = PW_KW + HD
C_ID, C_CAUSAL, C_PREV, C_STRIDED, C_TRI = 0, P, 2 * P, 3 * P, 4 * P
RT = 2 * NT + 1
C_COS = 5 * P
C_SIN = C_COS + RT * HD // 2
NCONST = C_SIN + RT * HD // 2


class Bank:

    def __init__(self, tile, filled, freed):
        self.tile, self.filled, self.freed = tile, filled, freed
        self.uses, self.frees = {}, 0

    def take(self, pe, key):
        assert key not in self.uses, key
        if self.frees:
            pe.wait_ge(self.freed, self.frees)
        self.uses[key] = len(self.uses) + 1
        self.frees += 1

    def full(self, eng, key):
        eng.wait_ge(self.filled, self.uses[key])


class Chain:

    def __init__(self, eng, sem):
        self.eng, self.sem, self.n = eng, sem, 0

    def link(self, ins):
        self.n += 1
        ins.then_inc(self.sem, 1)
        self.eng.wait_ge(self.sem, self.n)


class Arena:

    def __init__(self, nc, base, end):
        self.nc, self.at, self.end = nc, base, end

    def tile(self, name, shape, dt=F32):
        t = self.nc.alloc_sbuf_tensor_at(name, shape, dt, offset=self.at)
        self.at += (int(np.prod(shape[1:])) * 4 + 31) // 32 * 32
        assert self.at <= self.end, (name, self.at, self.end)
        return t


def hybrid_kernel(nc, xT, wpack, params, consts, sel_in, state_conv, ssm_in, caches,
                  y_out, tail_out, ssmp_out, kvp_out, ssms_out, kvs_out):
    ctx = ExitStack()
    with ctx:
        def sem(name):
            return ctx.enter_context(nc.semaphore(name))

        def sb(name, shape, dt=F32):
            return ctx.enter_context(nc.sbuf_tensor(name, shape, dt))

        xH = sb("xH", [P, KD, R], F32R)
        xL = sb("xL", [P, KD, R], F32R)
        raw = sb("w_raw", [P, 2, SLOT])
        wH = sb("wH", [P, 2, SLOT], F32R)
        wL = sb("wL", [P, 2, SLOT], F32R)
        par = sb("par", [P, NPARAM])
        con = sb("con", [P, NCONST])
        ones = sb("ones", [P, P])
        epsc = sb("epsc", [P, 1])
        oT = sb("oT", [P, HP, R])
        base = (nc.sbuf_base + 31) // 32 * 32
        end = nc.sbuf_usable_end
        sb("arena", [P, (end - base - 64) // 4])
        ident = con[:, C_ID:C_ID + P]

        a0 = Arena(nc, base, end)
        qS = a0.tile("qS", [B, 3, NG, T])
        oU = a0.tile("oU", [P, NG, HP, T])
        mst = a0.tile("mst", [P, NG, NT, SLOTS])
        lst = a0.tile("lst", [P, NG, NT, SLOTS])
        a1 = Arena(nc, a0.at, end)
        st = a1.tile("st", [P, 2, NT, T])
        qT = a1.tile("qT", [P, HP, T])
        kT = a1.tile("kT", [P, HP, T])
        vv = a1.tile("vv", [P, NT, T])
        ropeA = a1.tile("ropeA", [P, 2, RT, HD])
        ropeB = a1.tile("ropeB", [P, 2, RT, HD])
        pt_at = a1.at
        sq = a1.tile("sq", [P, 2, T])
        ss = a1.tile("ss", [P, 2, SLOTS])
        rst = a1.tile("rst", [P, 2, SLOTS])
        qn = a1.tile("qn", [P, T])
        t1 = a1.tile("t1", [P, T])
        t2 = a1.tile("t2", [P, T])
        Sx = a1.tile("Sx", [P, 2, 2 * NT - 1, P])
        PT = Arena(nc, pt_at, end).tile("PT", [P, 2, 2 * NT - 1, P])
        l2 = a1.tile("l2", [P, 2, NT - 1])
        mx2 = a1.tile("mx2", [P, 2, NT - 1])
        nm = a1.tile("nm", [P, 2, NT])
        ai = Arena(nc, a0.at, end)
        xw = ai.tile("xw", [P, KD, R])
        xsq = ai.tile("xsq", [P, KD, R])
        rs = ai.tile("rs", [P, R])

        a2 = Arena(nc, a0.at, end)
        sel = a2.tile("sel", [HEADS, UNITS, P])
        mT = a2.tile("mT", [SLOTS, NG, T])
        lT = a2.tile("lT", [SLOTS, NG, T])
        mm_ = a2.tile("mm_", [SLOTS, T])
        den = a2.tile("den", [SLOTS, T])
        dtmp = a2.tile("dtmp", [SLOTS, T])
        mtmp = a2.tile("mtmp", [P, T])
        Kc = a2.tile("Kc", [P, 3, T])
        Vc = a2.tile("Vc", [P, 3, T])
        prod = a2.tile("prod", [P, T])
        sS = a2.tile("sS", [P, B, NG, SLOTS])
        pself = a2.tile("pself", [B, NG, T])
        sself = a2.tile("sself", [B, NG, SLOTS])
        pS = a2.tile("pS", [B, SLOTS, NG, NKEYS + 1])
        Ms = a2.tile("Ms", [B, SLOTS])
        ls = a2.tile("ls", [B, SLOTS])
        SD = a2.tile("SD", [B, NG, SLOTS, B])
        pTs = a2.tile("pTs", [P, NG * SLOTS, B])
        gta = a2.tile("gta", [P, R])
        gtb = a2.tile("gtb", [P, R])

        a3 = Arena(nc, base, end)
        ygn = a3.tile("ygn", [P, UNITS, R])
        ceil_ = a3.at
        stc = a3.tile("stc", [P, XU, B, TAPS - 1])
        tail = a3.tile("tail", [P, XU, TAIL])
        buf = a3.tile("buf", [P, 2, BUF])
        cacc = a3.tile("cacc", [P, CONV])
        cth = a3.tile("cth", [P, CONV])
        wcv = a3.tile("wcv", [P, XU, TAPS + 1])
        BT = a3.tile("BT", [P, CONV])
        CT = a3.tile("CT", [P, CONV])
        xu = a3.tile("xu", [P, 3, CONV])
        Brm = a3.tile("Brm", [P, NT, P])
        CBm = a3.tile("CBm", [P, NT, P])
        BCb = a3.tile("BCb", [P, 2, B, P])
        zs = a3.tile("zs", [P, 2, R])
        ztn = a3.tile("ztn", [P, R])
        xdt = a3.tile("xdt", [P, NT, P])
        xdec = a3.tile("xdec", [P, NT, P])
        gn_at = a3.at
        Lb = a3.tile("Lb", [P, 2, NT, P])
        Eb = a3.tile("Eb", [P, 2, T])
        dcol = a3.tile("dcol", [P, 2, NT])
        hst = a3.tile("hst", [P, 2, NT, P])
        dtrm = a3.tile("dtrm", [P, NT, 3, HEADS])
        nac = a3.tile("nac", [P, NT, HEADS])
        dsb = a3.tile("dsb", [P, UNITS, 2 * B])
        stt_ = a3.tile("stt_", [P, 2, B, P])
        tt = a3.tile("tt", [P, B, P])
        yb = a3.tile("yb", [P, R])
        xds = a3.tile("xds", [P, B])
        y8 = a3.tile("y8", [P, B])
        acT = a3.tile("acT", [HEADS, T])
        ad = Arena(nc, base, ceil_)
        da = [ad.tile(f"da{i}", [HEADS, R]) for i in range(8)]
        onesm = ad.tile("onesm", [HEADS, T])
        dtT = ad.tile("dtT", [HEADS, R])
        decT = ad.tile("decT", [HEADS, T])
        dsS = ad.tile("dsS", [HEADS, 2 * B])
        Acol = ad.tile("Acol", [HEADS, 1])
        sel3 = ad.tile("sel3", [HEADS, UNITS, P])
        gsq = Arena(nc, gn_at, gn_at + 8192)
        sq2 = gsq.tile("sq2", [P, 2, R])
        grs = gsq.tile("grs", [P, R])

        a4 = Arena(nc, base, end)
        yL = a4.tile("yL", [P, UNITS, R], F32R)
        yH = a4.tile("yH", [P, UNITS, R], F32R)
        oH = a4.tile("oH", [P, HP, R], F32R)
        oL = a4.tile("oL", [P, HP, R], F32R)
        mix = a4.tile("mix", [P, KD, R])
        gate = a4.tile("gate", [P, 4, R])
        tmpg = a4.tile("tmpg", [P, R])
        a5 = Arena(nc, base, end)
        mH = a5.tile("mH", [P, KD, R], F32R)
        mL = a5.tile("mL", [P, KD, R], F32R)
        xres = a5.tile("xres", [P, KD, R])
        outb = a5.tile("outb", [P, 2, R])

        banks = [Bank(ctx.enter_context(nc.psum_tensor(f"bank{i}", [P, 512], F32)),
                      sem(f"filled{i}"), sem(f"freed{i}")) for i in range(8)]

        names = """act_order b_rows_ready bc_spread_ready cache_shifted cached_k_used cached_v_used chunk_decay_kept
            chunk_exps_ready constants_set conv_ready conv_rows_placed conv_state_loaded
            conv_state_placed conv_summed conv_tail_kept conv_tail_stored conv_tanh decay_args_ready
            decay_matrix_ready decays_ready dt_activations dt_operands dve_order even_head_summed
            gate_ready gate_used half_item_used head_pair_out head_scales_ready head_sums_ready
            k_cache_loaded0 k_cache_loaded1 k_cache_loaded2 k_stored last_state_ready
            masked_cb_ready maxima_sums_ready merge_exponents merge_exps merge_weights
            mix_high_ready mix_low_ready mix_ready neg_max_ready o_high_ready o_low_ready out_ready
            phase_ended prev_probs_turned probs_ready probs_turned qk_columns_ready qk_normed
            qk_rows_ready qk_squared residual_loaded rope_sine_ready row_scale_ready rows_loaded
            rows_squared sample_exponents sample_exps sample_probs sample_probs_turned
            sample_state_c_ready sample_state_loaded0 sample_state_loaded1 sample_state_ready
            sample_state_stored0 sample_state_stored1 sample_xb_ready sample_xdt_ready
            scaled_c_ready scaled_rows_ready selectors3_loaded selectors_loaded square_summed
            state_stored0 state_stored1 states_before_ready tables_loaded v_cache_loaded0
            v_cache_loaded1 v_cache_loaded2 v_rows_ready v_stored weight_high_ready weight_low_ready
            weights_loaded0 weights_loaded1 x_high_ready x_low_ready xdt_ready y_gated y_high_ready
            y_low_ready y_normed y_squared y_stored0 y_stored1 z_silu_ready z_tanh_ready za_applied
            za_tanh_ready""".split()
        S = {n: sem("s_" + n) for n in names}
        ends = {}

        def cm_units():
            out, c = {}, 0
            for i, it in enumerate(ITEMS):
                for s in range({"rm": 0, "dt": 1, "bs": 1, "ba": 4}.get(it[0], 2)):
                    out[i, s] = c
                    c += 1
            return out

        CMU = cm_units()

        def cm_bank(i, s, hf):
            return banks[2 * (CMU[i, s] % 2) + hf]

        def wslot(w, i):
            k, n = SHAPES.get(ITEMS[i][0], (KD, 2 * P))
            return w[:, i % 2, 0:k * n].rearrange("p (k n) -> p k n", k=k)

        def qk_count(g, si, t):
            return (g * 2 + si) * (NT + 1) + t

        CV = {}
        for i, it in enumerate(ITEMS):
            for s in range(2):
                if it[0] == "bc":
                    CV[i, s] = (len(CV), UNITS + s * GROUPS + it[1])
                elif it[0] == "x":
                    CV[i, s] = (len(CV), 2 * it[1] + s)
        CV_BC = [CV[ITEM_AT["bc", g], 1][0] + 1 for g in range(GROUPS)]
        CV_X = [CV[ITEM_AT["x", u // 2], u % 2][0] + 1 for u in range(UNITS)]

        def pv_done(eng, n):
            if n % 2:
                g, hp = n // SLOTS, n % SLOTS // 2
                banks[6 + hp % 2].full(eng, ("O", g, hp))
            else:
                eng.wait_ge(S["even_head_summed"], n // 2 + 1)

        block = ctx.enter_context(nc.Block())

        @block.tensor
        def _(pe):
            nbar = [0]
            turn_c = [0]

            def barrier():
                nbar[0] += 1
                pe.drain().then_inc(S["phase_ended"], 1)
                pe.wait_ge(S["phase_ended"], 5 * nbar[0])

            def proj_rows(i, g, s, half):
                for t in range(NT + 1):
                    bk = banks[t]
                    if half == 0:
                        bk.take(pe, ("rm", g, s, t))
                    cols = slice(0, P) if t == NT else (slice(B + P * t, B + P * (t + 1)) if g == 0 else slice(B + t, R, NT))
                    for k in range(4):
                        kk = 4 * half + k
                        for n, (a, b) in enumerate(((xH, wH), (xL, wH), (xH, wL))):
                            mm = pe.matmul(bk.tile[:, :], a[:, kk, cols], wslot(b, i)[:, k, :],
                                           start=(kk == 0 and n == 0), stop=(kk == KD - 1 and n == 2))
                    if half == 1:
                        mm.then_inc(bk.filled, 1)
                    elif t == NT:
                        mm.then_inc(S["half_item_used"], 1)
                ends[i] = (banks[NT].filled, banks[NT].uses["rm", g, s, NT]) if half else (S["half_item_used"], i // 2 + 1)

            def proj_cols(i, kind, j):
                srcH, srcL = {"bs": (yH, yL), "ba": (oH, oL), "wo": (mH, mL)}.get(kind, (xH, xL))
                nk = SHAPES.get(kind, (KD,))[0]
                units = [s for (ii, s) in CMU if ii == i]
                if kind == "ba":
                    pe.wait_ge(S["o_low_ready"], HP)
                for s in units:
                    bk = [cm_bank(i, s, hf) for hf in range(2)]
                    for hf in range(2):
                        bk[hf].take(pe, ("cm", i, s, hf))
                    for k in range(nk):
                        if kind == "bs" and j == 0:
                            pe.wait_ge(S["y_low_ready"], k + 1)
                        if kind == "wo" and j == 0 and s == 0:
                            pe.wait_ge(S["mix_low_ready"], k + 1)
                        for n, (w, x) in enumerate(((wH, srcH), (wH, srcL), (wL, srcH))):
                            for hf in range(2):
                                mm = pe.matmul(bk[hf].tile[:, 0:HALF], wslot(w, i)[:, k, s * P:(s + 1) * P],
                                               x[:, k, hf * HALF:(hf + 1) * HALF],
                                               start=(k == 0 and n == 0), stop=(k == nk - 1 and n == 2))
                                if k == nk - 1 and n == 2:
                                    mm.then_inc(bk[hf].filled, 1)
                ends[i] = (bk[1].filled, bk[1].uses["cm", i, s, 1])

            for step in PLAN:
                op, a = step[0], step[1:]
                if op == "barrier":
                    barrier()
                elif op == "init":
                    pe.wait_ge(S["constants_set"], 2)
                    for hf in range(2):
                        banks[hf].take(pe, ("ms", hf))
                    for k in range(KD):
                        pe.wait_ge(S["rows_squared"], k + 1)
                        for hf in range(2):
                            mm = pe.matmul(banks[hf].tile[:, 0:HALF], ones[:, :], xsq[:, k, hf * HALF:(hf + 1) * HALF],
                                           start=(k == 0), stop=(k == KD - 1))
                            if k == KD - 1:
                                mm.then_inc(banks[hf].filled, 1)
                    pe.wait_ge(S["x_low_ready"], KD)
                elif op == "proj":
                    i = a[0]
                    pe.wait_ge(S["weight_low_ready"], i + 1)
                    it = ITEMS[i]
                    if it[0] == "rm":
                        proj_rows(i, *it[1:])
                    else:
                        proj_cols(i, *it)
                elif op == "turn":
                    g, si = a
                    pe.wait_ge(S["tables_loaded"], 32)
                    for t in range(NT):
                        pe.wait_ge(S["qk_rows_ready"], qk_count(g, si, t) + 1)
                        bk = banks[5 + turn_c[0] % 3]
                        turn_c[0] += 1
                        bk.take(pe, ("turn", g, si, t))
                        for hp in range(HP):
                            mm = pe.transpose(bk.tile[:, hp * P:(hp + 1) * P], st[:, si, t, hp * P:(hp + 1) * P], ident)
                        mm.then_inc(bk.filled, 1)
                elif op == "scores":
                    g, h = a
                    n, o, hp = g * SLOTS + h, HD * (h % 2), h // 2
                    if h == 0:
                        pe.wait_ge(S["qk_columns_ready"], 2 * NT * (g + 1))
                    bk = banks[n % 2]
                    bk.take(pe, ("S", n))
                    for t in range(NT):
                        mm = pe.matmul(bk.tile[:, t * P:(t + 1) * P], qT[o:o + HD, hp, t * P:(t + 1) * P],
                                       kT[o:o + HD, hp, t * P:(t + 1) * P], start=True, stop=True)
                    mm.then_inc(bk.filled, 1)
                    if g == 0:
                        bk = banks[2 + n % 2]
                        bk.take(pe, ("Sp", n))
                        for t in range(1, NT):
                            mm = pe.matmul(bk.tile[:, (t - 1) * P:t * P], qT[o:o + HD, hp, t * P:(t + 1) * P],
                                           kT[o:o + HD, hp, (t - 1) * P:t * P], start=True, stop=True)
                        mm.then_inc(bk.filled, 1)
                elif op == "probs":
                    g, h = a
                    n = g * SLOTS + h
                    pe.wait_ge(S["probs_ready"], n + 1)
                    banks[4].take(pe, ("T", n))
                    for t in range(NT):
                        mm = pe.transpose(banks[4].tile[:, t * P:(t + 1) * P], Sx[:, n % 2, t, :], ident)
                    mm.then_inc(banks[4].filled, 1)
                    if g == 0:
                        banks[5].take(pe, ("Tp", n))
                        for t in range(NT - 1):
                            mm = pe.transpose(banks[5].tile[:, t * P:(t + 1) * P], Sx[:, n % 2, NT + t, :], ident)
                        mm.then_inc(banks[5].filled, 1)
                elif op == "values":
                    g, h = a
                    n, o, hp = g * SLOTS + h, HD * (h % 2), h // 2
                    if h == 0:
                        pe.wait_ge(S["v_rows_ready"], (NT + 1) * (g + 1))
                    pe.wait_ge(S["probs_turned"], n + 1)
                    if g == 0:
                        pe.wait_ge(S["prev_probs_turned"], n + 1)
                    bk = banks[6 + hp % 2]
                    if h % 2 == 0:
                        bk.take(pe, ("O", g, hp))
                    for t in range(NT):
                        out = bk.tile[o:o + HD, t * P:(t + 1) * P]
                        mm = pe.matmul(out, vv[:, t, h * HD:(h + 1) * HD], PT[:, n % 2, t, :],
                                       start=(t == 0), stop=True, skip_group_check=True)
                        if g == 0 and t > 0:
                            mm = pe.matmul(out, vv[:, t - 1, h * HD:(h + 1) * HD], PT[:, n % 2, NT + t - 1, :],
                                           start=False, stop=True, skip_group_check=True)
                    mm.then_inc(bk.filled if h % 2 else S["even_head_summed"], 1)
                elif op == "merge":
                    pe.wait_ge(S["maxima_sums_ready"], 1)
                    for g in range(NG):
                        for src, bk, key in ((mst, banks[g], "mt"), (lst, banks[NG + g], "lt")):
                            bk.take(pe, (key, g))
                            for t in range(NT):
                                mm = pe.transpose(bk.tile[0:SLOTS, t * P:(t + 1) * P], src[:, g, t, :], ident)
                            mm.then_inc(bk.filled, 1)
                    pe.wait_ge(S["selectors_loaded"], 16)
                    pe.wait_ge(S["merge_weights"], NG)
                    for hp in range(HP):
                        for g in range(NG):
                            bk = banks[(hp * NG + g) % 6]
                            bk.take(pe, ("wb", hp, g))
                            pe.matmul(bk.tile[:, :], sel[0:SLOTS, hp, :], mT[:, g, :], start=True, stop=True)\
                              .then_inc(bk.filled, 1)
                elif op == "sample":
                    for n in range(B * NG):
                        b, g = divmod(n, NG)
                        bk = banks[6 + n % 2]
                        bk.take(pe, ("qb", n))
                        pe.matmul(bk.tile[:, :], con[0:B, C_ID + b:C_ID + b + 1].to_broadcast([B, P]), qS[:, 0, g, :],
                                  start=True, stop=True).then_inc(bk.filled, 1)
                    pe.wait_ge(S["cached_k_used"], B * NG)
                    for g in range(NG):
                        for q in range(2):
                            bk = banks[2 * g + q]
                            bk.take(pe, ("sT", g, q))
                            for c in range(4):
                                mm = pe.transpose(bk.tile[0:B, c * P:(c + 1) * P], sS[:, :, g, 4 * q + c], ident)
                            mm.then_inc(bk.filled, 1)
                    pe.wait_ge(S["sample_probs"], 1)
                    banks[5].take(pe, ("pTs",))
                    for g in range(NG):
                        for h in range(SLOTS):
                            c = (g * SLOTS + h) * B
                            mm = pe.transpose(banks[5].tile[:, c:c + B], pS[:, h, g, 0:NKEYS], con[0:B, C_ID:C_ID + B])
                    mm.then_inc(banks[5].filled, 1)
                    pe.wait_ge(S["sample_probs_turned"], 1)
                    bk = banks[7]
                    bk.take(pe, ("so",))
                    for h in range(SLOTS):
                        o, hp = HD * (h % 2), h // 2
                        for g in range(NG):
                            pe.matmul(bk.tile[o:o + HD, hp * B:(hp + 1) * B], qS[:, 2, g, h * HD:(h + 1) * HD],
                                      SD[:, g, h, :], start=(h < 2 and g == 0), stop=True, skip_group_check=True)
                    for n in range(B * NG):
                        b, g = divmod(n, NG)
                        pe.wait_ge(S[f"v_cache_loaded{n % 3}"], 16 * (n // 3 + 1))
                        for h in range(SLOTS):
                            o, hp = HD * (h % 2), h // 2
                            mm = pe.matmul(bk.tile[o:o + HD, hp * B + b:hp * B + b + 1], Vc[:, n % 3, h * HD:(h + 1) * HD],
                                           pTs[:, g * SLOTS + h, b:b + 1], start=False, stop=True,
                                           skip_group_check=True)
                        mm.then_inc(S["cached_v_used"] if n < B * NG - 1 else bk.filled, 1)
                elif op == "dt":
                    pe.wait_ge(S["decays_ready"], 1)
                    banks[4].take(pe, ("dtr",))
                    for c in range(NT):
                        for q, src in enumerate((dtT[:, B + c * P:B + (c + 1) * P], acT[:, c * P:(c + 1) * P],
                                                 decT[:, c * P:(c + 1) * P])):
                            mm = pe.transpose(banks[4].tile[:, (c * 3 + q) * HEADS:(c * 3 + q + 1) * HEADS], src,
                                              con[0:HEADS, C_ID:C_ID + HEADS])
                    mm.then_inc(banks[4].filled, 1)
                    pe.wait_ge(S["selectors3_loaded"], 16)
                    banks[5].take(pe, ("dsb",))
                    for u in range(UNITS):
                        mm = pe.matmul(banks[5].tile[:, u * 2 * B:(u + 1) * 2 * B], sel3[:, u, :], dsS[:, :],
                                       start=True, stop=True)
                    mm.then_inc(banks[5].filled, 1)
                elif op == "bc":
                    g = a[0]
                    pe.wait_ge(S["conv_ready"], CV_BC[g])
                    banks[4].take(pe, ("Brm", g))
                    for c in range(NT):
                        mm = pe.transpose(banks[4].tile[:, c * P:(c + 1) * P], BT[:, c * P:(c + 1) * P], ident)
                    mm.then_inc(banks[4].filled, 1)
                    banks[5].take(pe, ("CB", g))
                    for c in range(NT):
                        mm = pe.matmul(banks[5].tile[:, c * P:(c + 1) * P], BT[:, c * P:(c + 1) * P],
                                       CT[:, c * P:(c + 1) * P], start=True, stop=True)
                    mm.then_inc(banks[5].filled, 1)
                    for q, src in enumerate((BT, CT)):
                        for half in range(2):
                            bk = banks[6 + half]
                            bk.take(pe, ("BCb", g, q, half))
                            for c in range(4):
                                b = 4 * half + c
                                mm = pe.matmul(bk.tile[:, c * P:(c + 1) * P],
                                               src[:, CS + TAPS * b:CS + TAPS * b + 1].to_broadcast([P, P]), ident,
                                               start=True, stop=True)
                            mm.then_inc(bk.filled, 1)
                elif op == "ssdA":
                    u = a[0]
                    pe.wait_ge(S["conv_ready"], CV_X[u])
                    banks[4].take(pe, ("xT", u))
                    for c in range(NT):
                        mm = pe.transpose(banks[4].tile[:, c * P:(c + 1) * P], xu[:, u % 3, c * P:(c + 1) * P], ident)
                    mm.then_inc(banks[4].filled, 1)
                    for e in range(2):
                        bk = banks[5 + e]
                        bk.take(pe, ("ac", u, e))
                        pe.matmul(bk.tile[:, :], con[0:HEADS, C_ID + 2 * u + e:C_ID + 2 * u + e + 1].to_broadcast([HEADS, P]),
                                  acT[:, :], start=True, stop=True).then_inc(bk.filled, 1)
                elif op == "ssdB":
                    u = a[0]
                    pe.wait_ge(S["b_rows_ready"], u // PER_GROUP + 1)
                    pe.wait_ge(S["xdt_ready"], u + 1)
                    banks[4].take(pe, ("st", u))
                    for c in range(NT):
                        mm = pe.matmul(banks[4].tile[:, c * P:(c + 1) * P], Brm[:, c, :], xdec[:, c, :], start=True, stop=True)
                    mm.then_inc(banks[4].filled, 1)
                    banks[7].take(pe, ("y", u))
                    for e in range(2):
                        o = e * HD
                        pe.wait_ge(S["masked_cb_ready"], 2 * u + e + 1)
                        for c in range(NT):
                            pe.matmul(banks[7].tile[o:o + HD, c * P:(c + 1) * P], xdt[:, c, o:o + HD], Lb[:, e, c, :],
                                      start=(c == 0), stop=(c == 0), skip_group_check=True)
                    pe.wait_ge(S["scaled_c_ready"], 2 * (u + 1))
                    pe.wait_ge(S["states_before_ready"], u + 1)
                    for e in range(2):
                        o = e * HD
                        for c in range(1, NT):
                            mm = pe.matmul(banks[7].tile[o:o + HD, c * P:(c + 1) * P], hst[:, u % 2, c - 1, o:o + HD],
                                           Eb[:, e, c * P:(c + 1) * P], start=False, stop=True, skip_group_check=True)
                    mm.then_inc(banks[7].filled, 1)
                elif op == "gnorm":
                    g = a[0]
                    for hf in range(2):
                        banks[5 + hf].take(pe, ("gn", g, hf))
                    for k in range(PER_GROUP):
                        pe.wait_ge(S["y_squared"], g * PER_GROUP + k + 1)
                        for hf in range(2):
                            mm = pe.matmul(banks[5 + hf].tile[:, 0:HALF], ones[:, :], sq2[:, k % 2, hf * HALF:(hf + 1) * HALF],
                                           start=(k == 0), stop=(k == PER_GROUP - 1))
                            if k == PER_GROUP - 1:
                                mm.then_inc(banks[5 + hf].filled, 1)
                            elif hf == 1:
                                mm.then_inc(S["square_summed"], 1)

        @block.sync
        def _(sp):
            nbar, outs = 0, 0
            sp.dma_start(xw[:, :, :], xT).then_inc(S["rows_loaded"], 16)
            sp.dma_start(par[:, :], params).then_inc(S["tables_loaded"], 16)
            sp.dma_start(con[:, :], consts).then_inc(S["tables_loaded"], 16)
            pieces = []
            for b in range(B):
                for g in (2, 1, 0):
                    w = WINDOWS[g]
                    for r in range(0, w - 1, 512):
                        pieces.append((g, b, r, min(512, w - 1 - r)))

            def shift(g, b, r, n):
                src = caches[g][b, r + 1:r + 1 + n].rearrange("r c -> (r c)").rearrange("(a x) -> a x", a=P)
                dst = kvs_out[g][b, r:r + n].rearrange("r c -> (r c)").rearrange("(a x) -> a x", a=P)
                sp.dma_start(dst, src).then_inc(S["cache_shifted"], 16)

            def load(i):
                it = ITEMS[i]
                if i >= 2:
                    sp.wait_ge(S["weight_low_ready"], i - 1)
                k, n = SHAPES.get(it[0], (KD, 2 * P))
                sp.dma_start(raw[:, i % 2, 0:k * n], wpack[i, :, 0:k * n]).then_inc(S[f"weights_loaded{i % 2}"], 16)

            per = -(-len(pieces) // (len(ITEMS) - 4))
            npieces = len(pieces)
            for step in PLAN:
                op, a = step[0], step[1:]
                if op == "barrier":
                    nbar += 1
                    sp.drain().then_inc(S["phase_ended"], 1)
                    sp.wait_ge(S["phase_ended"], 5 * nbar)
                elif op == "split":
                    load(a[0])
                    for _ in range(per):
                        if pieces:
                            shift(*pieces.pop(0))
                elif op == "merge":
                    sp.dma_start(sel[:, :, :], sel_in).then_inc(S["selectors_loaded"], 16)
                elif op == "sample":
                    for n in range(B * NG):
                        b, g = divmod(n, NG)
                        if n >= 3:
                            sp.wait_ge(S["cached_k_used"], n - 2)
                        sp.dma_start(Kc[:, n % 3, :], caches[g][b, 0:WINDOWS[g]:DILATIONS[g], 0:T]).then_inc(S[f"k_cache_loaded{n % 3}"], 16)
                    for n in range(B * NG):
                        b, g = divmod(n, NG)
                        if n >= 3:
                            sp.wait_ge(S["cached_v_used"], n - 2)
                        sp.dma_start(Vc[:, n % 3, :], caches[g][b, 0:WINDOWS[g]:DILATIONS[g], T:2 * T]).then_inc(S[f"v_cache_loaded{n % 3}"], 16)
                elif op == "dt":
                    sp.dma_start(sel3[:, :, :], sel_in).then_inc(S["selectors3_loaded"], 16)
                    sp.dma_start(stc[:, :, :, :], state_conv).then_inc(S["conv_state_loaded"], 16)
                elif op == "ssdA":
                    u = a[0]
                    if u >= 2:
                        sp.wait_ge(S[f"sample_state_stored{u % 2}"], 16 * (u // 2))
                        sp.wait_ge(S["sample_state_c_ready"], u - 1)
                    sp.dma_start(stt_[:, u % 2, :, :], ssm_in[u]).then_inc(S[f"sample_state_loaded{u % 2}"], 16)
                elif op == "mix" and a[0] == 3:
                    sp.wait_ge(*ends[ITEM_AT["bs", 7]])
                    sp.dma_start(xres[:, :, :], xT).then_inc(S["residual_loaded"], 16)
            for j in range(KD):
                sp.wait_ge(S["out_ready"], j + 1)
                sp.dma_start(y_out[:, j, :], outb[:, j % 2, :]).then_inc(S[f"y_stored{j % 2}"], 16)
            sp.wait_ge(S["cache_shifted"], 16 * npieces)
            for q in range(2):
                sp.wait_ge(S[f"y_stored{q}"], 16 * (KD // 2))
                sp.wait_ge(S[f"sample_state_stored{q}"], 16 * (UNITS // 2))
            sp.wait_ge(S["k_stored"], 16 * (1 + 4 + 4 + NG))
            sp.wait_ge(S["v_stored"], 16 * (1 + 4 + 4 + NG))
            sp.wait_ge(S["state_stored0"], 16 * (UNITS // 2))
            sp.wait_ge(S["state_stored1"], 16 * (UNITS // 2))
            sp.wait_ge(S["conv_tail_stored"], 16)

        @block.gpsimd
        def _(pool):
            nbar = 0
            outs = 0
            for step in PLAN:
                op, a = step[0], step[1:]
                if op == "barrier":
                    nbar += 1
                    if nbar == 1:
                        pool.wait_ge(S["k_stored"], 16 * (1 + 4 + 4 + NG))
                        pool.wait_ge(S["v_stored"], 16 * (1 + 4 + 4 + NG))
                    if nbar == 3:
                        pool.wait_ge(S["state_stored0"], 16 * (UNITS // 2))
                        pool.wait_ge(S["state_stored1"], 16 * (UNITS // 2))
                        pool.wait_ge(S["sample_state_stored0"], 16 * (UNITS // 2))
                        pool.wait_ge(S["sample_state_stored1"], 16 * (UNITS // 2))
                        pool.wait_ge(S["conv_tail_stored"], 16)
                    pool.drain().then_inc(S["phase_ended"], 1)
                    pool.wait_ge(S["phase_ended"], 5 * nbar)
                elif op == "proj" and ITEMS[a[0]][0] == "rm" and ITEMS[a[0]][3] == 1:
                    g, s = ITEMS[a[0]][1:3]
                    if s == "v":
                        for t in range(NT + 1):
                            pool.wait_ge(S["v_rows_ready"], (NT + 1) * g + t + 1)
                            if t == NT:
                                pool.dma_start(kvs_out[g][:, WINDOWS[g] - 1, T:2 * T], qS[:, 2, g, :]).then_inc(S["v_stored"], 16)
                            elif g > 0:
                                pool.dma_start(kvp_out[g][t:T:NT, T:2 * T], vv[:, t, :]).then_inc(S["v_stored"], 16)
                            elif t == NT - 1:
                                pool.dma_start(kvp_out[g][:, T:2 * T], vv[:, t, :]).then_inc(S["v_stored"], 16)
                        continue
                    si = "qk".index(s)
                    for t in range(NT + 1):
                        n = qk_count(g, si, t)
                        rows = B if t == NT else P
                        tab = 2 * NT if t == NT else (t if g == 0 else NT + t)
                        pool.wait_ge(S["qk_normed"], n + 1)
                        if n > 0:
                            pool.wait_ge(S["qk_rows_ready"], n)
                        v = qn[0:rows, :].rearrange("p (h x d) -> p h x d", h=SLOTS, x=2)
                        o = t2[0:rows, :].rearrange("p (h x d) -> p h x d", h=SLOTS, x=2)
                        for x in range(2):
                            rb = ropeB[0:rows, si, tab, 32 * x:32 * x + 32].unsqueeze(1).to_broadcast([rows, SLOTS, 32])
                            ins = nc.gpsimd.tensor_tensor(o[:, :, x, :], v[:, :, 1 - x, :], rb, ALU.mult)
                        ins.then_inc(S["rope_sine_ready"], 1)
                        if si == 1:
                            pool.wait_ge(S["qk_rows_ready"], n + 1)
                            if t == NT:
                                pool.dma_start(kvs_out[g][:, WINDOWS[g] - 1, 0:T], qS[:, 1, g, :]).then_inc(S["k_stored"], 16)
                            elif g > 0:
                                pool.dma_start(kvp_out[g][t:T:NT, 0:T], st[:, 1, t, :]).then_inc(S["k_stored"], 16)
                            elif t == NT - 1:
                                pool.dma_start(kvp_out[g][:, 0:T], st[:, 1, t, :]).then_inc(S["k_stored"], 16)
                elif op == "ssdA":
                    u = a[0]
                    for e in range(2):
                        n = 2 * u + e
                        pool.wait_ge(S["chunk_exps_ready"], n + 1)
                        if u > 0 and e == 0:
                            pool.wait_ge(S["last_state_ready"], u)
                        nc.gpsimd.tensor_copy(dcol[:, e, :], Eb[:, e, P - 1:T:P]).then_inc(S["chunk_decay_kept"], 1)
                        pool.wait_ge(S["chunk_decay_kept"], n + 1)
                        nc.gpsimd.tensor_tensor(Eb[:, e, :], Eb[:, e, :], CT[:, 0:T], ALU.mult).then_inc(S["scaled_c_ready"], 1)
                elif op == "ssdB":
                    u = a[0]
                    g = u // PER_GROUP
                    pool.wait_ge(S["sample_xdt_ready"], u + 1)
                    pool.wait_ge(S["bc_spread_ready"], 4 * (g + 1))
                    if u >= 1:
                        pool.wait_ge(S["y_gated"], u)
                    nc.gpsimd.tensor_tensor(tt[:, :, :], BCb[:, 0, :, :], xds[:, :].unsqueeze(2).to_broadcast([P, B, P]),
                                            ALU.mult).then_inc(S["sample_xb_ready"], 1)
                    pool.wait_ge(S["sample_state_ready"], u + 1)
                    pool.dma_start(ssms_out[u], stt_[:, u % 2, :, :]).then_inc(S[f"sample_state_stored{u % 2}"], 16)
                    nc.gpsimd.tensor_tensor(tt[:, :, :], BCb[:, 1, :, :], stt_[:, u % 2, :, :], ALU.mult).then_inc(S["sample_state_c_ready"], 1)
                    pool.wait_ge(S["last_state_ready"], u + 1)
                    pool.dma_start(ssmp_out[u], hst[:, u % 2, NT - 1, :]).then_inc(S[f"state_stored{u % 2}"], 16)
                elif op == "gnorm" and a[0] == GROUPS - 1:
                    pool.wait_ge(S["conv_tail_kept"], XU)
                    pool.dma_start(tail_out, tail[:, :, :]).then_inc(S["conv_tail_stored"], 16)

        @block.scalar
        def _(act):
            nbar = 0
            ch = Chain(act, S["act_order"])
            A = nc.scalar.activation

            def cp(out, in_):
                return nc.scalar.copy(out, in_)

            def free(bk):
                act.sem_inc(bk.freed, 1)

            def both(i, s):
                for hf in range(2):
                    cm_bank(i, s, hf).full(act, ("cm", i, s, hf))

            for step in PLAN:
                op, a = step[0], step[1:]
                if op == "barrier":
                    nbar += 1
                    act.drain().then_inc(S["phase_ended"], 1)
                    act.wait_ge(S["phase_ended"], 5 * nbar)
                elif op == "init":
                    act.wait_ge(S["rows_loaded"], 16)
                    for k in range(KD):
                        A(xsq[:, k, :], xw[:, k, :], ACT.Square).then_inc(S["rows_squared"], 1)
                    act.wait_ge(S["constants_set"], 2)
                    for hf in range(2):
                        banks[hf].full(act, ("ms", hf))
                        ch.link(A(rs[:, hf * HALF:(hf + 1) * HALF], banks[hf].tile[:, 0:HALF], ACT.Ln, bias=epsc[:, 0:1], scale=1.0 / D))
                        free(banks[hf])
                    A(rs[:, :], rs[:, :], ACT.Exp, scale=-0.5).then_inc(S["row_scale_ready"], 1)
                    for k in range(KD):
                        act.wait_ge(S["scaled_rows_ready"], k + 1)
                        cp(xH[:, k, :], xw[:, k, :]).then_inc(S["x_high_ready"], 1)
                elif op == "split":
                    i = a[0]
                    k, n = SHAPES.get(ITEMS[i][0], (KD, 2 * P))
                    act.wait_ge(S[f"weights_loaded{i % 2}"], 16 * (i // 2 + 1))
                    if i >= 2:
                        act.wait_ge(*ends[i - 2])
                    cp(wH[:, i % 2, 0:k * n], raw[:, i % 2, 0:k * n]).then_inc(S["weight_high_ready"], 1)
                elif op == "proj":
                    i = a[0]
                    it = ITEMS[i]
                    if it[0] == "rm" and it[3] == 1:
                        g, s = it[1:3]
                        if s == "v":
                            if g > 0:
                                act.wait_ge(S["v_stored"], 16 * {1: 2, 2: 7}[g])
                                pv_done(act, g * SLOTS - 1)
                            for t in range(NT + 1):
                                banks[t].full(act, ("rm", g, s, t))
                                dst = qS[:, 2, g, :] if t == NT else vv[:, t, :]
                                cp(dst, banks[t].tile[0:B if t == NT else P, :]).then_inc(S["v_rows_ready"], 1)
                                act.wait_ge(S["v_rows_ready"], (NT + 1) * g + t + 1)
                                free(banks[t])
                            continue
                        si = "qk".index(s)

                        def square(t):
                            n = qk_count(g, si, t)
                            rows = B if t == NT else P
                            banks[t].full(act, ("rm", g, s, t))
                            if n >= 2:
                                act.wait_ge(S["head_sums_ready"], n - 1)
                            A(sq[0:rows, n % 2, :], banks[t].tile[0:rows, :], ACT.Square, scale=HD ** -0.5).then_inc(S["qk_squared"], 1)

                        def root(t):
                            n = qk_count(g, si, t)
                            rows = B if t == NT else P
                            act.wait_ge(S["head_sums_ready"], n + 1)
                            ch.link(A(ss[0:rows, n % 2, :], ss[0:rows, n % 2, :], ACT.Ln, bias=epsc[0:rows, 0:1]))
                            if n >= 2:
                                act.wait_ge(S["qk_normed"], n - 1)
                            A(rst[0:rows, n % 2, :], ss[0:rows, n % 2, :], ACT.Exp, scale=-0.5).then_inc(S["head_scales_ready"], 1)

                        square(0)
                        for t in range(NT + 1):
                            if t < NT:
                                square(t + 1)
                            root(t)
                    elif it[0] == "za":
                        for s in range(2):
                            both(i, s)
                            hp = 2 * it[1] + s
                            if hp > 0:
                                act.wait_ge(S["za_applied"], hp)
                            for hf in range(2):
                                ins = A(gta[:, hf * HALF:(hf + 1) * HALF], cm_bank(i, s, hf).tile[:, 0:HALF], ACT.Tanh, scale=0.5)
                            ins.then_inc(S["za_tanh_ready"], 1)
                    elif it[0] in ("bc", "x"):
                        for s in range(2):
                            n, cu = CV[i, s]
                            both(i, s)
                            b0, b1 = (cm_bank(i, s, hf) for hf in range(2))
                            act.wait_ge(S["conv_state_placed"], n + 1)
                            cp(buf[:, n % 2, TAPS - 1:TAPS - 1 + HALF - B], b0.tile[:, B:HALF])
                            cp(buf[:, n % 2, TAPS - 1 + HALF - B:S0], b1.tile[:, 0:HALF])
                            ch.link(cp(buf[:, n % 2, S0 + TAPS - 1:BUF:TAPS], b0.tile[:, 0:B]))
                            free(b0)
                            free(b1)
                            act.sem_inc(S["conv_rows_placed"], 1)
                            act.wait_ge(S["conv_summed"], n + 1)
                            A(cth[:, :], cacc[:, :], ACT.Tanh).then_inc(S["conv_tanh"], 1)
                    elif it[0] == "z":
                        for s in range(2):
                            u = 2 * it[1] + s
                            both(i, s)
                            if u > 0:
                                act.wait_ge(S["z_silu_ready"], u)
                            for hf in range(2):
                                ins = A(ztn[:, hf * HALF:(hf + 1) * HALF], cm_bank(i, s, hf).tile[:, 0:HALF], ACT.Tanh, scale=0.5)
                            ins.then_inc(S["z_tanh_ready"], 1)
                    elif it[0] in ("gs", "ga"):
                        base_g = 0 if it[0] == "gs" else KD
                        for s in range(2):
                            both(i, s)
                            n = base_g + 2 * it[1] + s
                            if n >= 4:
                                act.wait_ge(S["gate_used"], n - 3)
                            for hf in range(2):
                                bk = cm_bank(i, s, hf)
                                ch.link(A(gate[:, n % 4, hf * HALF:(hf + 1) * HALF], bk.tile[:, 0:HALF], ACT.Tanh, scale=0.5))
                                free(bk)
                            act.sem_inc(S["gate_ready"], 1)
                elif op == "turn":
                    g, si = a
                    dst = (qT, kT)[si]
                    if g > 0:
                        n = g * SLOTS - 1
                        banks[n % 2].full(act, ("S", n))
                        if g == 1:
                            banks[2 + n % 2].full(act, ("Sp", n))
                    for t in range(NT):
                        bk = next(b for b in banks[5:8] if ("turn", g, si, t) in b.uses)
                        bk.full(act, ("turn", g, si, t))
                        cp(dst[:, :, t * P:(t + 1) * P], bk.tile[:, :].rearrange("p (h c) -> p h c", h=HP)).then_inc(S["qk_columns_ready"], 1)
                        act.wait_ge(S["qk_columns_ready"], (2 * g + si) * NT + t + 1)
                        free(bk)
                elif op == "scores":
                    g, h = a
                    n = g * SLOTS + h
                    act.wait_ge(S["neg_max_ready"], n + 1)
                    for t in range(NT):
                        ins = A(Sx[:, n % 2, t, :], Sx[:, n % 2, t, :], ACT.Exp, bias=nm[:, n % 2, t:t + 1],
                                accum_out=lst[:, g, t, h:h + 1])
                    if g == 0:
                        for t in range(1, NT):
                            ins = A(Sx[:, n % 2, NT + t - 1, :], Sx[:, n % 2, NT + t - 1, :], ACT.Exp, bias=nm[:, n % 2, t:t + 1],
                                    accum_out=l2[:, n % 2, t - 1:t])
                    ins.then_inc(S["probs_ready"], 1)
                elif op == "probs":
                    g, h = a
                    n = g * SLOTS + h
                    banks[4].full(act, ("T", n))
                    if n >= 2:
                        pv_done(act, n - 2)
                    cp(PT[:, n % 2, 0:NT, :], banks[4].tile[:, :].rearrange("p (t c) -> p t c", t=NT)).then_inc(S["probs_turned"], 1)
                    act.wait_ge(S["probs_turned"], n + 1)
                    free(banks[4])
                elif op == "values" and a[1] % 2:
                    g, h = a
                    hp = h // 2
                    bk = banks[6 + hp % 2]
                    bk.full(act, ("O", g, hp))
                    dst = oU[:, g, hp, :]
                    if g > 0:
                        dst = dst.rearrange("p (j t) -> p t j", t=NT)
                    else:
                        dst = dst.rearrange("p (t j) -> p t j", t=NT)
                    cp(dst, bk.tile[:, :].rearrange("p (t j) -> p t j", t=NT)).then_inc(S["head_pair_out"], 1)
                    act.wait_ge(S["head_pair_out"], g * HP + hp + 1)
                    free(bk)
                elif op == "merge":
                    for g in range(NG):
                        act.wait_ge(S["merge_exponents"], g + 1)
                        A(mT[:, g, :], mT[:, g, :], ACT.Exp).then_inc(S["merge_exps"], 1)
                elif op == "sample":
                    act.wait_ge(S["sample_exponents"], 1)
                    A(pS[:, :, :, :], pS[:, :, :, :], ACT.Exp).then_inc(S["sample_exps"], 1)
                elif op == "dt":
                    act.wait_ge(S["tables_loaded"], 32)
                    A(Acol[:, :], par[0:HEADS, PW_ALOG:PW_ALOG + 1], ACT.Exp).then_inc(S["dt_activations"], 1)
                    act.wait_ge(S["dt_operands"], 1)
                    A(da[2][:, :], da[1][:, :], ACT.Exp).then_inc(S["dt_activations"], 1)
                    act.wait_ge(S["dt_operands"], 2)
                    A(da[4][:, :], da[3][:, :], ACT.Ln).then_inc(S["dt_activations"], 1)
                    act.wait_ge(S["dt_operands"], 3)
                    A(dsS[:, 0:B], da[7][:, 0:B], ACT.Exp)
                    A(decT[:, :], decT[:, :], ACT.Exp).then_inc(S["decays_ready"], 1)
                elif op == "bc":
                    g = a[0]
                    banks[4].full(act, ("Brm", g))
                    if g > 0:
                        banks[4].full(act, ("st", 4 * g - 1))
                        act.wait_ge(S["sample_state_c_ready"], 4 * g)
                    cp(Brm[:, :, :], banks[4].tile[:, :].rearrange("p (c n) -> p c n", c=NT)).then_inc(S["b_rows_ready"], 1)
                    act.wait_ge(S["b_rows_ready"], g + 1)
                    free(banks[4])
                    for q in range(2):
                        for half in range(2):
                            bk = banks[6 + half]
                            bk.full(act, ("BCb", g, q, half))
                            cp(BCb[:, q, 4 * half:4 * half + 4, :], bk.tile[:, :].rearrange("p (c n) -> p c n", c=4)).then_inc(S["bc_spread_ready"], 1)
                            act.wait_ge(S["bc_spread_ready"], 4 * g + 2 * q + half + 1)
                            free(bk)
                elif op == "ssdA":
                    u = a[0]
                    if u > 0:
                        banks[7].full(act, ("y", u - 1))
                    if u > 0 and u % PER_GROUP == 0:
                        act.wait_ge(S["y_normed"], u // PER_GROUP)
                    for e in range(2):
                        n = 2 * u + e
                        banks[5 + e].full(act, ("ac", u, e))
                        A(Eb[:, e, :], banks[5 + e].tile[:, :], ACT.Exp).then_inc(S["chunk_exps_ready"], 1)
                        act.wait_ge(S["decay_args_ready"], n + 1)
                        for c in range(NT):
                            ins = A(Lb[:, e, c, :], Lb[:, e, c, :], ACT.Exp, bias=nac[:, c, 2 * u + e:2 * u + e + 1])
                        ins.then_inc(S["decay_matrix_ready"], 1)
                elif op == "gnorm":
                    g = a[0]
                    act.wait_ge(S["decay_matrix_ready"], 2 * PER_GROUP * (g + 1))
                    banks[7].full(act, ("y", PER_GROUP * (g + 1) - 1))
                    for k in range(PER_GROUP):
                        n = g * PER_GROUP + k
                        act.wait_ge(S["y_gated"], n + 1)
                        if k >= 2:
                            act.wait_ge(S["square_summed"], 3 * g + k - 1)
                        elif g > 0:
                            banks[6].full(act, ("gn", g - 1, 1))
                        A(sq2[:, k % 2, :], ygn[:, n, :], ACT.Square).then_inc(S["y_squared"], 1)
                    if g > 0:
                        act.wait_ge(S["y_normed"], g)
                    for hf in range(2):
                        banks[5 + hf].full(act, ("gn", g, hf))
                        ch.link(A(grs[:, hf * HALF:(hf + 1) * HALF], banks[5 + hf].tile[:, 0:HALF], ACT.Sqrt, bias=epsc[:, 0:1],
                                  scale=float(GROUPS) / DSSD))
                        free(banks[5 + hf])
                    act.sem_inc(S["scaled_rows_ready"], 1)
                elif op == "parts":
                    for u in range(UNITS):
                        cp(yH[:, u, :], ygn[:, u, :]).then_inc(S["y_high_ready"], 1)
                    for hp in range(HP):
                        cp(oH[:, hp, :], oT[:, hp, :]).then_inc(S["o_high_ready"], 1)
                elif op == "mix":
                    for s in range(2):
                        k = 2 * a[0] + s
                        act.wait_ge(S["mix_ready"], k + 1)
                        cp(mH[:, k, :], mix[:, k, :]).then_inc(S["mix_high_ready"], 1)

        @block.vector
        def _(dve):
            nbar = 0
            ch = Chain(dve, S["dve_order"])
            V = nc.vector
            TT, TS, STT = V.tensor_tensor, V.tensor_scalar, V.scalar_tensor_tensor

            def free(bk):
                dve.sem_inc(bk.freed, 1)

            V.memset(ones[:, :], 1.0).then_inc(S["constants_set"], 1)
            V.memset(epsc[:, :], EPS).then_inc(S["constants_set"], 1)
            for step in PLAN:
                op, a = step[0], step[1:]
                if op == "barrier":
                    nbar += 1
                    dve.drain().then_inc(S["phase_ended"], 1)
                    dve.wait_ge(S["phase_ended"], 5 * nbar)
                    if nbar == 2:
                        ch.link(V.memset(onesm[:, :], 1.0))
                        V.memset(buf[:, 0, 0:TAPS - 1], 0.0)
                        V.memset(buf[:, 1, 0:TAPS - 1], 0.0)
                        ch.link(TS(wcv[:, :, 0:TAPS], par[:, PW_CONV:PW_CONVB].rearrange("p (u w) -> p u w", w=TAPS), 0.5, None, ALU.mult))
                        ch.link(TS(wcv[:, :, TAPS:TAPS + 1], par[:, PW_CONVB:PW_SNORM].unsqueeze(2), 0.5, None, ALU.mult))
                elif op == "init":
                    dve.wait_ge(S["tables_loaded"], 32)
                    dve.wait_ge(S["row_scale_ready"], 1)
                    for k in range(KD):
                        STT(out=xw[:, k, :], in0=xw[:, k, :], scalar=par[:, PW_NORM + k:PW_NORM + k + 1], in1=rs[:, :],
                            op0=ALU.mult, op1=ALU.mult).then_inc(S["scaled_rows_ready"], 1)
                    for k in range(KD):
                        dve.wait_ge(S["x_high_ready"], k + 1)
                        TT(xL[:, k, :], xw[:, k, :], xH[:, k, :].bitcast(F32), ALU.subtract).then_inc(S["x_low_ready"], 1)
                    dve.wait_ge(S["x_low_ready"], KD)
                    cos = con[:, C_COS:C_SIN].rearrange("p (t d) -> p t d", d=32)
                    sin = con[:, C_SIN:NCONST].rearrange("p (t d) -> p t d", d=32)
                    for si, w0 in enumerate((PW_QW, PW_KW)):
                        for x in range(2):
                            own = par[:, w0 + 32 * x:w0 + 32 * x + 32].unsqueeze(1).to_broadcast([P, RT, 32])
                            other = par[:, w0 + 32 * (1 - x):w0 + 32 * (1 - x) + 32].unsqueeze(1).to_broadcast([P, RT, 32])
                            ch.link(TT(ropeA[:, si, :, 32 * x:32 * x + 32], cos, own, ALU.mult))
                            ch.link(STT(out=ropeB[:, si, :, 32 * x:32 * x + 32], in0=sin, scalar=-1.0 if x == 0 else 1.0,
                                        in1=other, op0=ALU.mult, op1=ALU.mult))
                elif op == "split":
                    i = a[0]
                    k, n = SHAPES.get(ITEMS[i][0], (KD, 2 * P))
                    dve.wait_ge(S["weight_high_ready"], i + 1)
                    TT(wL[:, i % 2, 0:k * n], raw[:, i % 2, 0:k * n], wH[:, i % 2, 0:k * n].bitcast(F32), ALU.subtract)\
                        .then_inc(S["weight_low_ready"], 1)
                elif op == "proj":
                    i = a[0]
                    it = ITEMS[i]
                    if it[0] == "rm" and it[3] == 1 and it[2] != "v":
                        g, s = it[1:3]
                        si = "qk".index(s)

                        def reduce(t):
                            n = qk_count(g, si, t)
                            rows = B if t == NT else P
                            dve.wait_ge(S["qk_squared"], n + 1)
                            if n >= 2:
                                dve.wait_ge(S["head_scales_ready"], n - 1)
                            V.tensor_reduce(ss[0:rows, n % 2, :], sq[0:rows, n % 2, :].rearrange("p (h d) -> p h d", h=SLOTS),
                                            AX.X, ALU.add).then_inc(S["head_sums_ready"], 1)

                        def norm(t):
                            n = qk_count(g, si, t)
                            rows = B if t == NT else P
                            tab = 2 * NT if t == NT else (t if g == 0 else NT + t)

                            def heads(x):
                                return x.rearrange("p (h d) -> p h d", h=SLOTS)

                            dve.wait_ge(S["head_scales_ready"], n + 1)
                            TT(heads(qn[0:rows, :]), heads(banks[t].tile[0:rows, :]),
                               rst[0:rows, n % 2, :].unsqueeze(2).to_broadcast([rows, SLOTS, HD]), ALU.mult).then_inc(S["qk_normed"], 1)
                            dve.wait_ge(S["qk_normed"], n + 1)
                            free(banks[t])
                            ch.link(TT(heads(t1[0:rows, :]), heads(qn[0:rows, :]),
                                       ropeA[0:rows, si, tab, :].unsqueeze(1).to_broadcast([rows, SLOTS, HD]), ALU.mult))
                            dst = qS[:, si, g, :] if t == NT else st[:, si, t, :]
                            if g > 0 and t < NT:
                                bk = next(b for b in banks[5:8] if ("turn", g - 1, si, t) in b.uses)
                                bk.full(dve, ("turn", g - 1, si, t))
                                if si == 1:
                                    dve.wait_ge(S["k_stored"], 16 * {1: 2, 2: 7}[g])
                            dve.wait_ge(S["rope_sine_ready"], n + 1)
                            TT(dst, t1[0:rows, :], t2[0:rows, :], ALU.add).then_inc(S["qk_rows_ready"], 1)

                        reduce(0)
                        for t in range(1, NT + 1):
                            reduce(t)
                            norm(t - 1)
                        norm(NT)
                    elif it[0] == "za":
                        for s in range(2):
                            hp = 2 * it[1] + s
                            dve.wait_ge(S["za_tanh_ready"], hp + 1)
                            for hf in range(2):
                                bk = cm_bank(i, s, hf)
                                sl = slice(hf * HALF, (hf + 1) * HALF)
                                ch.link(STT(out=gtb[:, sl], in0=gta[:, sl], scalar=1.0, in1=bk.tile[:, 0:HALF], op0=ALU.add, op1=ALU.mult))
                                free(bk)
                            STT(out=oT[:, hp, :], in0=oT[:, hp, :], scalar=0.5, in1=gtb[:, :], op0=ALU.mult, op1=ALU.mult)\
                                .then_inc(S["za_applied"], 1)
                            dve.wait_ge(S["za_applied"], hp + 1)
                    elif it[0] in ("bc", "x"):
                        for s in range(2):
                            n, cu = CV[i, s]
                            if n == 0:
                                dve.wait_ge(S["conv_state_loaded"], 16)
                            bb = buf[:, n % 2, :]
                            V.tensor_copy(bb[:, S0:BUF].rearrange("p (b w) -> p b w", w=TAPS)[:, :, 0:TAPS - 1], stc[:, cu, :, :])\
                                .then_inc(S["conv_state_placed"], 1)
                            dve.wait_ge(S["conv_rows_placed"], n + 1)
                            V.tensor_copy(tail[:, cu, 0:TAPS - 1], bb[:, T:T + TAPS - 1])
                            V.tensor_copy(tail[:, cu, TAPS - 1:TAIL].rearrange("p (b w) -> p b w", w=TAPS - 1),
                                          bb[:, S0:BUF].rearrange("p (b w) -> p b w", w=TAPS)[:, :, 1:TAPS]).then_inc(S["conv_tail_kept"], 1)
                            ch.link(TS(cacc[:, :], bb[:, 0:CONV], wcv[:, cu, 0:1], wcv[:, cu, TAPS:TAPS + 1], ALU.mult, ALU.add))
                            for w in range(1, TAPS):
                                ins = STT(out=cacc[:, :], in0=bb[:, w:w + CONV], scalar=wcv[:, cu, w:w + 1], in1=cacc[:, :],
                                          op0=ALU.mult, op1=ALU.add)
                                if w < TAPS - 1:
                                    ch.link(ins)
                            ins.then_inc(S["conv_summed"], 1)
                            dve.wait_ge(S["conv_tanh"], n + 1)
                            if it[0] == "x":
                                u = 2 * it[1] + s
                                dst = xu[:, u % 3, :]
                                if u >= 3:
                                    banks[4].full(dve, ("xT", u - 3))
                            else:
                                dst = (BT, CT)[s]
                                if it[1] > 0:
                                    g = it[1] - 1
                                    banks[5].full(dve, ("CB", g))
                                    banks[7].full(dve, ("BCb", g, 1, 1))
                                    dve.wait_ge(S["scaled_c_ready"], 2 * PER_GROUP * (g + 1))
                                dst = dst[:, :]
                            STT(out=dst, in0=cth[:, :], scalar=1.0, in1=cacc[:, :], op0=ALU.add, op1=ALU.mult).then_inc(S["conv_ready"], 1)
                            dve.wait_ge(S["conv_ready"], n + 1)
                    elif it[0] == "z":
                        for s in range(2):
                            u = 2 * it[1] + s
                            dve.wait_ge(S["z_tanh_ready"], u + 1)
                            for hf in range(2):
                                bk = cm_bank(i, s, hf)
                                sl = slice(hf * HALF, (hf + 1) * HALF)
                                ch.link(STT(out=zs[:, u % 2, sl], in0=ztn[:, sl], scalar=1.0, in1=bk.tile[:, 0:HALF],
                                            op0=ALU.add, op1=ALU.mult))
                                free(bk)
                            dve.sem_inc(S["z_silu_ready"], 1)
                    elif it[0] in ("bs", "ba"):
                        for s in range(1 if it[0] == "bs" else 4):
                            j = it[1] if it[0] == "bs" else 4 * it[1] + s
                            n = j + (KD if it[0] == "ba" else 0)
                            dve.wait_ge(S["gate_ready"], n + 1)
                            for hf in range(2):
                                bk = cm_bank(i, s, hf)
                                bk.full(dve, ("cm", i, s, hf))
                                sl = slice(hf * HALF, (hf + 1) * HALF)
                                dst = mix[:, j, sl] if it[0] == "bs" else tmpg[:, sl]
                                ch.link(STT(out=dst, in0=gate[:, n % 4, sl], scalar=1.0, in1=bk.tile[:, 0:HALF],
                                            op0=ALU.add, op1=ALU.mult))
                                free(bk)
                            dve.sem_inc(S["gate_used"], 1)
                            if it[0] == "ba":
                                TT(mix[:, j, :], mix[:, j, :], tmpg[:, :], ALU.add).then_inc(S["mix_ready"], 1)
                                dve.wait_ge(S["mix_ready"], j + 1)
                    elif it[0] == "wo":
                        for s in range(2):
                            j = 2 * it[1] + s
                            if j == 0:
                                dve.wait_ge(S["residual_loaded"], 16)
                            if j >= 2:
                                dve.wait_ge(S[f"y_stored{j % 2}"], 16 * (j // 2))
                            for hf in range(2):
                                bk = cm_bank(i, s, hf)
                                bk.full(dve, ("cm", i, s, hf))
                                sl = slice(hf * HALF, (hf + 1) * HALF)
                                ch.link(STT(out=outb[:, j % 2, sl], in0=bk.tile[:, 0:HALF], scalar=0.5, in1=xres[:, j, sl],
                                            op0=ALU.mult, op1=ALU.add))
                                free(bk)
                            dve.sem_inc(S["out_ready"], 1)
                elif op == "scores":
                    g, h = a
                    n = g * SLOTS + h
                    if n >= 2:
                        banks[4].full(dve, ("T", n - 2))
                        if n - 2 < SLOTS:
                            banks[5].full(dve, ("Tp", n - 2))
                    bk = banks[n % 2]
                    bk.full(dve, ("S", n))
                    c0 = (C_CAUSAL, C_STRIDED if False else C_CAUSAL, C_STRIDED)[g]
                    mask = con[:, c0:c0 + P].unsqueeze(1).to_broadcast([P, NT, P])
                    ch.link(STT(out=Sx[:, n % 2, 0:NT, :], in0=bk.tile[:, :].rearrange("p (t c) -> p t c", t=NT), scalar=SCALE,
                                in1=mask, op0=ALU.mult, op1=ALU.add))
                    free(bk)
                    ch.link(V.tensor_reduce(mst[:, g, :, h], Sx[:, n % 2, 0:NT, :], AX.X, ALU.max))
                    if g == 0:
                        bk = banks[2 + n % 2]
                        bk.full(dve, ("Sp", n))
                        mask = con[:, C_PREV:C_PREV + P].unsqueeze(1).to_broadcast([P, NT - 1, P])
                        ch.link(STT(out=Sx[:, n % 2, NT:2 * NT - 1, :],
                                    in0=bk.tile[:, 0:(NT - 1) * P].rearrange("p (t c) -> p t c", t=NT - 1), scalar=SCALE,
                                    in1=mask, op0=ALU.mult, op1=ALU.add))
                        free(bk)
                        ch.link(V.tensor_reduce(mx2[:, n % 2, :], Sx[:, n % 2, NT:2 * NT - 1, :], AX.X, ALU.max))
                        ch.link(TT(mst[:, g, 1:NT, h], mst[:, g, 1:NT, h], mx2[:, n % 2, :], ALU.max))
                    TS(nm[:, n % 2, :], mst[:, g, :, h], -1.0, None, ALU.mult).then_inc(S["neg_max_ready"], 1)
                elif op == "probs":
                    g, h = a
                    n = g * SLOTS + h
                    if g == 0:
                        dve.wait_ge(S["probs_ready"], n + 1)
                        ch.link(TT(lst[:, g, 1:NT, h], lst[:, g, 1:NT, h], l2[:, n % 2, :], ALU.add))
                        banks[5].full(dve, ("Tp", n))
                        if n >= 2:
                            pv_done(dve, n - 2)
                        V.tensor_copy(PT[:, n % 2, NT:2 * NT - 1, :], banks[5].tile[:, 0:(NT - 1) * P].rearrange("p (t c) -> p t c", t=NT - 1))\
                            .then_inc(S["prev_probs_turned"], 1)
                        dve.wait_ge(S["prev_probs_turned"], n + 1)
                        free(banks[5])
                    if n == NG * SLOTS - 1:
                        dve.wait_ge(S["probs_ready"], n + 1)
                        dve.sem_inc(S["maxima_sums_ready"], 1)
                elif op == "merge":
                    for g in range(NG):
                        for dst, bk, key in ((mT, banks[g], "mt"), (lT, banks[NG + g], "lt")):
                            bk.full(dve, (key, g))
                            pat = "p (j t) -> p t j" if g > 0 else "p (t j) -> p t j"
                            ch.link(V.tensor_copy(dst[:, g, :].rearrange(pat, t=NT),
                                                  bk.tile[0:SLOTS, :].rearrange("p (t j) -> p t j", t=NT)))
                            free(bk)
                    ch.link(TT(mm_[:, :], mT[:, 0, :], mT[:, 1, :], ALU.max))
                    ch.link(TT(mm_[:, :], mm_[:, :], mT[:, 2, :], ALU.max))
                    for g in range(NG):
                        TT(mT[:, g, :], mT[:, g, :], mm_[:, :], ALU.subtract).then_inc(S["merge_exponents"], 1)
                    dve.wait_ge(S["merge_exps"], 1)
                    ch.link(TT(den[:, :], mT[:, 0, :], lT[:, 0, :], ALU.mult))
                    for g in range(1, NG):
                        dve.wait_ge(S["merge_exps"], g + 1)
                        ch.link(TT(dtmp[:, :], mT[:, g, :], lT[:, g, :], ALU.mult))
                        ch.link(TT(den[:, :], den[:, :], dtmp[:, :], ALU.add))
                    ch.link(V.reciprocal(den[:, :], den[:, :]))
                    for g in range(NG):
                        TT(mT[:, g, :], mT[:, g, :], den[:, :], ALU.mult).then_inc(S["merge_weights"], 1)
                    dve.wait_ge(S["head_pair_out"], NG * HP)
                    for hp in range(HP):
                        for g in range(NG):
                            bk = banks[(hp * NG + g) % 6]
                            bk.full(dve, ("wb", hp, g))
                            ch.link(TT(mtmp[:, :] if g else oT[:, hp, B:R], oU[:, g, hp, :], bk.tile[:, :], ALU.mult))
                            free(bk)
                            if g:
                                ch.link(TT(oT[:, hp, B:R], oT[:, hp, B:R], mtmp[:, :], ALU.add))
                elif op == "sample":
                    for n in range(B * NG):
                        b, g = divmod(n, NG)
                        bk = banks[6 + n % 2]
                        bk.full(dve, ("qb", n))
                        dve.wait_ge(S[f"k_cache_loaded{n % 3}"], 16 * (n // 3 + 1))
                        ch.link(TT(prod[:, :], Kc[:, n % 3, :], bk.tile[:, :], ALU.mult))
                        free(bk)
                        V.tensor_reduce(sS[:, b, g, :], prod[:, :].rearrange("p (h d) -> p h d", h=SLOTS), AX.X, ALU.add)\
                            .then_inc(S["cached_k_used"], 1)
                        dve.wait_ge(S["cached_k_used"], n + 1)
                    ch.link(TT(pself[:, :, :], qS[:, 0, :, :], qS[:, 1, :, :], ALU.mult))
                    ch.link(V.tensor_reduce(sself[:, :, :], pself[:, :, :].rearrange("p g (h d) -> p g h d", h=SLOTS), AX.X, ALU.add))
                    for g in range(NG):
                        for q in range(2):
                            bk = banks[2 * g + q]
                            bk.full(dve, ("sT", g, q))
                            ch.link(TS(pS[:, 4 * q:4 * q + 4, g, 0:NKEYS], bk.tile[0:B, :].rearrange("p (h k) -> p h k", h=4),
                                       SCALE, None, ALU.mult))
                            free(bk)
                    ch.link(TS(pS[:, :, :, NKEYS:NKEYS + 1].rearrange("p h g o -> p g h o"), sself[:, :, :].unsqueeze(3),
                               SCALE, None, ALU.mult))
                    flat = pS[:, :, :, :].rearrange("p h g k -> p h (g k)")
                    nk = NG * (NKEYS + 1)
                    ch.link(V.tensor_reduce(Ms[:, :], flat, AX.X, ALU.max))
                    TT(flat, flat, Ms[:, :].unsqueeze(2).to_broadcast([B, SLOTS, nk]), ALU.subtract).then_inc(S["sample_exponents"], 1)
                    dve.wait_ge(S["sample_exps"], 1)
                    ch.link(V.tensor_reduce(ls[:, :], flat, AX.X, ALU.add))
                    ch.link(V.reciprocal(ls[:, :], ls[:, :]))
                    ch.link(TT(flat, flat, ls[:, :].unsqueeze(2).to_broadcast([B, SLOTS, nk]), ALU.mult))
                    for g in range(NG):
                        ins = TT(SD[:, g, :, :], con[0:B, C_ID:C_ID + B].unsqueeze(1).to_broadcast([B, SLOTS, B]),
                                 pS[:, :, g, NKEYS:NKEYS + 1].to_broadcast([B, SLOTS, B]), ALU.mult)
                    ins.then_inc(S["sample_probs"], 1)
                    banks[5].full(dve, ("pTs",))
                    V.tensor_copy(pTs[:, :, :], banks[5].tile[:, 0:NG * SLOTS * B].rearrange("p (n b) -> p n b", b=B)).then_inc(S["sample_probs_turned"], 1)
                    dve.wait_ge(S["sample_probs_turned"], 1)
                    free(banks[5])
                    banks[7].full(dve, ("so",))
                    ch.link(V.tensor_copy(oT[:, :, 0:B], banks[7].tile[:, 0:HP * B].rearrange("p (h b) -> p h b", b=B)))
                    free(banks[7])
                elif op == "dt":
                    i = ITEM_AT["dt", 0]
                    for hf in range(2):
                        bk = cm_bank(i, 0, hf)
                        bk.full(dve, ("cm", i, 0, hf))
                        ch.link(TS(da[0][:, hf * HALF:(hf + 1) * HALF], bk.tile[0:HEADS, 0:HALF], par[0:HEADS, PW_DTB:PW_DTB + 1], None, ALU.add))
                        free(bk)
                    STT(out=da[1][:, :], in0=da[0][:, :], scalar=-1.0, in1=da[0][:, :], op0=ALU.mult, op1=ALU.min).then_inc(S["dt_operands"], 1)
                    dve.wait_ge(S["dt_activations"], 2)
                    TS(da[3][:, :], da[2][:, :], 1.0, None, ALU.add).then_inc(S["dt_operands"], 1)
                    dve.wait_ge(S["dt_operands"], 2)
                    ch.link(TS(da[5][:, :], da[3][:, :], -1.0, None, ALU.add))
                    ch.link(TS(da[6][:, :], da[5][:, :], 0.0, None, ALU.is_equal))
                    ch.link(TT(da[6][:, :], da[6][:, :], da[2][:, :], ALU.mult))
                    ch.link(TS(da[5][:, :], da[5][:, :], 1e-30, None, ALU.max))
                    ch.link(V.reciprocal(da[5][:, :], da[5][:, :]))
                    ch.link(TT(da[5][:, :], da[5][:, :], da[2][:, :], ALU.mult))
                    dve.wait_ge(S["dt_activations"], 3)
                    ch.link(TT(da[5][:, :], da[5][:, :], da[4][:, :], ALU.mult))
                    ch.link(TT(da[5][:, :], da[5][:, :], da[6][:, :], ALU.add))
                    ch.link(STT(out=dtT[:, :], in0=da[0][:, :], scalar=0.0, in1=da[5][:, :], op0=ALU.max, op1=ALU.add))
                    ch.link(TS(da[7][:, :], dtT[:, :], Acol[:, 0:1], -1.0, ALU.mult, ALU.mult))
                    ch.link(V.memset(onesm[:, 0:T:P], 0.0))
                    ch.link(V.tensor_copy(dsS[:, B:2 * B], dtT[:, 0:B]))
                    ch.link(V.tensor_tensor_scan(acT[:, :], onesm[:, :], da[7][:, B:R], 0.0, ALU.mult, ALU.add))
                    ac3 = acT[:, :].rearrange("p (c l) -> p c l", c=NT)
                    TT(decT[:, :].rearrange("p (c l) -> p c l", c=NT), ac3[:, :, P - 1:P].to_broadcast([HEADS, NT, P]), ac3,
                       ALU.subtract).then_inc(S["dt_operands"], 1)
                    banks[4].full(dve, ("dtr",))
                    ch.link(V.tensor_copy(dtrm[:, :, :, :], banks[4].tile[:, 0:NT * 3 * HEADS].rearrange("p (c q h) -> p c q h", c=NT, q=3)))
                    free(banks[4])
                    ch.link(TS(nac[:, :, :], dtrm[:, :, 1, :], -1.0, None, ALU.mult))
                    banks[5].full(dve, ("dsb",))
                    ch.link(V.tensor_copy(dsb[:, :, :], banks[5].tile[:, 0:UNITS * 2 * B].rearrange("p (u b) -> p u b", u=UNITS)))
                    free(banks[5])
                elif op == "bc":
                    g = a[0]
                    if g > 0:
                        banks[7].full(dve, ("y", 4 * g - 1))
                    banks[5].full(dve, ("CB", g))
                    ch.link(TT(CBm[:, :, :], banks[5].tile[:, :].rearrange("p (c l) -> p c l", c=NT),
                               con[:, C_TRI:C_TRI + P].unsqueeze(1).to_broadcast([P, NT, P]), ALU.mult))
                    free(banks[5])
                elif op == "ssdA":
                    u = a[0]
                    h0 = 2 * u
                    if u > 0:
                        banks[7].full(dve, ("y", u - 1))
                    for e in range(2):
                        bk = banks[5 + e]
                        dve.wait_ge(S["chunk_exps_ready"], 2 * u + e + 1)
                        TT(Lb[:, e, :, :], bk.tile[:, :].rearrange("p (c l) -> p c l", c=NT),
                           dtrm[:, :, 1, h0 + e:h0 + e + 1].to_broadcast([P, NT, P]), ALU.min).then_inc(S["decay_args_ready"], 1)
                        dve.wait_ge(S["decay_args_ready"], 2 * u + e + 1)
                        free(bk)
                    banks[4].full(dve, ("xT", u))
                    x4 = "p c (e d) -> p c e d"
                    ch.link(TT(xdt[:, :, :].rearrange(x4, e=2), banks[4].tile[:, :].rearrange("p (c e d) -> p c e d", c=NT, e=2),
                               dtrm[:, :, 0, h0:h0 + 2].unsqueeze(3).to_broadcast([P, NT, 2, HD]), ALU.mult))
                    free(banks[4])
                    TT(xdec[:, :, :].rearrange(x4, e=2), xdt[:, :, :].rearrange(x4, e=2),
                       dtrm[:, :, 2, h0:h0 + 2].unsqueeze(3).to_broadcast([P, NT, 2, HD]), ALU.mult).then_inc(S["xdt_ready"], 1)
                    for e in range(2):
                        dve.wait_ge(S["decay_matrix_ready"], 2 * u + e + 1)
                        TT(Lb[:, e, :, :], Lb[:, e, :, :], CBm[:, :, :], ALU.mult).then_inc(S["masked_cb_ready"], 1)
                elif op == "ssdB":
                    u = a[0]
                    xs = xu[:, u % 3, :]
                    dcl = par[:, PW_D + u:PW_D + u + 1]
                    dve.wait_ge(S[f"sample_state_loaded{u % 2}"], 16 * (u // 2 + 1))
                    TT(xds[:, :], xs[:, CS:CONV:TAPS], dsb[:, u, B:2 * B], ALU.mult).then_inc(S["sample_xdt_ready"], 1)
                    ch.link(TT(stt_[:, u % 2, :, :], stt_[:, u % 2, :, :], dsb[:, u, 0:B].unsqueeze(2).to_broadcast([P, B, P]), ALU.mult))
                    banks[4].full(dve, ("st", u))
                    if u >= 2:
                        dve.wait_ge(S[f"state_stored{u % 2}"], 16 * (u // 2))
                    dve.wait_ge(S["scaled_c_ready"], 2 * (u + 1))
                    hh = hst[:, u % 2, :, :]
                    ch.link(V.tensor_copy(hh[:, 0, :], banks[4].tile[:, 0:P]))
                    for c in range(1, NT):
                        for e in range(2):
                            o = e * HD
                            ins = STT(out=hh[:, c, o:o + HD], in0=hh[:, c - 1, o:o + HD], scalar=dcol[:, e, c:c + 1],
                                      in1=banks[4].tile[:, c * P + o:c * P + o + HD], op0=ALU.mult, op1=ALU.add)
                            if e == 1 and c == NT - 2:
                                ins.then_inc(S["states_before_ready"], 1)
                                dve.wait_ge(S["states_before_ready"], u + 1)
                            elif c < NT - 1:
                                ch.link(ins)
                    ins.then_inc(S["last_state_ready"], 1)
                    dve.wait_ge(S["last_state_ready"], u + 1)
                    free(banks[4])
                    dve.wait_ge(S["sample_xb_ready"], u + 1)
                    TT(stt_[:, u % 2, :, :], stt_[:, u % 2, :, :], tt[:, :, :], ALU.add).then_inc(S["sample_state_ready"], 1)
                    if u > 0:
                        dve.wait_ge(S["y_gated"], u)
                    dve.wait_ge(S["sample_state_c_ready"], u + 1)
                    ch.link(V.tensor_reduce(y8[:, :], tt[:, :, :], AX.X, ALU.add))
                    ch.link(STT(out=yb[:, 0:B], in0=xs[:, CS:CONV:TAPS], scalar=dcl, in1=y8[:, :], op0=ALU.mult, op1=ALU.add))
                    banks[7].full(dve, ("y", u))
                    ch.link(STT(out=yb[:, B:R], in0=xs[:, 0:T], scalar=dcl, in1=banks[7].tile[:, :], op0=ALU.mult, op1=ALU.add))
                    free(banks[7])
                    dve.wait_ge(S["z_silu_ready"], u + 1)
                    STT(out=ygn[:, u, :], in0=yb[:, :], scalar=0.5, in1=zs[:, u % 2, :], op0=ALU.mult, op1=ALU.mult).then_inc(S["y_gated"], 1)
                elif op == "gnorm":
                    g = a[0]
                    dve.wait_ge(S["scaled_rows_ready"], KD + g + 1)
                    ch.link(V.reciprocal(grs[:, :], grs[:, :]))
                    for k in range(PER_GROUP):
                        u = g * PER_GROUP + k
                        ins = STT(out=ygn[:, u, :], in0=ygn[:, u, :], scalar=par[:, PW_SNORM + u:PW_SNORM + u + 1], in1=grs[:, :],
                                  op0=ALU.mult, op1=ALU.mult)
                    ins.then_inc(S["y_normed"], 1)
                elif op == "parts":
                    for u in range(UNITS):
                        dve.wait_ge(S["y_high_ready"], u + 1)
                        TT(yL[:, u, :], ygn[:, u, :], yH[:, u, :].bitcast(F32), ALU.subtract).then_inc(S["y_low_ready"], 1)
                    for hp in range(HP):
                        dve.wait_ge(S["o_high_ready"], hp + 1)
                        TT(oL[:, hp, :], oT[:, hp, :], oH[:, hp, :].bitcast(F32), ALU.subtract).then_inc(S["o_low_ready"], 1)
                elif op == "mix":
                    for s in range(2):
                        k = 2 * a[0] + s
                        dve.wait_ge(S["mix_high_ready"], k + 1)
                        TT(mL[:, k, :], mix[:, k, :], mH[:, k, :].bitcast(F32), ALU.subtract).then_inc(S["mix_low_ready"], 1)


def _tables():
    con = np.zeros((P, NCONST), np.float32)
    q, k = np.arange(P)[:, None], np.arange(P)[None, :]
    low = np.float32(-1e30)
    con[:, C_ID:C_ID + P] = np.eye(P)
    con[:, C_CAUSAL:C_CAUSAL + P] = np.where(k <= q, 0, low)
    con[:, C_PREV:C_PREV + P] = np.where(k >= q, 0, low)
    con[:, C_STRIDED:C_STRIDED + P] = np.where((k <= q) & ((q - k) % (DILATIONS[2] // NT) == 0), 0, low)
    con[:, C_TRI:C_TRI + P] = k >= q
    half = HD // 2
    inv = (10000.0 ** (-np.arange(half) / half)).astype(np.float32)
    p = np.arange(P)
    pos = [P * t + p for t in range(NT)] + [NT * p + t for t in range(NT)] + [np.full(P, WINDOWS[-1])]
    for t, x in enumerate(pos):
        ang = x.astype(np.float32)[:, None] * inv[None, :]
        con[:, C_COS + t * half:C_COS + (t + 1) * half] = np.cos(ang)
        con[:, C_SIN + t * half:C_SIN + (t + 1) * half] = np.sin(ang)
    sel = np.zeros((HEADS, UNITS, P), np.float32)
    for h in range(HEADS):
        sel[h, h // 2, (h % 2) * HD:(h % 2 + 1) * HD] = 1
    return con, sel


def kernel(**inputs):
    from concourse import bacc
    from concourse.bass_utils import run_bass_kernel_spmd

    x = {n: np.ascontiguousarray(v) for n, v in inputs.items()}
    f = np.float32

    def rows_to_tiles(a, n):
        return np.ascontiguousarray(np.swapaxes(a.reshape(n, P, *a.shape[1:]), 0, 1))

    w_in, w_ssd, w_att, w_out = x["w_in"][0], x["w_ssd_br"][0], x["w_att_br"][0], x["w_out"][0]
    wpack = np.zeros((len(ITEMS), P, SLOT), f)
    for i, it in enumerate(ITEMS):
        kind, j = it[0], it[1]
        if kind == "rm":
            c = OFF[it[2]] + j * DATT
            a = w_in[512 * it[3]:512 * (it[3] + 1), c:c + DATT]
        elif kind == "dt":
            a = np.zeros((D, P), f)
            a[:, :HEADS] = w_in[:, OFF["dt"]:OFF["dt"] + HEADS]
        elif kind == "bc":
            a = np.concatenate([w_in[:, o + j * P:o + (j + 1) * P] for o in (OFF_B, OFF_C)], axis=1)
        elif kind == "bs":
            a = w_ssd[:, j * P:(j + 1) * P]
        elif kind == "ba":
            a = w_att[:, j * 512:(j + 1) * 512]
        elif kind == "wo":
            a = w_out[:, j * 2 * P:(j + 1) * 2 * P]
        else:
            c = {"x": OFF_X}.get(kind, OFF.get(kind)) + j * 2 * P
            a = w_in[:, c:c + 2 * P]
        k = a.shape[0] // P
        wpack[i, :, :k * a.shape[1]] = rows_to_tiles(a, k).reshape(P, -1)

    par = np.zeros((P, NPARAM), f)
    par[:, PW_NORM:PW_CONV] = x["norm_w"][0].reshape(KD, P).T
    par[:, PW_CONV:PW_CONVB] = x["conv_w"][0].reshape(TAPS, XU, P).transpose(2, 1, 0).reshape(P, -1)
    par[:, PW_CONVB:PW_SNORM] = x["conv_b"][0].reshape(XU, P).T
    par[:, PW_SNORM:PW_D] = x["ssd_norm_w"][0].reshape(UNITS, P).T
    par[:, PW_D:PW_DTB] = np.repeat(x["d_skip"][0], HD).reshape(UNITS, P).T
    par[:HEADS, PW_DTB] = x["dt_bias"][0]
    par[:HEADS, PW_ALOG] = x["a_log"][0]
    par[:, PW_QW:PW_KW] = x["q_norm_w"][0]
    par[:, PW_KW:NPARAM] = x["k_norm_w"][0]
    con, sel = _tables()

    rows = np.concatenate([x["x_sample"][:, 0], x["x_prompt"][0]], axis=0)
    arrays = {
        "in_xT": rows_to_tiles(np.ascontiguousarray(rows.T), KD),
        "in_weights": wpack,
        "in_params": par,
        "in_consts": con,
        "in_sel": sel,
        "in_state_conv": np.ascontiguousarray(x["state_conv"][0].reshape(B, TAPS - 1, XU, P).transpose(3, 2, 0, 1)),
        "in_state_ssm": np.ascontiguousarray(x["state_ssm"][0].reshape(B, UNITS, P, NSTATE).transpose(1, 2, 0, 3)),
    }
    for w in WINDOWS:
        arrays[f"in_cache{w}"] = x[f"cache_kv_w{w}"][0].reshape(B, w, 2 * DATT)
    outs = {"out_y": (P, KD, R), "out_tail": (P, XU, TAIL), "out_ssm_p": (UNITS, P, P), "out_ssm_s": (UNITS, P, B, P)}
    for w in WINDOWS:
        outs[f"out_kvp{w}"] = (min(w, T), 2 * DATT)
        outs[f"out_kvs{w}"] = (B, w, 2 * DATT)

    nc = bacc.Bacc("TRN2", target_bir_lowering=False, num_devices=1)
    ap = {n: nc.dram_tensor(n, a.shape, F32, kind="ExternalInput").ap() for n, a in arrays.items()}
    ap.update({n: nc.dram_tensor(n, s, F32, kind="ExternalOutput").ap() for n, s in outs.items()})
    hybrid_kernel(nc, ap["in_xT"], ap["in_weights"], ap["in_params"], ap["in_consts"], ap["in_sel"],
                  ap["in_state_conv"], ap["in_state_ssm"], [ap[f"in_cache{w}"] for w in WINDOWS],
                  ap["out_y"], ap["out_tail"], ap["out_ssm_p"], [ap[f"out_kvp{w}"] for w in WINDOWS],
                  ap["out_ssm_s"], [ap[f"out_kvs{w}"] for w in WINDOWS])
    r = run_bass_kernel_spmd(nc, [arrays], core_ids=[0]).results[0]

    y = np.swapaxes(r["out_y"], 0, 1).reshape(D, R).T
    tail = np.swapaxes(r["out_tail"], 0, 1).reshape(DXBC, TAIL)
    conv_p = tail[:, :TAPS - 1].T.reshape(1, 1, TAPS - 1, DXBC)
    conv_s = tail[:, TAPS - 1:].reshape(DXBC, B, TAPS - 1).transpose(1, 2, 0).reshape(1, B, TAPS - 1, DXBC)
    ssm_p = np.swapaxes(r["out_ssm_p"], 1, 2).reshape(1, 1, HEADS, HD, NSTATE)
    ssm_s = r["out_ssm_s"].transpose(2, 0, 1, 3).reshape(1, B, HEADS, HD, NSTATE)
    kvp = [r[f"out_kvp{w}"].reshape(1, 1, min(w, T), 2, SLOTS, HD) for w in WINDOWS]
    kvs = [r[f"out_kvs{w}"].reshape(1, B, w, 2, SLOTS, HD) for w in WINDOWS]
    out = [y[B:].reshape(1, T, D), y[:B].reshape(B, 1, D), conv_p, ssm_p, *kvp, conv_s, ssm_s, *kvs]
    return tuple(np.ascontiguousarray(o) for o in out)
```

```python
from contextlib import ExitStack

import numpy as np
import concourse.bass as bass
from concourse import mybir

F32 = mybir.dt.float32
F32R = mybir.dt.float32r
ALU = mybir.AluOpType
ACT = mybir.ActivationFunctionType
AX = mybir.AxisListType

P = 128
D = 1024
T = 512
B = 8
R = B + T
HALF = R // 2
KD = D // P
SLOT = 2048
NT = T // P
DSSD, GROUPS, NSTATE, HEADS = 2048, 4, 128, 32
DXBC = DSSD + 2 * GROUPS * NSTATE
UNITS = DSSD // P
PER_GROUP = UNITS // GROUPS
SLOTS, HD, NG = 8, 64, 3
DATT = SLOTS * HD
HP = SLOTS // 2
WINDOWS = (128, 512, 2048)
DILATIONS = (1, 4, 16)
EPS = 1e-6
EXP_LN = 6
SCALE = HD ** -0.5
TAPS = 4
XU = DXBC // P
S0 = TAPS - 1 + T
BUF = S0 + TAPS * B
CONV = BUF - (TAPS - 1)
CS = T + TAPS - 1
TAIL = (TAPS - 1) * (1 + B)
RING = 7
NKEYS = P

_SIZES = [DSSD, DXBC, HEADS, NG * DATT, NG * DATT, NG * DATT, DATT, D, D]
OFF = dict(zip(["z", "xbc", "dt", "q", "k", "v", "za", "gs", "ga"], np.cumsum([0] + _SIZES[:-1]).tolist()))
OFF_X, OFF_B, OFF_C = OFF["xbc"], OFF["xbc"] + DSSD, OFF["xbc"] + DSSD + GROUPS * NSTATE


def weight_items():
    items = [("rm", g, s, half) for g in range(NG) for s in "qkv" for half in range(2)]
    items += [("za", 0), ("za", 1), ("dt", 0)]
    for g in range(GROUPS):
        items.append(("bc", g))
        for j in range(2 * g, 2 * g + 2):
            items += [("x", j), ("z", j)]
    items += [("gs", 0), ("gs", 1), ("bs", 0), ("bs", 1), ("bs", 2), ("bs", 3)]
    for j in range(2, 4):
        items += [("gs", j), ("bs", 2 * j), ("bs", 2 * j + 1)]
    for j in range(2):
        items += [("ga", 2 * j), ("ga", 2 * j + 1), ("ba", j)]
    items += [("wo", j) for j in range(4)]
    return items


ITEMS = weight_items()
ITEM_AT = {it: i for i, it in enumerate(ITEMS)}
POOL_SPLITS = ("x", "z")
BESIDE_HEADS = {1: {0: 7}, 2: {0: 7, 1: 5}}
SPREAD_FIRST = 5
SHAPES = {"rm": (4, 512), "dt": (KD, P), "bs": (UNITS, P), "ba": (4, 512)}


def item_units(i):
    return tuple(range({"rm": 0, "dt": 1, "bs": 1, "ba": 4}.get(ITEMS[i][0], 2)))


def plan():
    out = [("squares",), ("split", 0), ("init",)]

    def proj(*item, unit=None):
        i = ITEM_AT[item]
        if i + 1 < len(ITEMS) and not unit and ("split", i + 1) not in out:
            out.append(("split", i + 1))
        units = item_units(i) if unit is None else (unit,)
        out.append(("proj", i, units))
        return ("use", i, units)

    za_uses = []

    def whole(*item):
        out.append(proj(*item))

    for g in range(NG):
        for s in "qkv":
            whole("rm", g, s, 0)
            if (g, s) == (0, "q"):
                out.append(("rope",))
            if s == "v":
                out.append(("turn", g, 0))
            whole("rm", g, s, 1)
        out.append(("turn", g, 1))
        if g + 1 < NG:
            out.append(("split", ITEM_AT["rm", g + 1, "q", 1]))
            beside = [("rowtile", g + 1, t, k) for t in BESIDE_HEADS[g + 1] for k in range(KD)]
        else:
            beside = []
            for unit in range(2):
                za_uses.append(proj("za", 0, unit=unit))
                _, i, units = out.pop()
                beside += [("proj", i, units, k) for k in range(KD)]
        total, steps = len(beside), 3 * SLOTS + 2
        count = 0
        for h in range(SLOTS + 2):
            for step in (("scores", g, h), ("probs", g, h - 1), ("values", g, h - 2)):
                if 0 <= step[2] < SLOTS:
                    out.append(step)
                    count += 1
                    while beside and total - len(beside) < total * (count + 2) / steps:
                        out.append(beside.pop(0))
    def tiles(item, unit):
        use = proj(*item, unit=unit)
        _, i, units = out.pop()
        return [("proj", i, units, k) for k in range(KD)], use

    def pieces():
        for item, unit in ((("za", 1), 1), (("dt", 0), 0), (("bc", 0), 0)):
            ks, use = tiles(item, unit)
            for k in ks:
                out.append(k)
                if k is ks[-1] and item[0] == "za":
                    out.append(use)
                yield use

    n, piece = B * NG, pieces()
    out += [("barrier",)] + za_uses
    use = proj("za", 1, unit=0)
    out += [use, ("turnq",), ("merge",)]
    for i in range(n):
        out.append(("key", i))
        if i == 3:
            out.append(("exps",))
        if i == n // 2:
            out.append(("ownkeys",))
        use = next(piece)
        if use[1] == ITEM_AT["dt", 0]:
            use_dt = use
    out.append(("key", n))
    for i in range(SPREAD_FIRST):
        if i == 2:
            out.append(("samplemax",))
        out.append(("spread", i))
    out += [("sampleprobs",), ("ownvalues",)]
    late = NG * HP - SPREAD_FIRST
    for i in range(n):
        out.append(("value", i))
        if i * late // n > (i - 1) * late // n:
            out.append(("spread", SPREAD_FIRST + i * late // n))
    out += [("gated",), ("barrier",), use_dt, ("dt",)]
    for g in range(GROUPS):
        u = PER_GROUP * g
        if g > 0:
            use = proj("bc", g, unit=0)
            out.append(("ssdS", u - 1))
        out.append(use)
        use = proj("bc", g, unit=1)
        out += [("ssdY", u - 1), ("ssdZ", u - 1)] if g > 0 else [("dtrows",)]
        out.append(use)
        use = proj("x", 2 * g, unit=0)
        out.append(("bc", g))
        if g > 0:
            out.append(("gnorm", g - 1))
        out.append(use)
        use = proj("x", 2 * g, unit=1)
        out += [("ssdA", u), use]
        for kind, j in (("z", 2 * g), ("x", 2 * g + 1), ("z", 2 * g + 1)):
            use = proj(kind, j, unit=0)
            out += [("ssdS", u), use]
            if g > 0 and u == PER_GROUP * g + 1:
                out.append(("gscale", g - 1))
            use = proj(kind, j, unit=1)
            out += [("ssdY", u), ("ssdA", u + 1), ("ssdZ", u), use]
            u += 1
    uses = [proj("gs", 0, unit=0)]
    out.append(("ssdS", UNITS - 1))
    uses.append(proj("gs", 0, unit=1))
    out += [("ssdY", UNITS - 1), ("ssdZ", UNITS - 1), ("gnorm", GROUPS - 1)]
    uses += [proj("gs", 1, unit=0), proj("gs", 1, unit=1)]
    out += [("gscale", GROUPS - 1), ("barrier",)] + uses + [("parts",)]
    for j in range(4):
        if j > 1:
            whole("gs", j)
        whole("bs", 2 * j)
        whole("bs", 2 * j + 1)
    for j in range(2):
        whole("ga", 2 * j)
        whole("ga", 2 * j + 1)
        whole("ba", j)
        out += [("mix", 2 * j), ("mix", 2 * j + 1)]
    for j in range(4):
        whole("wo", j)
    return out


PLAN = plan()

PW_NORM, PW_CONV = 0, KD
PW_CONVB = PW_CONV + XU * TAPS
PW_SNORM = PW_CONVB + XU
PW_D = PW_SNORM + UNITS
PW_DTB, PW_ALOG = PW_D + UNITS, PW_D + UNITS + 1
PW_QW = PW_ALOG + 1
PW_KW = PW_QW + HD
NPARAM = PW_KW + HD
C_ID, C_CAUSAL, C_PREV, C_STRIDED, C_TRI = 0, P, 2 * P, 3 * P, 4 * P
C_PLACE = 5 * P
RT = 2 * NT + 1
C_COS = C_PLACE + 2 * SLOTS * B - B
C_SIN = C_COS + RT * HD // 2
NCONST = C_SIN + RT * HD // 2


class Bank:

    def __init__(self, tile, filled, freed):
        self.tile, self.filled, self.freed = tile, filled, freed
        self.uses, self.frees = {}, 0

    def take(self, pe, key):
        assert key not in self.uses, key
        if self.frees:
            pe.wait_ge(self.freed, self.frees)
        self.uses[key] = len(self.uses) + 1
        self.frees += 1

    def full(self, eng, key):
        eng.wait_ge(self.filled, self.uses[key])


class Chain:

    def __init__(self, eng, sem):
        self.eng, self.sem, self.n = eng, sem, 0

    def link(self, ins):
        self.n += 1
        ins.then_inc(self.sem, 1)
        self.eng.wait_ge(self.sem, self.n)


class Arena:

    def __init__(self, nc, base, end):
        self.nc, self.at, self.end = nc, base, end

    def tile(self, name, shape, dt=F32):
        t = self.nc.alloc_sbuf_tensor_at(name, shape, dt, offset=self.at)
        self.at += (int(np.prod(shape[1:])) * 4 + 31) // 32 * 32
        assert self.at <= self.end, (name, self.at, self.end)
        return t


def hybrid_kernel(nc, xT, wpack, params, consts, sel_in, state_conv, ssm_in, caches,
                  y_out, tail_out, ssmp_out, kvp_out, ssms_out, kvs_out):
    ctx = ExitStack()
    with ctx:
        def sem(name):
            return ctx.enter_context(nc.semaphore(name))

        def sb(name, shape, dt=F32):
            return ctx.enter_context(nc.sbuf_tensor(name, shape, dt))

        xH = sb("xH", [P, KD, R], F32R)
        xL = sb("xL", [P, KD, R], F32R)
        raw = sb("w_raw", [P, 2, SLOT])
        wH = sb("wH", [P, 2, SLOT], F32R)
        wL = sb("wL", [P, 2, SLOT], F32R)
        par = sb("par", [P, NPARAM])
        con = sb("con", [P, NCONST])
        ones = sb("ones", [P, P])
        epsc = sb("epsc", [P, 1])
        oT = sb("oT", [P, HP, R])
        base = (nc.sbuf_base + 31) // 32 * 32
        end = nc.sbuf_usable_end
        sb("arena", [P, (end - base - 64) // 4])
        ident = con[:, C_ID:C_ID + P]

        a0 = Arena(nc, base, end)
        qS = a0.tile("qS", [B, 3, NG, T])
        oU = a0.tile("oU", [P, NG, HP, T])
        mst = a0.tile("mst", [P, NG, NT, SLOTS])
        lst = a0.tile("lst", [P, NG, NT, SLOTS])
        a1 = Arena(nc, a0.at, end)
        st = a1.tile("st", [P, 2, NT, T])
        qT = a1.tile("qT", [P, HP, T])
        kT = a1.tile("kT", [P, HP, T])
        vv = a1.tile("vv", [P, NT, T])
        ropeA = a1.tile("ropeA", [P, 2, RT, HD])
        ropeB = a1.tile("ropeB", [P, 2, RT, HD])
        pt_at = a1.at
        sq = a1.tile("sq", [P, 2, T])
        ss = a1.tile("ss", [P, 2, SLOTS])
        rst = a1.tile("rst", [P, 2, SLOTS])
        qn = a1.tile("qn", [P, T])
        t1 = a1.tile("t1", [P, T])
        t2 = a1.tile("t2", [P, T])
        Sx = a1.tile("Sx", [P, 2, 2 * NT - 1, P])
        PT = Arena(nc, pt_at, end).tile("PT", [P, 2, 2 * NT - 1, P])
        l2 = a1.tile("l2", [P, 2, NT - 1])
        mx2 = a1.tile("mx2", [P, 2, NT - 1])
        nm = a1.tile("nm", [P, 2, NT])
        ai = Arena(nc, a0.at, end)
        xw = ai.tile("xw", [P, KD, R])
        xsq = ai.tile("xsq", [P, KD, R])
        rs = ai.tile("rs", [P, R])

        a2 = Arena(nc, a0.at, end)
        sel = a2.tile("sel", [SLOTS, HP, P])
        selR = a2.tile("selR", [SLOTS, HP, P], F32R)
        mH_ = a2.tile("mH_", [SLOTS, NG, T], F32R)
        mT = a2.tile("mT", [SLOTS, NG, T])
        lT = a2.tile("lT", [SLOTS, NG, T])
        mL_ = nc.alloc_sbuf_tensor_at("mL_", [SLOTS, NG, T], F32R, offset=a2.at - 4 * NG * T)
        mm_ = a2.tile("mm_", [SLOTS, T])
        den = a2.tile("den", [SLOTS, T])
        dtmp = a2.tile("dtmp", [SLOTS, T])
        mtmp = a2.tile("mtmp", [P, T])
        ring = a2.tile("ring", [P, RING, T])
        KT = a2.tile("KT", [P, 2, HP, NKEYS])
        qd = a2.tile("qd", [P, NG * HP * B, 2])
        sS = a2.tile("sS", [P, NG, SLOTS, B])
        pself = a2.tile("pself", [B, NG, T])
        sself = a2.tile("sself", [B, NG, SLOTS])
        pS = a2.tile("pS", [SLOTS * B, NG * NKEYS + NG])
        Ms = a2.tile("Ms", [SLOTS * B, 1])
        nMs = a2.tile("nMs", [SLOTS * B, 1])
        ls = a2.tile("ls", [SLOTS * B, 1])
        pTs = a2.tile("pTs", [P, NG, SLOTS, B])
        pB = a2.tile("pB", [B, SLOTS, NG])
        SD = a2.tile("SD", [B, NG, SLOTS, B])
        gta = a2.tile("gta", [P, R])
        zg = a2.tile("zg", [P, HP, R])

        a3 = Arena(nc, base, end)
        ygn = a3.tile("ygn", [P, UNITS, R])
        ceil_ = a3.at
        stc = a3.tile("stc", [P, XU, B, TAPS - 1])
        tail = a3.tile("tail", [P, XU, TAIL])
        buf = a3.tile("buf", [P, 2, BUF])
        cacc = a3.tile("cacc", [P, CONV])
        cth = a3.tile("cth", [P, CONV])
        wcv = a3.tile("wcv", [P, XU, TAPS + 1])
        BT = a3.tile("BT", [P, CONV])
        CT = a3.tile("CT", [P, CONV])
        xu = a3.tile("xu", [P, 3, CONV])
        Brm = a3.tile("Brm", [P, NT, P])
        CBm = a3.tile("CBm", [P, NT, P])
        BCb = a3.tile("BCb", [P, 2, B, P])
        zs = a3.tile("zs", [P, 2, R])
        ztn = a3.tile("ztn", [P, R])
        xdt = a3.tile("xdt", [P, NT, P])
        xdec = a3.tile("xdec", [P, NT, P])
        gn_at = a3.at
        Lb = a3.tile("Lb", [P, 2, NT, P])
        Eb = a3.tile("Eb", [P, 2, T])
        dcol = a3.tile("dcol", [P, 2, NT])
        hst = a3.tile("hst", [P, 2, NT, P])
        dtrm = a3.tile("dtrm", [P, NT, 3, HEADS])
        nac = a3.tile("nac", [P, NT, HEADS])
        dsb = a3.tile("dsb", [P, UNITS, 2 * B])
        stt_ = a3.tile("stt_", [P, 2, B, P])
        tt = a3.tile("tt", [P, B, P])
        yb = a3.tile("yb", [P, R])
        xds = a3.tile("xds", [P, B])
        y8 = a3.tile("y8", [P, B])
        acH = a3.tile("acH", [HEADS, T], F32R)
        acL = a3.tile("acL", [HEADS, T], F32R)
        idR = a3.tile("idR", [HEADS, HEADS], F32R)
        ad = Arena(nc, base, ceil_)
        da = [ad.tile(f"da{i}", [HEADS, R]) for i in range(8)]
        onesm = ad.tile("onesm", [HEADS, T])
        acT = ad.tile("acT", [HEADS, T])
        dtT = ad.tile("dtT", [HEADS, R])
        decT = ad.tile("decT", [HEADS, T])
        dsS = ad.tile("dsS", [HEADS, 2 * B])
        Acol = ad.tile("Acol", [HEADS, 1])
        sel3 = ad.tile("sel3", [HEADS, UNITS, P])
        gsq = Arena(nc, gn_at, gn_at + 8192)
        sq2 = gsq.tile("sq2", [P, 2, R])
        grs = con[:, C_COS:C_COS + R]

        a4 = Arena(nc, base, end)
        yL = a4.tile("yL", [P, UNITS, R], F32R)
        yH = a4.tile("yH", [P, UNITS, R], F32R)
        oH = a4.tile("oH", [P, HP, R], F32R)
        oL = a4.tile("oL", [P, HP, R], F32R)
        mix = a4.tile("mix", [P, KD, R])
        gate = a4.tile("gate", [P, 4, R])
        tmpg = a4.tile("tmpg", [P, R])
        a5 = Arena(nc, base, end)
        mH = a5.tile("mH", [P, KD, R], F32R)
        mL = a5.tile("mL", [P, KD, R], F32R)
        xres = a5.tile("xres", [P, KD, R])
        outb = a5.tile("outb", [P, 2, R])

        banks = [Bank(ctx.enter_context(nc.psum_tensor(f"bank{i}", [P, 512], F32)),
                      sem(f"filled{i}"), sem(f"freed{i}")) for i in range(8)]

        names = """squares_added ac_parts_ready act_order b_rows_ready bc_spread_ready cache_shifted cached_v_used chunk_decay_kept
            chunk_exps_ready constants_set conv_ready conv_rows_placed conv_state_loaded conv_summed
            conv_tail_kept conv_tail_stored conv_tanh conv_weights_ready decay_args_ready
            decay_matrix_ready decays_ready dt_activations dt_operands dve_order even_head_summed
            gate_ready gate_used half_item_used head_pair_out head_scales_ready head_sums_ready
            k_stored keys_scored keys_turned last_state_ready masked_cb_ready maxima_sums_ready
            merge_exponents merge_exps merge_weights mix_high_ready mix_low_ready mix_ready
            neg_max_ready o_high_ready o_low_ready out_ready phase_ended prev_probs_turned
            probs_ready probs_turned qk_columns_ready qk_normed qk_rows_ready qk_squared
            residual_loaded rope_sine_ready row_scale_ready rows_squared sample_decayed
            sample_dt_ready sample_exponents sample_exps sample_probs sample_probs_turned
            sample_q_ready sample_scores_kept sample_state_c_ready sample_state_loaded0
            sample_state_loaded1 sample_state_ready sample_state_stored0 sample_state_stored1
            sample_xb_ready sample_xdt_ready scaled_c_ready scaled_rows_ready selectors3_loaded
            selectors_loaded self_scores_ready square_summed state_stored0 state_stored1
            states_before_ready tables_loaded v_rows_ready v_stored weight_high_ready
            weight_low_ready weights_loaded0 weights_loaded1 x_high_ready x_low_ready xdt_ready
            y_gated y_high_ready y_low_ready y_normed y_squared y_stored0 y_stored1 z_silu_ready
            z_tanh_ready za_applied za_tanh_ready""".split()
        names += [f"rows_loaded{k}" for k in range(KD)]
        names += [f"cache_loaded{i}" for i in range(RING)]
        S = {n: sem("s_" + n) for n in names}
        ends = {}

        def cm_units():
            out, c = {}, 0
            for i, it in enumerate(ITEMS):
                for s in item_units(i):
                    out[i, s] = c
                    c += 1
            return out

        CMU = cm_units()

        def cm_bank(i, s, hf):
            if ITEMS[i] == ("za", 0):
                return banks[((2, 3), (5, 7))[s][hf]]
            if ITEMS[i] == ("gs", 1):
                return banks[((4, 7), (5, 6))[s][hf]]
            return banks[2 * (CMU[i, s] % 2) + hf]

        def wslot(w, i):
            k, n = SHAPES.get(ITEMS[i][0], (KD, 2 * P))
            return w[:, i % 2, 0:k * n].rearrange("p (k n) -> p k n", k=k)

        def qk_count(g, si, t):
            return (g * 2 + si) * (NT + 1) + t

        CV = {}
        for i, it in enumerate(ITEMS):
            for s in range(2):
                if it[0] == "bc":
                    CV[i, s] = (len(CV), UNITS + s * GROUPS + it[1])
                elif it[0] == "x":
                    CV[i, s] = (len(CV), 2 * it[1] + s)
        CV_BC = [CV[ITEM_AT["bc", g], 1][0] + 1 for g in range(GROUPS)]
        CV_X = [CV[ITEM_AT["x", u // 2], u % 2][0] + 1 for u in range(UNITS)]

        def pv_done(eng, n):
            if n % 2:
                g, hp = n // SLOTS, n % SLOTS // 2
                banks[6].full(eng, ("O", g, hp))
            else:
                eng.wait_ge(S["even_head_summed"], n // 2 + 1)

        def row_bank(g, s, t):
            return banks[BESIDE_HEADS.get(g, {}).get(t, t) if s == "q" else t]

        def spread_bank(i):
            return banks[((7, 5) if i < 2 else (7, 6) if i < SPREAD_FIRST else (4, 6))[i % 2]]

        merge_banks = [banks[i] for i in (2, 6, 0, 3, 7, 1)]
        block = ctx.enter_context(nc.Block())

        @block.tensor
        def _(pe):
            nbar = [0]
            turn_c = [0]

            def barrier():
                nbar[0] += 1
                pe.drain().then_inc(S["phase_ended"], 1)
                pe.wait_ge(S["phase_ended"], 5 * nbar[0])

            def row_columns(g, t):
                return slice(0, P) if t == NT else (slice(B + P * t, B + P * (t + 1)) if g == 0 else slice(B + t, R, NT))

            def proj_rows(i, g, s, half):
                for t in range(NT + 1):
                    if s == "q" and t in BESIDE_HEADS.get(g, {}):
                        continue
                    bk = row_bank(g, s, t)
                    if half == 0:
                        bk.take(pe, ("rm", g, s, t))
                    cols = row_columns(g, t)
                    for k in range(4):
                        kk = 4 * half + k
                        if t == 0 and (g, s) == (0, "q"):
                            pe.wait_ge(S["x_low_ready"], kk + 1)
                        for n, (a, b) in enumerate(((xH, wH), (xL, wH), (xH, wL))):
                            mm = pe.matmul(bk.tile[:, :], a[:, kk, cols], wslot(b, i)[:, k, :],
                                           start=(kk == 0 and n == 0), stop=(kk == KD - 1 and n == 2))
                    if half == 1:
                        mm.then_inc(bk.filled, 1)
                    elif t == NT:
                        mm.then_inc(S["half_item_used"], 1)
                ends[i] = (banks[NT].filled, banks[NT].uses["rm", g, s, NT]) if half else (S["half_item_used"], i // 2 + 1)

            def proj_cols(i, units, tile, kind, j):
                srcH, srcL = {"bs": (yH, yL), "ba": (oH, oL), "wo": (mH, mL)}.get(kind, (xH, xL))
                nk = SHAPES.get(kind, (KD,))[0]
                if kind == "ba":
                    pe.wait_ge(S["o_low_ready"], HP)
                for s in units:
                    bk = [cm_bank(i, s, hf) for hf in range(2)]
                    for hf in range(2):
                        if tile in (None, 0):
                            bk[hf].take(pe, ("cm", i, s, hf))
                    for k in range(nk) if tile is None else (tile,):
                        if kind == "bs" and j == 0:
                            pe.wait_ge(S["y_low_ready"], k + 1)
                        if kind == "wo" and j == 0 and s == 0:
                            pe.wait_ge(S["mix_low_ready"], k + 1)
                        for n, (w, x) in enumerate(((wH, srcH), (wH, srcL), (wL, srcH))):
                            for hf in range(2):
                                mm = pe.matmul(bk[hf].tile[:, 0:HALF], wslot(w, i)[:, k, s * P:(s + 1) * P],
                                               x[:, k, hf * HALF:(hf + 1) * HALF],
                                               start=(k == 0 and n == 0), stop=(k == nk - 1 and n == 2))
                                if k == nk - 1 and n == 2:
                                    mm.then_inc(bk[hf].filled, 1)
                ends[i] = (bk[1].filled, bk[1].uses["cm", i, s, 1])

            for step in PLAN:
                op, a = step[0], step[1:]
                if op == "barrier":
                    barrier()
                elif op == "init":
                    pe.wait_ge(S["constants_set"], 2)
                    pe.wait_ge(S["squares_added"], 1)
                    for hf in range(2):
                        banks[hf].take(pe, ("ms", hf))
                        pe.matmul(banks[hf].tile[:, 0:HALF], ones[:, :], xsq[:, 0, hf * HALF:(hf + 1) * HALF],
                                  start=True, stop=True).then_inc(banks[hf].filled, 1)
                elif op == "proj":
                    i = a[0]
                    pe.wait_ge(S["weight_low_ready"], i + 1)
                    it = ITEMS[i]
                    if it[0] == "rm":
                        proj_rows(i, *it[1:])
                    else:
                        proj_cols(i, a[1], a[2] if len(a) > 2 else None, *it)
                elif op == "rowtile":
                    g, t, kk = a
                    i = ITEM_AT["rm", g, "q", kk // 4]
                    pe.wait_ge(S["weight_low_ready"], i + 1)
                    bk = row_bank(g, "q", t)
                    if kk == 0:
                        bk.take(pe, ("rm", g, "q", t))
                    for n, (x, w) in enumerate(((xH, wH), (xL, wH), (xH, wL))):
                        mm = pe.matmul(bk.tile[:, :], x[:, kk, row_columns(g, t)], wslot(w, i)[:, kk % 4, :],
                                       start=(kk == 0 and n == 0), stop=(kk == KD - 1 and n == 2))
                    if kk == KD - 1:
                        mm.then_inc(bk.filled, 1)
                elif op == "turn":
                    g, si = a
                    pe.wait_ge(S["tables_loaded"], 32)
                    for t in range(NT):
                        pe.wait_ge(S["qk_rows_ready"], qk_count(g, si, t) + 1)
                        bk = banks[5 + turn_c[0] % 3]
                        turn_c[0] += 1
                        bk.take(pe, ("turn", g, si, t))
                        for hp in range(HP):
                            mm = pe.transpose(bk.tile[:, hp * P:(hp + 1) * P], st[:, si, t, hp * P:(hp + 1) * P], ident)
                        mm.then_inc(bk.filled, 1)
                elif op == "scores":
                    g, h = a
                    n, o, hp = g * SLOTS + h, HD * (h % 2), h // 2
                    if h == 0:
                        pe.wait_ge(S["qk_columns_ready"], 2 * NT * (g + 1))
                    bk = banks[n % 2]
                    bk.take(pe, ("S", n))
                    for t in range(NT):
                        mm = pe.matmul(bk.tile[:, t * P:(t + 1) * P], qT[o:o + HD, hp, t * P:(t + 1) * P],
                                       kT[o:o + HD, hp, t * P:(t + 1) * P], start=True, stop=True)
                    mm.then_inc(bk.filled, 1)
                    if g == 0:
                        bk = banks[2 + n % 2]
                        bk.take(pe, ("Sp", n))
                        for t in range(1, NT):
                            mm = pe.matmul(bk.tile[:, (t - 1) * P:t * P], qT[o:o + HD, hp, t * P:(t + 1) * P],
                                           kT[o:o + HD, hp, (t - 1) * P:t * P], start=True, stop=True)
                        mm.then_inc(bk.filled, 1)
                elif op == "probs":
                    g, h = a
                    n = g * SLOTS + h
                    pe.wait_ge(S["probs_ready"], n + 1)
                    banks[4].take(pe, ("T", n))
                    for t in range(NT):
                        mm = pe.transpose(banks[4].tile[:, t * P:(t + 1) * P], Sx[:, n % 2, t, :], ident)
                    mm.then_inc(banks[4].filled, 1)
                    if g == 0:
                        banks[5].take(pe, ("Tp", n))
                        for t in range(NT - 1):
                            mm = pe.transpose(banks[5].tile[:, t * P:(t + 1) * P], Sx[:, n % 2, NT + t, :], ident)
                        mm.then_inc(banks[5].filled, 1)
                elif op == "values":
                    g, h = a
                    n, o, hp = g * SLOTS + h, HD * (h % 2), h // 2
                    if h == 0:
                        pe.wait_ge(S["v_rows_ready"], (NT + 1) * (g + 1))
                    pe.wait_ge(S["probs_turned"], n + 1)
                    if g == 0:
                        pe.wait_ge(S["prev_probs_turned"], n + 1)
                    bk = banks[6]
                    if h % 2 == 0:
                        bk.take(pe, ("O", g, hp))
                    for t in range(NT):
                        out = bk.tile[o:o + HD, t * P:(t + 1) * P]
                        mm = pe.matmul(out, vv[:, t, h * HD:(h + 1) * HD], PT[:, n % 2, t, :],
                                       start=(t == 0), stop=True, skip_group_check=True)
                        if g == 0 and t > 0:
                            mm = pe.matmul(out, vv[:, t - 1, h * HD:(h + 1) * HD], PT[:, n % 2, NT + t - 1, :],
                                           start=False, stop=True, skip_group_check=True)
                    mm.then_inc(bk.filled if h % 2 else S["even_head_summed"], 1)
                elif op == "turnq":
                    banks[5].take(pe, ("qT",))
                    for g in range(NG):
                        for hp in range(HP):
                            c = (g * HP + hp) * B
                            mm = pe.transpose(banks[5].tile[:, c:c + B], qS[:, 0, g, hp * P:(hp + 1) * P], con[0:B, C_ID:C_ID + B])
                    mm.then_inc(banks[5].filled, 1)
                elif op == "merge":
                    pe.wait_ge(S["maxima_sums_ready"], 1)
                    for g in range(NG):
                        for src, bk, key in ((mst, merge_banks[g], "mt"), (lst, merge_banks[NG + g], "lt")):
                            bk.take(pe, (key, g))
                            for t in range(NT):
                                mm = pe.transpose(bk.tile[0:SLOTS, t * P:(t + 1) * P], src[:, g, t, :], ident)
                            mm.then_inc(bk.filled, 1)
                elif op == "spread":
                    pe.wait_ge(S["merge_weights"], 1)
                    hp, g = divmod(a[0], NG)
                    bk = spread_bank(a[0])
                    bk.take(pe, ("wb", hp, g))
                    pe.matmul(bk.tile[:, :], selR[:, hp, :], mH_[:, g, :], start=True, stop=False)
                    pe.matmul(bk.tile[:, :], selR[:, hp, :], mL_[:, g, :], start=False, stop=True).then_inc(bk.filled, 1)
                elif op == "key":
                    n = a[0]
                    if n < B * NG:
                        pe.wait_ge(S[f"cache_loaded{n % RING}"], 16 * (n // RING + 1))
                        bk = banks[4 + n % 2]
                        bk.take(pe, ("K", n))
                        for hp in range(HP):
                            mm = pe.transpose(bk.tile[:, hp * P:(hp + 1) * P], ring[:, n % RING, hp * P:(hp + 1) * P], ident)
                        mm.then_inc(bk.filled, 1)
                    if n > 0:
                        n -= 1
                        b, g = divmod(n, NG)
                        if n == 0:
                            pe.wait_ge(S["sample_q_ready"], 1)
                            banks[6].take(pe, ("sS",))
                        pe.wait_ge(S["keys_turned"], n + 1)
                        for hp in range(HP):
                            c = g * SLOTS * B + 2 * hp * B + b
                            q0 = (g * HP + hp) * B + b
                            mm = pe.matmul(banks[6].tile[:, c:c + B + 1:B], KT[:, n % 2, hp, :], qd[:, q0, :],
                                           start=True, stop=True, skip_group_check=True)
                        mm.then_inc(banks[6].filled if n == B * NG - 1 else S["keys_scored"], 1)
                elif op == "samplemax":
                    pe.wait_ge(S["sample_scores_kept"], 1)
                    banks[4].take(pe, ("sT",))
                    for g in range(NG):
                        pe.transpose(banks[4].tile[0:SLOTS * B, g * NKEYS:(g + 1) * NKEYS],
                                     sS[:, g, :, :].rearrange("p h b -> p (h b)"), ident)
                    pe.wait_ge(S["self_scores_ready"], 1)
                    for h in range(SLOTS):
                        c = C_PLACE + (SLOTS - 1 - h) * B
                        mm = pe.matmul(banks[4].tile[0:SLOTS * B, NG * NKEYS:NG * NKEYS + NG], con[0:B, c:c + SLOTS * B],
                                       sself[:, :, h], start=(h == 0), stop=(h == SLOTS - 1))
                    mm.then_inc(banks[4].filled, 1)
                elif op == "sampleprobs":
                    pe.wait_ge(S["sample_probs"], 1)
                    banks[5].take(pe, ("pTs",))
                    n = SLOTS * B
                    for g in range(NG):
                        pe.transpose(banks[5].tile[:, g * n:(g + 1) * n], pS[:, g * NKEYS:(g + 1) * NKEYS],
                                     con[0:n, C_ID:C_ID + n])
                    for h in range(SLOTS):
                        c = NG * n + h * NG
                        mm = pe.matmul(banks[5].tile[0:B, c:c + NG], con[0:n, C_ID + h * B:C_ID + (h + 1) * B],
                                       pS[:, NG * NKEYS:NG * NKEYS + NG], start=True, stop=True, skip_group_check=True)
                    mm.then_inc(banks[5].filled, 1)
                elif op == "ownvalues":
                    pe.wait_ge(S["sample_probs_turned"], 1)
                    bk = banks[7]
                    bk.take(pe, ("so",))
                    for h in range(SLOTS):
                        o, hp = HD * (h % 2), h // 2
                        for g in range(NG):
                            pe.matmul(bk.tile[o:o + HD, hp * B:(hp + 1) * B], qS[:, 2, g, h * HD:(h + 1) * HD],
                                      SD[:, g, h, :], start=(h < 2 and g == 0), stop=True, skip_group_check=True)
                elif op == "value":
                    n = a[0]
                    b, g = divmod(n, NG)
                    m = B * NG + n
                    pe.wait_ge(S[f"cache_loaded{m % RING}"], 16 * (m // RING + 1))
                    for h in range(SLOTS):
                        o, hp = HD * (h % 2), h // 2
                        mm = pe.matmul(banks[7].tile[o:o + HD, hp * B + b:hp * B + b + 1], ring[:, m % RING, h * HD:(h + 1) * HD],
                                       pTs[:, g, h, b:b + 1], start=False, stop=True, skip_group_check=True)
                    mm.then_inc(S["cached_v_used"] if n < B * NG - 1 else banks[7].filled, 1)
                elif op == "dtrows":
                    pe.wait_ge(S["decays_ready"], 1)
                    banks[4].take(pe, ("dtr",))
                    for c in range(NT):
                        for q, src in enumerate((dtT[:, B + c * P:B + (c + 1) * P], acT[:, c * P:(c + 1) * P],
                                                 decT[:, c * P:(c + 1) * P])):
                            mm = pe.transpose(banks[4].tile[:, (c * 3 + q) * HEADS:(c * 3 + q + 1) * HEADS], src,
                                              con[0:HEADS, C_ID:C_ID + HEADS])
                    mm.then_inc(banks[4].filled, 1)
                    pe.wait_ge(S["selectors3_loaded"], 16)
                    banks[5].take(pe, ("dsb",))
                    for u in range(UNITS):
                        mm = pe.matmul(banks[5].tile[:, u * 2 * B:(u + 1) * 2 * B], sel3[:, u, :], dsS[:, :],
                                       start=True, stop=True)
                    mm.then_inc(banks[5].filled, 1)
                elif op == "bc":
                    g = a[0]
                    pe.wait_ge(S["conv_ready"], CV_BC[g])
                    banks[4].take(pe, ("Brm", g))
                    for c in range(NT):
                        mm = pe.transpose(banks[4].tile[:, c * P:(c + 1) * P], BT[:, c * P:(c + 1) * P], ident)
                    mm.then_inc(banks[4].filled, 1)
                    banks[7].take(pe, ("CB", g))
                    for c in range(NT):
                        mm = pe.matmul(banks[7].tile[:, c * P:(c + 1) * P], BT[:, c * P:(c + 1) * P],
                                       CT[:, c * P:(c + 1) * P], start=True, stop=True)
                    mm.then_inc(banks[7].filled, 1)
                    for q, src in enumerate((BT, CT)):
                        for half in range(2):
                            bk = banks[4 + 3 * half]
                            bk.take(pe, ("BCb", g, q, half))
                            for c in range(4):
                                b = 4 * half + c
                                mm = pe.matmul(bk.tile[:, c * P:(c + 1) * P],
                                               src[:, CS + TAPS * b:CS + TAPS * b + 1].to_broadcast([P, P]), ident,
                                               start=True, stop=True)
                            mm.then_inc(bk.filled, 1)
                elif op == "ssdA":
                    u = a[0]
                    if u == 0:
                        pe.wait_ge(S["ac_parts_ready"], 1)
                    for e in range(2):
                        bk = banks[5 + e]
                        bk.take(pe, ("ac", u, e))
                        head = idR[:, 2 * u + e:2 * u + e + 1].to_broadcast([HEADS, P])
                        pe.matmul(bk.tile[:, :], head, acH[:, :], start=True, stop=False)
                        pe.matmul(bk.tile[:, :], head, acL[:, :], start=False, stop=True).then_inc(bk.filled, 1)
                    pe.wait_ge(S["conv_ready"], CV_X[u])
                    banks[4].take(pe, ("xT", u))
                    for c in range(NT):
                        mm = pe.transpose(banks[4].tile[:, c * P:(c + 1) * P], xu[:, u % 3, c * P:(c + 1) * P], ident)
                    mm.then_inc(banks[4].filled, 1)
                elif op == "ssdS":
                    u = a[0]
                    pe.wait_ge(S["b_rows_ready"], u // PER_GROUP + 1)
                    pe.wait_ge(S["xdt_ready"], u + 1)
                    banks[4].take(pe, ("st", u))
                    for c in range(NT):
                        mm = pe.matmul(banks[4].tile[:, c * P:(c + 1) * P], Brm[:, c, :], xdec[:, c, :], start=True, stop=True)
                    mm.then_inc(banks[4].filled, 1)
                    banks[7].take(pe, ("y", u))
                    for e in range(2):
                        o = e * HD
                        pe.wait_ge(S["masked_cb_ready"], 2 * u + e + 1)
                        for c in range(NT):
                            pe.matmul(banks[7].tile[o:o + HD, c * P:(c + 1) * P], xdt[:, c, o:o + HD], Lb[:, e, c, :],
                                      start=(c == 0), stop=(c == 0), skip_group_check=True)
                elif op == "ssdY":
                    u = a[0]
                    pe.wait_ge(S["scaled_c_ready"], 2 * (u + 1))
                    pe.wait_ge(S["states_before_ready"], u + 1)
                    for e in range(2):
                        o = e * HD
                        for c in range(1, NT):
                            mm = pe.matmul(banks[7].tile[o:o + HD, c * P:(c + 1) * P], hst[:, u % 2, c - 1, o:o + HD],
                                           Eb[:, e, c * P:(c + 1) * P], start=False, stop=True, skip_group_check=True)
                    mm.then_inc(banks[7].filled, 1)
                elif op == "gnorm":
                    g = a[0]
                    for hf in range(2):
                        banks[5 + hf].take(pe, ("gn", g, hf))
                    for k in range(PER_GROUP):
                        pe.wait_ge(S["y_squared"], g * PER_GROUP + k + 1)
                        for hf in range(2):
                            mm = pe.matmul(banks[5 + hf].tile[:, 0:HALF], ones[:, :], sq2[:, k % 2, hf * HALF:(hf + 1) * HALF],
                                           start=(k == 0), stop=(k == PER_GROUP - 1))
                            if k == PER_GROUP - 1:
                                mm.then_inc(banks[5 + hf].filled, 1)
                            elif hf == 1:
                                mm.then_inc(S["square_summed"], 1)

        @block.sync
        def _(sp):
            nbar, outs = 0, 0
            for k in range(KD):
                sp.dma_start(xw[:, k, :], xT[:, k, :]).then_inc(S[f"rows_loaded{k}"], 16)
            pieces = []
            for b in range(B):
                for g in (2, 1, 0):
                    w = WINDOWS[g]
                    for r in range(0, w - 1, 512):
                        pieces.append((g, b, r, min(512, w - 1 - r)))

            def shift(g, b, r, n):
                src = caches[g][b, r + 1:r + 1 + n].rearrange("r c -> (r c)").rearrange("(a x) -> a x", a=P)
                dst = kvs_out[g][b, r:r + n].rearrange("r c -> (r c)").rearrange("(a x) -> a x", a=P)
                sp.dma_start(dst, src).then_inc(S["cache_shifted"], 16)

            def load(i):
                it = ITEMS[i]
                if i >= 2:
                    sp.wait_ge(S["weight_low_ready"], i - 1)
                k, n = SHAPES.get(it[0], (KD, 2 * P))
                sp.dma_start(raw[:, i % 2, 0:k * n], wpack[i, :, 0:k * n]).then_inc(S[f"weights_loaded{i % 2}"], 16)

            per = -(-len(pieces) // (len(ITEMS) - 8))
            npieces = len(pieces)
            for step in PLAN:
                op, a = step[0], step[1:]
                if op == "barrier":
                    nbar += 1
                    sp.drain().then_inc(S["phase_ended"], 1)
                    sp.wait_ge(S["phase_ended"], 5 * nbar)
                elif op == "init":
                    sp.dma_start(par[:, :], params).then_inc(S["tables_loaded"], 16)
                    sp.dma_start(con[:, :], consts).then_inc(S["tables_loaded"], 16)
                elif op == "split":
                    load(a[0])
                    for _ in range(0 if a[0] == 0 or ITEMS[a[0]][0] in ("za", "dt") else per):
                        if pieces:
                            shift(*pieces.pop(0))
                elif op == "merge":
                    sp.dma_start(sel[:, :, :], sel_in[0:SLOTS, 0:HP, :]).then_inc(S["selectors_loaded"], 16)
                elif op == "key" and a[0] < B * NG or op == "value":
                    b, g = divmod(a[0], NG)
                    m = a[0] + (B * NG if op == "value" else 0)
                    c = T if op == "value" else 0
                    if RING <= m < B * NG + RING:
                        sp.wait_ge(S["keys_turned"], m - RING + 1)
                    elif m >= B * NG + RING:
                        sp.wait_ge(S["cached_v_used"], m - B * NG - RING + 1)
                    sp.dma_start(ring[:, m % RING, :], caches[g][b, 0:WINDOWS[g]:DILATIONS[g], c:c + T])\
                      .then_inc(S[f"cache_loaded{m % RING}"], 16)
                elif op == "dt":
                    sp.dma_start(sel3[:, :, :], sel_in).then_inc(S["selectors3_loaded"], 16)
                    sp.dma_start(stc[:, :, :, :], state_conv).then_inc(S["conv_state_loaded"], 16)
                elif op == "ssdA":
                    u = a[0]
                    if u >= 2:
                        sp.wait_ge(S[f"sample_state_stored{u % 2}"], 16 * (u // 2))
                        sp.wait_ge(S["sample_state_c_ready"], u - 1)
                    sp.dma_start(stt_[:, u % 2, :, :], ssm_in[u]).then_inc(S[f"sample_state_loaded{u % 2}"], 16)
                elif op == "ssdZ":
                    u = a[0]
                    sp.wait_ge(S["last_state_ready"], u + 1)
                    sp.dma_start(ssmp_out[u], hst[:, u % 2, NT - 1, :]).then_inc(S[f"state_stored{u % 2}"], 16)
                    sp.wait_ge(S["sample_state_ready"], u + 1)
                    sp.dma_start(ssms_out[u], stt_[:, u % 2, :, :]).then_inc(S[f"sample_state_stored{u % 2}"], 16)
                elif op == "mix" and a[0] == 3:
                    sp.wait_ge(*ends[ITEM_AT["bs", 7]])
                    sp.dma_start(xres[:, :, :], xT).then_inc(S["residual_loaded"], 16)
            for j in range(KD):
                sp.wait_ge(S["out_ready"], j + 1)
                sp.dma_start(y_out[:, j, :], outb[:, j % 2, :]).then_inc(S[f"y_stored{j % 2}"], 16)
            sp.wait_ge(S["cache_shifted"], 16 * npieces)
            for q in range(2):
                sp.wait_ge(S[f"y_stored{q}"], 16 * (KD // 2))
                sp.wait_ge(S[f"sample_state_stored{q}"], 16 * (UNITS // 2))
            sp.wait_ge(S["k_stored"], 16 * (1 + 4 + 4 + NG))
            sp.wait_ge(S["v_stored"], 16 * (1 + 4 + 4 + NG))
            sp.wait_ge(S["state_stored0"], 16 * (UNITS // 2))
            sp.wait_ge(S["state_stored1"], 16 * (UNITS // 2))
            sp.wait_ge(S["conv_tail_stored"], 16)

        @block.gpsimd
        def _(pool):
            nbar = 0
            outs = 0
            for step in PLAN:
                op, a = step[0], step[1:]
                if op == "barrier":
                    nbar += 1
                    if nbar == 1:
                        pool.wait_ge(S["k_stored"], 16 * (1 + 4 + 4 + NG))
                        pool.wait_ge(S["v_stored"], 16 * (1 + 4 + 4 + NG))
                    if nbar == 3:
                        pool.wait_ge(S["state_stored0"], 16 * (UNITS // 2))
                        pool.wait_ge(S["state_stored1"], 16 * (UNITS // 2))
                        pool.wait_ge(S["sample_state_stored0"], 16 * (UNITS // 2))
                        pool.wait_ge(S["sample_state_stored1"], 16 * (UNITS // 2))
                        pool.wait_ge(S["conv_tail_stored"], 16)
                    pool.drain().then_inc(S["phase_ended"], 1)
                    pool.wait_ge(S["phase_ended"], 5 * nbar)
                elif op == "use" and a[1][:1] == (0,) and ITEMS[a[0] + 1:][:1] and ITEMS[a[0] + 1][0] in POOL_SPLITS:
                    i = a[0] + 1
                    pool.wait_ge(S["weight_high_ready"], i + 1)
                    pool.wait_ge(S["weight_low_ready"], i)
                    nc.gpsimd.tensor_tensor(wL[:, i % 2, :], raw[:, i % 2, :], wH[:, i % 2, :].bitcast(F32), ALU.subtract)\
                        .then_inc(S["weight_low_ready"], 1)
                elif op == "use" and ITEMS[a[0]][0] == "rm" and ITEMS[a[0]][3] == 1:
                    g, s = ITEMS[a[0]][1:3]
                    if s == "v":
                        for t in range(NT + 1):
                            pool.wait_ge(S["v_rows_ready"], (NT + 1) * g + t + 1)
                            if t == NT:
                                pool.dma_start(kvs_out[g][:, WINDOWS[g] - 1, T:2 * T], qS[:, 2, g, :]).then_inc(S["v_stored"], 16)
                            elif g > 0:
                                pool.dma_start(kvp_out[g][t:T:NT, T:2 * T], vv[:, t, :]).then_inc(S["v_stored"], 16)
                            elif t == NT - 1:
                                pool.dma_start(kvp_out[g][:, T:2 * T], vv[:, t, :]).then_inc(S["v_stored"], 16)
                        continue
                    si = "qk".index(s)
                    for t in range(NT + 1):
                        n = qk_count(g, si, t)
                        rows = B if t == NT else P
                        tab = 2 * NT if t == NT else (t if g == 0 else NT + t)
                        pool.wait_ge(S["qk_normed"], n + 1)
                        if n > 0:
                            pool.wait_ge(S["qk_rows_ready"], n)
                        v = qn[0:rows, :].rearrange("p (h x d) -> p h x d", h=SLOTS, x=2)
                        o = t2[0:rows, :].rearrange("p (h x d) -> p h x d", h=SLOTS, x=2)
                        for x in range(2):
                            rb = ropeB[0:rows, si, tab, 32 * x:32 * x + 32].unsqueeze(1).to_broadcast([rows, SLOTS, 32])
                            ins = nc.gpsimd.tensor_tensor(o[:, :, x, :], v[:, :, 1 - x, :], rb, ALU.mult)
                        ins.then_inc(S["rope_sine_ready"], 1)
                        if si == 1:
                            pool.wait_ge(S["qk_rows_ready"], n + 1)
                            if t == NT:
                                pool.dma_start(kvs_out[g][:, WINDOWS[g] - 1, 0:T], qS[:, 1, g, :]).then_inc(S["k_stored"], 16)
                            elif g > 0:
                                pool.dma_start(kvp_out[g][t:T:NT, 0:T], st[:, 1, t, :]).then_inc(S["k_stored"], 16)
                            elif t == NT - 1:
                                pool.dma_start(kvp_out[g][:, 0:T], st[:, 1, t, :]).then_inc(S["k_stored"], 16)
                elif op == "ssdA":
                    u = a[0]
                    pool.wait_ge(S[f"sample_state_loaded{u % 2}"], 16 * (u // 2 + 1))
                    if u == 0:
                        pool.wait_ge(S["sample_dt_ready"], 1)
                    nc.gpsimd.tensor_tensor(stt_[:, u % 2, :, :], stt_[:, u % 2, :, :], dsb[:, u, 0:B].unsqueeze(2).to_broadcast([P, B, P]),
                                            ALU.mult).then_inc(S["sample_decayed"], 1)
                    for e in range(2):
                        n = 2 * u + e
                        pool.wait_ge(S["chunk_exps_ready"], n + 1)
                        if u > 0 and e == 0:
                            pool.wait_ge(S["last_state_ready"], u)
                        nc.gpsimd.tensor_copy(dcol[:, e, :], Eb[:, e, P - 1:T:P]).then_inc(S["chunk_decay_kept"], 1)
                        pool.wait_ge(S["chunk_decay_kept"], n + 1)
                        nc.gpsimd.tensor_tensor(Eb[:, e, :], Eb[:, e, :], CT[:, 0:T], ALU.mult).then_inc(S["scaled_c_ready"], 1)
                elif op == "ssdS":
                    u = a[0]
                    g = u // PER_GROUP
                    pool.wait_ge(S["sample_xdt_ready"], u + 1)
                    pool.wait_ge(S["bc_spread_ready"], 4 * (g + 1))
                    if u >= 1:
                        pool.wait_ge(S["y_gated"], u)
                    nc.gpsimd.tensor_tensor(tt[:, :, :], BCb[:, 0, :, :], xds[:, :].unsqueeze(2).to_broadcast([P, B, P]),
                                            ALU.mult).then_inc(S["sample_xb_ready"], 1)
                elif op == "ssdY":
                    u = a[0]
                    pool.wait_ge(S["sample_state_ready"], u + 1)
                    nc.gpsimd.tensor_tensor(tt[:, :, :], BCb[:, 1, :, :], stt_[:, u % 2, :, :], ALU.mult).then_inc(S["sample_state_c_ready"], 1)
                elif op == "gnorm" and a[0] == GROUPS - 1:
                    pool.wait_ge(S["conv_tail_kept"], XU)
                    pool.dma_start(tail_out, tail[:, :, :]).then_inc(S["conv_tail_stored"], 16)

        @block.scalar
        def _(act):
            nbar = 0
            ch = Chain(act, S["act_order"])
            A = nc.scalar.activation

            def cp(out, in_):
                return nc.scalar.copy(out, in_)

            def free(bk):
                act.sem_inc(bk.freed, 1)

            def both(i, s):
                for hf in range(2):
                    cm_bank(i, s, hf).full(act, ("cm", i, s, hf))

            def table(n):
                act.add_instruction(mybir.InstLoadActFuncSet(name=nc.get_next_instruction_name(), act_func_set_id=n, ins=[], outs=[]))

            table(EXP_LN)
            for step in PLAN:
                op, a = step[0], step[1:]
                if op == "barrier":
                    nbar += 1
                    act.drain().then_inc(S["phase_ended"], 1)
                    act.wait_ge(S["phase_ended"], 5 * nbar)
                elif op == "squares":
                    for k in range(KD):
                        act.wait_ge(S[f"rows_loaded{k}"], 16)
                        A(xsq[:, k, :], xw[:, k, :], ACT.Square).then_inc(S["rows_squared"], 1)
                elif op == "init":
                    act.wait_ge(S["constants_set"], 2)
                    for hf in range(2):
                        banks[hf].full(act, ("ms", hf))
                        ch.link(A(rs[:, hf * HALF:(hf + 1) * HALF], banks[hf].tile[:, 0:HALF], ACT.Ln, bias=epsc[:, 0:1], scale=1.0 / D))
                        free(banks[hf])
                    A(rs[:, :], rs[:, :], ACT.Exp, scale=-0.5).then_inc(S["row_scale_ready"], 1)
                    for k in range(KD):
                        act.wait_ge(S["scaled_rows_ready"], k + 1)
                        cp(xH[:, k, :], xw[:, k, :]).then_inc(S["x_high_ready"], 1)
                elif op == "split":
                    i = a[0]
                    k, n = SHAPES.get(ITEMS[i][0], (KD, 2 * P))
                    act.wait_ge(S[f"weights_loaded{i % 2}"], 16 * (i // 2 + 1))
                    if i >= 2:
                        act.wait_ge(*ends[i - 2])
                    cp(wH[:, i % 2, 0:k * n], raw[:, i % 2, 0:k * n]).then_inc(S["weight_high_ready"], 1)
                elif op == "use":
                    i = a[0]
                    it = ITEMS[i]
                    if it[0] == "rm" and it[3] == 1:
                        g, s = it[1:3]
                        if s == "v":
                            if g > 0:
                                act.wait_ge(S["v_stored"], 16 * {1: 2, 2: 7}[g])
                                pv_done(act, g * SLOTS - 1)
                            for t in range(NT + 1):
                                banks[t].full(act, ("rm", g, s, t))
                                dst = qS[:, 2, g, :] if t == NT else vv[:, t, :]
                                cp(dst, banks[t].tile[0:B if t == NT else P, :]).then_inc(S["v_rows_ready"], 1)
                                act.wait_ge(S["v_rows_ready"], (NT + 1) * g + t + 1)
                                free(banks[t])
                            continue
                        si = "qk".index(s)

                        def square(t):
                            n = qk_count(g, si, t)
                            rows = B if t == NT else P
                            bk = row_bank(g, s, t)
                            bk.full(act, ("rm", g, s, t))
                            if n >= 2:
                                act.wait_ge(S["head_sums_ready"], n - 1)
                            A(sq[0:rows, n % 2, :], bk.tile[0:rows, :], ACT.Square, scale=HD ** -0.5).then_inc(S["qk_squared"], 1)

                        def root(t):
                            n = qk_count(g, si, t)
                            rows = B if t == NT else P
                            act.wait_ge(S["head_sums_ready"], n + 1)
                            ch.link(A(ss[0:rows, n % 2, :], ss[0:rows, n % 2, :], ACT.Ln, bias=epsc[0:rows, 0:1]))
                            if n >= 2:
                                act.wait_ge(S["qk_normed"], n - 1)
                            A(rst[0:rows, n % 2, :], ss[0:rows, n % 2, :], ACT.Exp, scale=-0.5).then_inc(S["head_scales_ready"], 1)

                        square(0)
                        for t in range(NT + 1):
                            if t < NT:
                                square(t + 1)
                            root(t)
                    elif it[0] == "za":
                        for s in a[1]:
                            both(i, s)
                            hp = 2 * it[1] + s
                            if hp > 0:
                                act.wait_ge(S["za_applied"], hp)
                            for hf in range(2):
                                ins = A(gta[:, hf * HALF:(hf + 1) * HALF], cm_bank(i, s, hf).tile[:, 0:HALF], ACT.Tanh, scale=0.5)
                            ins.then_inc(S["za_tanh_ready"], 1)
                    elif it[0] in ("bc", "x"):
                        for s in a[1]:
                            n, cu = CV[i, s]
                            both(i, s)
                            b0, b1 = (cm_bank(i, s, hf) for hf in range(2))
                            if n == 0:
                                act.wait_ge(S["conv_state_loaded"], 16)
                                act.wait_ge(S["conv_weights_ready"], 1)
                            else:
                                act.wait_ge(S["conv_ready"], n)
                            bb = buf[:, n % 2, :]
                            cp(bb[:, S0:BUF].rearrange("p (b w) -> p b w", w=TAPS)[:, :, 0:TAPS - 1], stc[:, cu, :, :])
                            cp(buf[:, n % 2, TAPS - 1:TAPS - 1 + HALF - B], b0.tile[:, B:HALF])
                            cp(buf[:, n % 2, TAPS - 1 + HALF - B:S0], b1.tile[:, 0:HALF])
                            ch.link(cp(buf[:, n % 2, S0 + TAPS - 1:BUF:TAPS], b0.tile[:, 0:B]))
                            free(b0)
                            free(b1)
                            cp(tail[:, cu, 0:TAPS - 1], bb[:, T:T + TAPS - 1])
                            cp(tail[:, cu, TAPS - 1:TAIL].rearrange("p (b w) -> p b w", w=TAPS - 1),
                               bb[:, S0:BUF].rearrange("p (b w) -> p b w", w=TAPS)[:, :, 1:TAPS]).then_inc(S["conv_tail_kept"], 1)
                            A(cacc[:, :], bb[:, 0:CONV], ACT.Identity, bias=wcv[:, cu, TAPS:TAPS + 1], scale=wcv[:, cu, 0:1])\
                                .then_inc(S["conv_rows_placed"], 1)
                            act.wait_ge(S["conv_summed"], n + 1)
                            A(cth[:, :], cacc[:, :], ACT.Tanh).then_inc(S["conv_tanh"], 1)
                    elif it[0] == "z":
                        for s in a[1]:
                            u = 2 * it[1] + s
                            both(i, s)
                            if u > 0:
                                act.wait_ge(S["z_silu_ready"], u)
                            for hf in range(2):
                                ins = A(ztn[:, hf * HALF:(hf + 1) * HALF], cm_bank(i, s, hf).tile[:, 0:HALF], ACT.Tanh, scale=0.5)
                            ins.then_inc(S["z_tanh_ready"], 1)
                    elif it[0] in ("gs", "ga"):
                        base_g = 0 if it[0] == "gs" else KD
                        for s in a[1]:
                            both(i, s)
                            n = base_g + 2 * it[1] + s
                            if n >= 4:
                                act.wait_ge(S["gate_used"], n - 3)
                            for hf in range(2):
                                bk = cm_bank(i, s, hf)
                                ch.link(A(gate[:, n % 4, hf * HALF:(hf + 1) * HALF], bk.tile[:, 0:HALF], ACT.Tanh, scale=0.5))
                                free(bk)
                            act.sem_inc(S["gate_ready"], 1)
                elif op == "turn":
                    g, si = a
                    dst = (qT, kT)[si]
                    if g > 0:
                        n = g * SLOTS - 1
                        banks[n % 2].full(act, ("S", n))
                        if g == 1:
                            banks[2 + n % 2].full(act, ("Sp", n))
                    for t in range(NT):
                        bk = next(b for b in banks[5:8] if ("turn", g, si, t) in b.uses)
                        bk.full(act, ("turn", g, si, t))
                        cp(dst[:, :, t * P:(t + 1) * P], bk.tile[:, :].rearrange("p (h c) -> p h c", h=HP)).then_inc(S["qk_columns_ready"], 1)
                        act.wait_ge(S["qk_columns_ready"], (2 * g + si) * NT + t + 1)
                        free(bk)
                elif op == "scores":
                    g, h = a
                    n = g * SLOTS + h
                    act.wait_ge(S["neg_max_ready"], n + 1)
                    for t in range(NT):
                        ins = A(Sx[:, n % 2, t, :], Sx[:, n % 2, t, :], ACT.Exp, bias=nm[:, n % 2, t:t + 1],
                                accum_out=lst[:, g, t, h:h + 1])
                    if g == 0:
                        for t in range(1, NT):
                            ins = A(Sx[:, n % 2, NT + t - 1, :], Sx[:, n % 2, NT + t - 1, :], ACT.Exp, bias=nm[:, n % 2, t:t + 1],
                                    accum_out=l2[:, n % 2, t - 1:t])
                    ins.then_inc(S["probs_ready"], 1)
                elif op == "probs":
                    g, h = a
                    n = g * SLOTS + h
                    banks[4].full(act, ("T", n))
                    if n >= 2:
                        pv_done(act, n - 2)
                    cp(PT[:, n % 2, 0:NT, :], banks[4].tile[:, :].rearrange("p (t c) -> p t c", t=NT)).then_inc(S["probs_turned"], 1)
                    act.wait_ge(S["probs_turned"], n + 1)
                    free(banks[4])
                elif op == "values" and a[1] % 2:
                    g, h = a
                    hp = h // 2
                    bk = banks[6]
                    bk.full(act, ("O", g, hp))
                    dst = oU[:, g, hp, :]
                    if g > 0:
                        dst = dst.rearrange("p (j t) -> p t j", t=NT)
                    else:
                        dst = dst.rearrange("p (t j) -> p t j", t=NT)
                    cp(dst, bk.tile[:, :].rearrange("p (t j) -> p t j", t=NT)).then_inc(S["head_pair_out"], 1)
                    act.wait_ge(S["head_pair_out"], g * HP + hp + 1)
                    free(bk)
                elif op == "key" and a[0] < B * NG:
                    n = a[0]
                    bk = banks[4 + n % 2]
                    bk.full(act, ("K", n))
                    if n >= 2:
                        act.wait_ge(S["keys_scored"], n - 1)
                    cp(KT[:, n % 2, :, :], bk.tile[:, :].rearrange("p (h k) -> p h k", h=HP)).then_inc(S["keys_turned"], 1)
                    act.wait_ge(S["keys_turned"], n + 1)
                    free(bk)
                elif op == "exps":
                    for g in range(NG):
                        act.wait_ge(S["merge_exponents"], g + 1)
                        A(mT[:, g, :], mT[:, g, :], ACT.Exp).then_inc(S["merge_exps"], 1)
                elif op == "samplemax":
                    act.wait_ge(S["sample_exponents"], 1)
                    A(pS[:, :], banks[4].tile[0:SLOTS * B, 0:NG * NKEYS + NG], ACT.Exp, bias=nMs[:, 0:1], scale=SCALE,
                      accum_out=ls[:, 0:1]).then_inc(S["sample_exps"], 1)
                    act.wait_ge(S["sample_exps"], 1)
                    free(banks[4])
                elif op == "dt":
                    table(EXP_LN)
                    act.wait_ge(S["tables_loaded"], 32)
                    A(Acol[:, :], par[0:HEADS, PW_ALOG:PW_ALOG + 1], ACT.Exp).then_inc(S["dt_activations"], 1)
                    act.wait_ge(S["dt_operands"], 1)
                    A(da[2][:, :], da[1][:, :], ACT.Exp).then_inc(S["dt_activations"], 1)
                    act.wait_ge(S["dt_operands"], 2)
                    A(da[4][:, :], da[3][:, :], ACT.Ln).then_inc(S["dt_activations"], 1)
                    act.wait_ge(S["dt_operands"], 3)
                    A(dsS[:, 0:B], da[7][:, 0:B], ACT.Exp)
                    A(decT[:, :], decT[:, :], ACT.Exp).then_inc(S["decays_ready"], 1)
                elif op == "bc":
                    g = a[0]
                    banks[4].full(act, ("Brm", g))
                    if g > 0:
                        banks[4].full(act, ("st", 4 * g - 1))
                        act.wait_ge(S["sample_state_c_ready"], 4 * g)
                    cp(Brm[:, :, :], banks[4].tile[:, :].rearrange("p (c n) -> p c n", c=NT)).then_inc(S["b_rows_ready"], 1)
                    act.wait_ge(S["b_rows_ready"], g + 1)
                    free(banks[4])
                    for q in range(2):
                        for half in range(2):
                            bk = banks[4 + 3 * half]
                            bk.full(act, ("BCb", g, q, half))
                            cp(BCb[:, q, 4 * half:4 * half + 4, :], bk.tile[:, :].rearrange("p (c n) -> p c n", c=4)).then_inc(S["bc_spread_ready"], 1)
                            act.wait_ge(S["bc_spread_ready"], 4 * g + 2 * q + half + 1)
                            free(bk)
                elif op == "ssdA":
                    u = a[0]
                    if u > 0:
                        banks[7].full(act, ("y", u - 1))
                    for e in range(2):
                        n = 2 * u + e
                        banks[5 + e].full(act, ("ac", u, e))
                        A(Eb[:, e, :], banks[5 + e].tile[:, :], ACT.Exp).then_inc(S["chunk_exps_ready"], 1)
                        act.wait_ge(S["decay_args_ready"], n + 1)
                        for c in range(NT):
                            ins = A(Lb[:, e, c, :], Lb[:, e, c, :], ACT.Exp, bias=nac[:, c, 2 * u + e:2 * u + e + 1])
                        ins.then_inc(S["decay_matrix_ready"], 1)
                elif op == "gnorm":
                    g = a[0]
                    act.wait_ge(S["decay_matrix_ready"], 2 * PER_GROUP * (g + 1))
                    banks[7].full(act, ("y", PER_GROUP * (g + 1) - 1))
                    for k in range(PER_GROUP):
                        n = g * PER_GROUP + k
                        act.wait_ge(S["y_gated"], n + 1)
                        if k >= 2:
                            act.wait_ge(S["square_summed"], 3 * g + k - 1)
                        elif g > 0:
                            banks[6].full(act, ("gn", g - 1, 1))
                        A(sq2[:, k % 2, :], ygn[:, n, :], ACT.Square).then_inc(S["y_squared"], 1)
                    if g > 0:
                        act.wait_ge(S["y_normed"], g)
                    for hf in range(2):
                        banks[5 + hf].full(act, ("gn", g, hf))
                        ch.link(A(grs[:, hf * HALF:(hf + 1) * HALF], banks[5 + hf].tile[:, 0:HALF], ACT.Sqrt, bias=epsc[:, 0:1],
                                  scale=float(GROUPS) / DSSD))
                        free(banks[5 + hf])
                    act.sem_inc(S["scaled_rows_ready"], 1)
                elif op == "parts":
                    for u in range(UNITS):
                        cp(yH[:, u, :], ygn[:, u, :]).then_inc(S["y_high_ready"], 1)
                    for hp in range(HP):
                        cp(oH[:, hp, :], oT[:, hp, :]).then_inc(S["o_high_ready"], 1)
                elif op == "mix":
                    for s in range(2):
                        k = 2 * a[0] + s
                        act.wait_ge(S["mix_ready"], k + 1)
                        cp(mH[:, k, :], mix[:, k, :]).then_inc(S["mix_high_ready"], 1)

        @block.vector
        def _(dve):
            nbar = 0
            ch = Chain(dve, S["dve_order"])
            V = nc.vector
            TT, TS, STT = V.tensor_tensor, V.tensor_scalar, V.scalar_tensor_tensor

            def free(bk):
                dve.sem_inc(bk.freed, 1)

            V.memset(ones[:, :], 1.0).then_inc(S["constants_set"], 1)
            V.memset(epsc[:, :], EPS).then_inc(S["constants_set"], 1)
            for step in PLAN:
                op, a = step[0], step[1:]
                if op == "barrier":
                    nbar += 1
                    dve.drain().then_inc(S["phase_ended"], 1)
                    dve.wait_ge(S["phase_ended"], 5 * nbar)
                    if nbar == 2:
                        ch.link(V.memset(onesm[:, :], 1.0))
                        V.memset(buf[:, 0, 0:TAPS - 1], 0.0)
                        V.memset(buf[:, 1, 0:TAPS - 1], 0.0)
                        ch.link(TS(wcv[:, :, 0:TAPS], par[:, PW_CONV:PW_CONVB].rearrange("p (u w) -> p u w", w=TAPS), 0.5, None, ALU.mult))
                        ch.link(TS(wcv[:, :, TAPS:TAPS + 1], par[:, PW_CONVB:PW_SNORM].unsqueeze(2), 0.5, None, ALU.mult))
                        dve.sem_inc(S["conv_weights_ready"], 1)
                elif op == "squares":
                    for k in range(1, KD):
                        dve.wait_ge(S["rows_squared"], k + 1)
                        ins = TT(xsq[:, 0, :], xsq[:, 0, :], xsq[:, k, :], ALU.add)
                        if k < KD - 1:
                            ch.link(ins)
                    ins.then_inc(S["squares_added"], 1)
                elif op == "init":
                    dve.wait_ge(S["tables_loaded"], 32)
                    dve.wait_ge(S["row_scale_ready"], 1)
                    for k in range(KD + 2):
                        if k < KD:
                            STT(out=xw[:, k, :], in0=xw[:, k, :], scalar=par[:, PW_NORM + k:PW_NORM + k + 1], in1=rs[:, :],
                                op0=ALU.mult, op1=ALU.mult).then_inc(S["scaled_rows_ready"], 1)
                        if k >= 2:
                            dve.wait_ge(S["x_high_ready"], k - 1)
                            TT(xL[:, k - 2, :], xw[:, k - 2, :], xH[:, k - 2, :].bitcast(F32), ALU.subtract).then_inc(S["x_low_ready"], 1)
                elif op == "rope":
                    cos = con[:, C_COS:C_SIN].rearrange("p (t d) -> p t d", d=32)
                    sin = con[:, C_SIN:NCONST].rearrange("p (t d) -> p t d", d=32)
                    for si, w0 in enumerate((PW_QW, PW_KW)):
                        for x in range(2):
                            own = par[:, w0 + 32 * x:w0 + 32 * x + 32].unsqueeze(1).to_broadcast([P, RT, 32])
                            other = par[:, w0 + 32 * (1 - x):w0 + 32 * (1 - x) + 32].unsqueeze(1).to_broadcast([P, RT, 32])
                            ch.link(TT(ropeA[:, si, :, 32 * x:32 * x + 32], cos, own, ALU.mult))
                            ch.link(STT(out=ropeB[:, si, :, 32 * x:32 * x + 32], in0=sin, scalar=-1.0 if x == 0 else 1.0,
                                        in1=other, op0=ALU.mult, op1=ALU.mult))
                elif op == "split":
                    i = a[0]
                    k, n = SHAPES.get(ITEMS[i][0], (KD, 2 * P))
                    if ITEMS[i][0] in POOL_SPLITS:
                        continue
                    dve.wait_ge(S["weight_high_ready"], i + 1)
                    if i and ITEMS[i - 1][0] in POOL_SPLITS:
                        dve.wait_ge(S["weight_low_ready"], i)
                    TT(wL[:, i % 2, 0:k * n], raw[:, i % 2, 0:k * n], wH[:, i % 2, 0:k * n].bitcast(F32), ALU.subtract)\
                        .then_inc(S["weight_low_ready"], 1)
                elif op == "use":
                    i = a[0]
                    it = ITEMS[i]
                    if it[0] == "rm" and it[3] == 1 and it[2] != "v":
                        g, s = it[1:3]
                        si = "qk".index(s)

                        def reduce(t):
                            n = qk_count(g, si, t)
                            rows = B if t == NT else P
                            dve.wait_ge(S["qk_squared"], n + 1)
                            if n >= 2:
                                dve.wait_ge(S["head_scales_ready"], n - 1)
                            V.tensor_reduce(ss[0:rows, n % 2, :], sq[0:rows, n % 2, :].rearrange("p (h d) -> p h d", h=SLOTS),
                                            AX.X, ALU.add).then_inc(S["head_sums_ready"], 1)

                        def norm(t):
                            n = qk_count(g, si, t)
                            rows = B if t == NT else P
                            tab = 2 * NT if t == NT else (t if g == 0 else NT + t)

                            def heads(x):
                                return x.rearrange("p (h d) -> p h d", h=SLOTS)

                            dve.wait_ge(S["head_scales_ready"], n + 1)
                            row_tile = row_bank(g, s, t)
                            TT(heads(qn[0:rows, :]), heads(row_tile.tile[0:rows, :]),
                               rst[0:rows, n % 2, :].unsqueeze(2).to_broadcast([rows, SLOTS, HD]), ALU.mult).then_inc(S["qk_normed"], 1)
                            dve.wait_ge(S["qk_normed"], n + 1)
                            free(row_tile)
                            ch.link(TT(heads(t1[0:rows, :]), heads(qn[0:rows, :]),
                                       ropeA[0:rows, si, tab, :].unsqueeze(1).to_broadcast([rows, SLOTS, HD]), ALU.mult))
                            dst = qS[:, si, g, :] if t == NT else st[:, si, t, :]
                            if g > 0 and t < NT:
                                bk = next(b for b in banks[5:8] if ("turn", g - 1, si, t) in b.uses)
                                bk.full(dve, ("turn", g - 1, si, t))
                                if si == 1:
                                    dve.wait_ge(S["k_stored"], 16 * {1: 2, 2: 7}[g])
                            dve.wait_ge(S["rope_sine_ready"], n + 1)
                            TT(dst, t1[0:rows, :], t2[0:rows, :], ALU.add).then_inc(S["qk_rows_ready"], 1)

                        reduce(0)
                        for t in range(1, NT + 1):
                            reduce(t)
                            norm(t - 1)
                        norm(NT)
                    elif it[0] == "za":
                        for s in a[1]:
                            hp = 2 * it[1] + s
                            dve.wait_ge(S["za_tanh_ready"], hp + 1)
                            for hf in range(2):
                                bk = cm_bank(i, s, hf)
                                sl = slice(hf * HALF, (hf + 1) * HALF)
                                ch.link(STT(out=zg[:, hp, sl], in0=gta[:, sl], scalar=1.0, in1=bk.tile[:, 0:HALF], op0=ALU.add, op1=ALU.mult))
                                free(bk)
                            dve.sem_inc(S["za_applied"], 1)
                    elif it[0] in ("bc", "x"):
                        for s in a[1]:
                            n, cu = CV[i, s]
                            bb = buf[:, n % 2, :]
                            dve.wait_ge(S["conv_rows_placed"], n + 1)
                            for w in range(1, TAPS):
                                ins = STT(out=cacc[:, :], in0=bb[:, w:w + CONV], scalar=wcv[:, cu, w:w + 1], in1=cacc[:, :],
                                          op0=ALU.mult, op1=ALU.add)
                                if w < TAPS - 1:
                                    ch.link(ins)
                            ins.then_inc(S["conv_summed"], 1)
                            dve.wait_ge(S["conv_tanh"], n + 1)
                            if it[0] == "x":
                                u = 2 * it[1] + s
                                dst = xu[:, u % 3, :]
                                if u >= 3:
                                    banks[4].full(dve, ("xT", u - 3))
                            else:
                                dst = (BT, CT)[s]
                                if it[1] > 0:
                                    g = it[1] - 1
                                    banks[7].full(dve, ("CB", g))
                                    banks[7].full(dve, ("BCb", g, 1, 1))
                                    if s == 1:
                                        dve.wait_ge(S["scaled_c_ready"], 2 * PER_GROUP * (g + 1))
                                dst = dst[:, :]
                            STT(out=dst, in0=cth[:, :], scalar=1.0, in1=cacc[:, :], op0=ALU.add, op1=ALU.mult).then_inc(S["conv_ready"], 1)
                            dve.wait_ge(S["conv_ready"], n + 1)
                    elif it[0] == "z":
                        for s in a[1]:
                            u = 2 * it[1] + s
                            dve.wait_ge(S["z_tanh_ready"], u + 1)
                            for hf in range(2):
                                bk = cm_bank(i, s, hf)
                                sl = slice(hf * HALF, (hf + 1) * HALF)
                                ch.link(STT(out=zs[:, u % 2, sl], in0=ztn[:, sl], scalar=1.0, in1=bk.tile[:, 0:HALF],
                                            op0=ALU.add, op1=ALU.mult))
                                free(bk)
                            dve.sem_inc(S["z_silu_ready"], 1)
                    elif it[0] in ("bs", "ba"):
                        for s in a[1]:
                            j = it[1] if it[0] == "bs" else 4 * it[1] + s
                            n = j + (KD if it[0] == "ba" else 0)
                            dve.wait_ge(S["gate_ready"], n + 1)
                            for hf in range(2):
                                bk = cm_bank(i, s, hf)
                                bk.full(dve, ("cm", i, s, hf))
                                sl = slice(hf * HALF, (hf + 1) * HALF)
                                dst = mix[:, j, sl] if it[0] == "bs" else tmpg[:, sl]
                                ch.link(STT(out=dst, in0=gate[:, n % 4, sl], scalar=1.0, in1=bk.tile[:, 0:HALF],
                                            op0=ALU.add, op1=ALU.mult))
                                free(bk)
                            dve.sem_inc(S["gate_used"], 1)
                            if it[0] == "ba":
                                TT(mix[:, j, :], mix[:, j, :], tmpg[:, :], ALU.add).then_inc(S["mix_ready"], 1)
                                dve.wait_ge(S["mix_ready"], j + 1)
                    elif it[0] == "wo":
                        for s in a[1]:
                            j = 2 * it[1] + s
                            if j == 0:
                                dve.wait_ge(S["residual_loaded"], 16)
                            if j >= 2:
                                dve.wait_ge(S[f"y_stored{j % 2}"], 16 * (j // 2))
                            for hf in range(2):
                                bk = cm_bank(i, s, hf)
                                bk.full(dve, ("cm", i, s, hf))
                                sl = slice(hf * HALF, (hf + 1) * HALF)
                                ch.link(STT(out=outb[:, j % 2, sl], in0=bk.tile[:, 0:HALF], scalar=0.5, in1=xres[:, j, sl],
                                            op0=ALU.mult, op1=ALU.add))
                                free(bk)
                            dve.sem_inc(S["out_ready"], 1)
                elif op == "scores":
                    g, h = a
                    n = g * SLOTS + h
                    if n >= 2:
                        banks[4].full(dve, ("T", n - 2))
                        if n - 2 < SLOTS:
                            banks[5].full(dve, ("Tp", n - 2))
                    bk = banks[n % 2]
                    bk.full(dve, ("S", n))
                    c0 = (C_CAUSAL, C_CAUSAL, C_STRIDED)[g]
                    mask = con[:, c0:c0 + P].unsqueeze(1).to_broadcast([P, NT, P])
                    ch.link(STT(out=Sx[:, n % 2, 0:NT, :], in0=bk.tile[:, :].rearrange("p (t c) -> p t c", t=NT), scalar=SCALE,
                                in1=mask, op0=ALU.mult, op1=ALU.add))
                    free(bk)
                    ch.link(V.tensor_reduce(mst[:, g, :, h], Sx[:, n % 2, 0:NT, :], AX.X, ALU.max))
                    if g == 0:
                        bk = banks[2 + n % 2]
                        bk.full(dve, ("Sp", n))
                        mask = con[:, C_PREV:C_PREV + P].unsqueeze(1).to_broadcast([P, NT - 1, P])
                        ch.link(STT(out=Sx[:, n % 2, NT:2 * NT - 1, :],
                                    in0=bk.tile[:, 0:(NT - 1) * P].rearrange("p (t c) -> p t c", t=NT - 1), scalar=SCALE,
                                    in1=mask, op0=ALU.mult, op1=ALU.add))
                        free(bk)
                        ch.link(V.tensor_reduce(mx2[:, n % 2, :], Sx[:, n % 2, NT:2 * NT - 1, :], AX.X, ALU.max))
                        ch.link(TT(mst[:, g, 1:NT, h], mst[:, g, 1:NT, h], mx2[:, n % 2, :], ALU.max))
                    TS(nm[:, n % 2, :], mst[:, g, :, h], -1.0, None, ALU.mult).then_inc(S["neg_max_ready"], 1)
                elif op == "probs":
                    g, h = a
                    n = g * SLOTS + h
                    if g == 0:
                        dve.wait_ge(S["probs_ready"], n + 1)
                        ch.link(TT(lst[:, g, 1:NT, h], lst[:, g, 1:NT, h], l2[:, n % 2, :], ALU.add))
                        banks[5].full(dve, ("Tp", n))
                        if n >= 2:
                            pv_done(dve, n - 2)
                        V.tensor_copy(PT[:, n % 2, NT:2 * NT - 1, :], banks[5].tile[:, 0:(NT - 1) * P].rearrange("p (t c) -> p t c", t=NT - 1))\
                            .then_inc(S["prev_probs_turned"], 1)
                        dve.wait_ge(S["prev_probs_turned"], n + 1)
                        free(banks[5])
                    if n == NG * SLOTS - 1:
                        dve.wait_ge(S["probs_ready"], n + 1)
                        dve.sem_inc(S["maxima_sums_ready"], 1)
                elif op == "turnq":
                    ch.link(V.memset(qd[:, :, :], 0.0))
                    banks[5].full(dve, ("qT",))
                    for x in range(2):
                        o = x * HD
                        ch.link(V.tensor_copy(qd[o:o + HD, :, x], banks[5].tile[o:o + HD, 0:NG * HP * B]))
                    free(banks[5])
                    dve.sem_inc(S["sample_q_ready"], 1)
                elif op == "merge":
                    for g in range(NG):
                        for dst, bk, key in ((mT, merge_banks[g], "mt"), (lT, merge_banks[NG + g], "lt")):
                            bk.full(dve, (key, g))
                            pat = "p (j t) -> p t j" if g > 0 else "p (t j) -> p t j"
                            ch.link(V.tensor_copy(dst[:, g, :].rearrange(pat, t=NT),
                                                  bk.tile[0:SLOTS, :].rearrange("p (t j) -> p t j", t=NT)))
                            free(bk)
                    ch.link(TT(mm_[:, :], mT[:, 0, :], mT[:, 1, :], ALU.max))
                    ch.link(TT(mm_[:, :], mm_[:, :], mT[:, 2, :], ALU.max))
                    for g in range(NG):
                        TT(mT[:, g, :], mT[:, g, :], mm_[:, :], ALU.subtract).then_inc(S["merge_exponents"], 1)
                    dve.wait_ge(S["merge_exps"], 1)
                    ch.link(TT(den[:, :], mT[:, 0, :], lT[:, 0, :], ALU.mult))
                    for g in range(1, NG):
                        dve.wait_ge(S["merge_exps"], g + 1)
                        ch.link(TT(dtmp[:, :], mT[:, g, :], lT[:, g, :], ALU.mult))
                        ch.link(TT(den[:, :], den[:, :], dtmp[:, :], ALU.add))
                    ch.link(V.reciprocal(den[:, :], den[:, :]))
                    for g in range(NG):
                        ch.link(TT(mT[:, g, :], mT[:, g, :], den[:, :], ALU.mult))
                        ch.link(V.tensor_copy(mH_[:, g, :], mT[:, g, :]))
                        ch.link(TT(mL_[:, g, :], mT[:, g, :], mH_[:, g, :].bitcast(F32), ALU.subtract))
                    dve.wait_ge(S["selectors_loaded"], 16)
                    V.tensor_copy(selR[:, :, :], sel[:, :, :]).then_inc(S["merge_weights"], 1)
                elif op == "spread":
                    dve.wait_ge(S["head_pair_out"], NG * HP)
                    hp, g = divmod(a[0], NG)
                    bk = spread_bank(a[0])
                    bk.full(dve, ("wb", hp, g))
                    ch.link(TT(mtmp[:, :] if g else oT[:, hp, B:R], oU[:, g, hp, :], bk.tile[:, :], ALU.mult))
                    free(bk)
                    if g:
                        ch.link(TT(oT[:, hp, B:R], oT[:, hp, B:R], mtmp[:, :], ALU.add))
                elif op == "ownkeys":
                    ch.link(TT(pself[:, :, :], qS[:, 0, :, :], qS[:, 1, :, :], ALU.mult))
                    V.tensor_reduce(sself[:, :, :], pself[:, :, :].rearrange("p g (h d) -> p g h d", h=SLOTS), AX.X, ALU.add)\
                        .then_inc(S["self_scores_ready"], 1)
                elif op == "samplemax":
                    banks[6].full(dve, ("sS",))
                    V.tensor_copy(sS[:, :, :, :].rearrange("p g h b -> p (g h b)"), banks[6].tile[:, 0:NG * SLOTS * B])\
                        .then_inc(S["sample_scores_kept"], 1)
                    dve.wait_ge(S["sample_scores_kept"], 1)
                    free(banks[6])
                    banks[4].full(dve, ("sT",))
                    ch.link(V.tensor_reduce(Ms[:, :], banks[4].tile[0:SLOTS * B, 0:NG * NKEYS + NG], AX.X, ALU.max))
                    TS(nMs[:, :], Ms[:, :], -SCALE, None, ALU.mult).then_inc(S["sample_exponents"], 1)
                    dve.wait_ge(S["sample_exps"], 1)
                    ch.link(V.reciprocal(ls[:, :], ls[:, :]))
                    TS(pS[:, :], pS[:, :], ls[:, 0:1], None, ALU.mult).then_inc(S["sample_probs"], 1)
                elif op == "sampleprobs":
                    banks[5].full(dve, ("pTs",))
                    n = NG * SLOTS * B
                    ch.link(V.tensor_copy(pTs[:, :, :, :].rearrange("p g h b -> p (g h b)"), banks[5].tile[:, 0:n]))
                    ch.link(V.tensor_copy(pB[:, :, :].rearrange("p h g -> p (h g)"), banks[5].tile[0:B, n:n + SLOTS * NG]))
                    free(banks[5])
                    for g in range(NG):
                        ins = TT(SD[:, g, :, :], con[0:B, C_ID:C_ID + B].unsqueeze(1).to_broadcast([B, SLOTS, B]),
                                 pB[:, :, g:g + 1].to_broadcast([B, SLOTS, B]), ALU.mult)
                    ins.then_inc(S["sample_probs_turned"], 1)
                elif op == "gated":
                    banks[7].full(dve, ("so",))
                    ch.link(V.tensor_copy(oT[:, :, 0:B], banks[7].tile[:, 0:HP * B].rearrange("p (h b) -> p h b", b=B)))
                    free(banks[7])
                    STT(out=oT[:, :, :], in0=oT[:, :, :], scalar=0.5, in1=zg[:, :, :], op0=ALU.mult, op1=ALU.mult)
                elif op == "dt":
                    i = ITEM_AT["dt", 0]
                    for hf in range(2):
                        bk = cm_bank(i, 0, hf)
                        bk.full(dve, ("cm", i, 0, hf))
                        ch.link(TS(da[0][:, hf * HALF:(hf + 1) * HALF], bk.tile[0:HEADS, 0:HALF], par[0:HEADS, PW_DTB:PW_DTB + 1], None, ALU.add))
                        free(bk)
                    STT(out=da[1][:, :], in0=da[0][:, :], scalar=-1.0, in1=da[0][:, :], op0=ALU.mult, op1=ALU.min).then_inc(S["dt_operands"], 1)
                    dve.wait_ge(S["dt_activations"], 2)
                    TS(da[3][:, :], da[2][:, :], 1.0, None, ALU.add).then_inc(S["dt_operands"], 1)
                    dve.wait_ge(S["dt_operands"], 2)
                    ch.link(TS(da[5][:, :], da[3][:, :], -1.0, None, ALU.add))
                    ch.link(TS(da[6][:, :], da[5][:, :], 0.0, None, ALU.is_equal))
                    ch.link(TT(da[6][:, :], da[6][:, :], da[2][:, :], ALU.mult))
                    ch.link(TS(da[5][:, :], da[5][:, :], 1e-30, None, ALU.max))
                    ch.link(V.reciprocal(da[5][:, :], da[5][:, :]))
                    ch.link(TT(da[5][:, :], da[5][:, :], da[2][:, :], ALU.mult))
                    dve.wait_ge(S["dt_activations"], 3)
                    ch.link(TT(da[5][:, :], da[5][:, :], da[4][:, :], ALU.mult))
                    ch.link(TT(da[5][:, :], da[5][:, :], da[6][:, :], ALU.add))
                    ch.link(STT(out=dtT[:, :], in0=da[0][:, :], scalar=0.0, in1=da[5][:, :], op0=ALU.max, op1=ALU.add))
                    ch.link(TS(da[7][:, :], dtT[:, :], Acol[:, 0:1], -1.0, ALU.mult, ALU.mult))
                    ch.link(V.memset(onesm[:, 0:T:P], 0.0))
                    ch.link(V.tensor_copy(dsS[:, B:2 * B], dtT[:, 0:B]))
                    ch.link(V.tensor_tensor_scan(acT[:, :], onesm[:, :], da[7][:, B:R], 0.0, ALU.mult, ALU.add))
                    ac3 = acT[:, :].rearrange("p (c l) -> p c l", c=NT)
                    TT(decT[:, :].rearrange("p (c l) -> p c l", c=NT), ac3[:, :, P - 1:P].to_broadcast([HEADS, NT, P]), ac3,
                       ALU.subtract).then_inc(S["dt_operands"], 1)
                    ch.link(V.tensor_copy(acH[:, :], acT[:, :]))
                    V.tensor_copy(idR[:, :], con[0:HEADS, C_ID:C_ID + HEADS])
                    ch.link(TT(acL[:, :], acT[:, :], acH[:, :].bitcast(F32), ALU.subtract))
                    dve.sem_inc(S["ac_parts_ready"], 1)
                elif op == "dtrows":
                    banks[4].full(dve, ("dtr",))
                    ch.link(V.tensor_copy(dtrm[:, :, :, :], banks[4].tile[:, 0:NT * 3 * HEADS].rearrange("p (c q h) -> p c q h", c=NT, q=3)))
                    free(banks[4])
                    ch.link(TS(nac[:, :, :], dtrm[:, :, 1, :], -1.0, None, ALU.mult))
                    banks[5].full(dve, ("dsb",))
                    ch.link(V.tensor_copy(dsb[:, :, :], banks[5].tile[:, 0:UNITS * 2 * B].rearrange("p (u b) -> p u b", u=UNITS)))
                    dve.sem_inc(S["sample_dt_ready"], 1)
                    free(banks[5])
                elif op == "bc":
                    g = a[0]
                    if g > 0:
                        banks[7].full(dve, ("y", 4 * g - 1))
                    banks[7].full(dve, ("CB", g))
                    ch.link(TT(CBm[:, :, :], banks[7].tile[:, :].rearrange("p (c l) -> p c l", c=NT),
                               con[:, C_TRI:C_TRI + P].unsqueeze(1).to_broadcast([P, NT, P]), ALU.mult))
                    free(banks[7])
                elif op == "ssdA":
                    u = a[0]
                    h0 = 2 * u
                    if u > 0:
                        banks[7].full(dve, ("y", u - 1))
                    for e in range(2):
                        bk = banks[5 + e]
                        dve.wait_ge(S["chunk_exps_ready"], 2 * u + e + 1)
                        TT(Lb[:, e, :, :], bk.tile[:, :].rearrange("p (c l) -> p c l", c=NT),
                           dtrm[:, :, 1, h0 + e:h0 + e + 1].to_broadcast([P, NT, P]), ALU.min).then_inc(S["decay_args_ready"], 1)
                        dve.wait_ge(S["decay_args_ready"], 2 * u + e + 1)
                        free(bk)
                    banks[4].full(dve, ("xT", u))
                    x4 = "p c (e d) -> p c e d"
                    ch.link(TT(xdt[:, :, :].rearrange(x4, e=2), banks[4].tile[:, :].rearrange("p (c e d) -> p c e d", c=NT, e=2),
                               dtrm[:, :, 0, h0:h0 + 2].unsqueeze(3).to_broadcast([P, NT, 2, HD]), ALU.mult))
                    free(banks[4])
                    TT(xdec[:, :, :].rearrange(x4, e=2), xdt[:, :, :].rearrange(x4, e=2),
                       dtrm[:, :, 2, h0:h0 + 2].unsqueeze(3).to_broadcast([P, NT, 2, HD]), ALU.mult).then_inc(S["xdt_ready"], 1)
                    for e in range(2):
                        dve.wait_ge(S["decay_matrix_ready"], 2 * u + e + 1)
                        TT(Lb[:, e, :, :], Lb[:, e, :, :], CBm[:, :, :], ALU.mult).then_inc(S["masked_cb_ready"], 1)
                elif op == "ssdS":
                    u = a[0]
                    xs = xu[:, u % 3, :]
                    TT(xds[:, :], xs[:, CS:CONV:TAPS], dsb[:, u, B:2 * B], ALU.mult).then_inc(S["sample_xdt_ready"], 1)
                    banks[4].full(dve, ("st", u))
                    if u >= 2:
                        dve.wait_ge(S[f"state_stored{u % 2}"], 16 * (u // 2))
                    dve.wait_ge(S["scaled_c_ready"], 2 * (u + 1))
                    hh = hst[:, u % 2, :, :]
                    ch.link(V.tensor_copy(hh[:, 0, :], banks[4].tile[:, 0:P]))
                    for c in range(1, NT):
                        for e in range(2):
                            o = e * HD
                            ins = STT(out=hh[:, c, o:o + HD], in0=hh[:, c - 1, o:o + HD], scalar=dcol[:, e, c:c + 1],
                                      in1=banks[4].tile[:, c * P + o:c * P + o + HD], op0=ALU.mult, op1=ALU.add)
                            if e == 1 and c == NT - 2:
                                ins.then_inc(S["states_before_ready"], 1)
                                dve.wait_ge(S["states_before_ready"], u + 1)
                            elif c < NT - 1:
                                ch.link(ins)
                    ins.then_inc(S["last_state_ready"], 1)
                    dve.wait_ge(S["last_state_ready"], u + 1)
                    free(banks[4])
                    dve.wait_ge(S["sample_decayed"], u + 1)
                    dve.wait_ge(S["sample_xb_ready"], u + 1)
                    TT(stt_[:, u % 2, :, :], stt_[:, u % 2, :, :], tt[:, :, :], ALU.add).then_inc(S["sample_state_ready"], 1)
                elif op == "ssdZ":
                    u = a[0]
                    xs = xu[:, u % 3, :]
                    dcl = par[:, PW_D + u:PW_D + u + 1]
                    if u > 0:
                        dve.wait_ge(S["y_gated"], u)
                    dve.wait_ge(S["sample_state_c_ready"], u + 1)
                    ch.link(V.tensor_reduce(y8[:, :], tt[:, :, :], AX.X, ALU.add))
                    ch.link(STT(out=yb[:, 0:B], in0=xs[:, CS:CONV:TAPS], scalar=dcl, in1=y8[:, :], op0=ALU.mult, op1=ALU.add))
                    banks[7].full(dve, ("y", u))
                    ch.link(STT(out=yb[:, B:R], in0=xs[:, 0:T], scalar=dcl, in1=banks[7].tile[:, :], op0=ALU.mult, op1=ALU.add))
                    free(banks[7])
                    dve.wait_ge(S["z_silu_ready"], u + 1)
                    STT(out=ygn[:, u, :], in0=yb[:, :], scalar=0.5, in1=zs[:, u % 2, :], op0=ALU.mult, op1=ALU.mult).then_inc(S["y_gated"], 1)
                elif op == "gscale":
                    g = a[0]
                    dve.wait_ge(S["scaled_rows_ready"], KD + g + 1)
                    ch.link(V.reciprocal(grs[:, :], grs[:, :]))
                    for k in range(PER_GROUP):
                        u = g * PER_GROUP + k
                        ins = STT(out=ygn[:, u, :], in0=ygn[:, u, :], scalar=par[:, PW_SNORM + u:PW_SNORM + u + 1], in1=grs[:, :],
                                  op0=ALU.mult, op1=ALU.mult)
                    ins.then_inc(S["y_normed"], 1)
                elif op == "parts":
                    for u in range(UNITS):
                        dve.wait_ge(S["y_high_ready"], u + 1)
                        TT(yL[:, u, :], ygn[:, u, :], yH[:, u, :].bitcast(F32), ALU.subtract).then_inc(S["y_low_ready"], 1)
                    for hp in range(HP):
                        dve.wait_ge(S["o_high_ready"], hp + 1)
                        TT(oL[:, hp, :], oT[:, hp, :], oH[:, hp, :].bitcast(F32), ALU.subtract).then_inc(S["o_low_ready"], 1)
                elif op == "mix":
                    for s in range(2):
                        k = 2 * a[0] + s
                        dve.wait_ge(S["mix_high_ready"], k + 1)
                        TT(mL[:, k, :], mix[:, k, :], mH[:, k, :].bitcast(F32), ALU.subtract).then_inc(S["mix_low_ready"], 1)


def _tables():
    con = np.zeros((P, NCONST), np.float32)
    q, k = np.arange(P)[:, None], np.arange(P)[None, :]
    low = np.float32(-1e30)
    con[:, C_ID:C_ID + P] = np.eye(P)
    con[:, C_CAUSAL:C_CAUSAL + P] = np.where(k <= q, 0, low)
    con[:, C_PREV:C_PREV + P] = np.where(k >= q, 0, low)
    con[:, C_STRIDED:C_STRIDED + P] = np.where((k <= q) & ((q - k) % (DILATIONS[2] // NT) == 0), 0, low)
    con[:, C_TRI:C_TRI + P] = k >= q
    con[np.arange(B), C_PLACE + (SLOTS - 1) * B + np.arange(B)] = 1
    half = HD // 2
    inv = (10000.0 ** (-np.arange(half) / half)).astype(np.float32)
    p = np.arange(P)
    pos = [P * t + p for t in range(NT)] + [NT * p + t for t in range(NT)] + [np.full(P, WINDOWS[-1])]
    for t, x in enumerate(pos):
        ang = x.astype(np.float32)[:, None] * inv[None, :]
        con[:, C_COS + t * half:C_COS + (t + 1) * half] = np.cos(ang)
        con[:, C_SIN + t * half:C_SIN + (t + 1) * half] = np.sin(ang)
    sel = np.zeros((HEADS, UNITS, P), np.float32)
    for h in range(HEADS):
        sel[h, h // 2, (h % 2) * HD:(h % 2 + 1) * HD] = 1
    return con, sel


def kernel(**inputs):
    from concourse import bacc
    from concourse.bass_utils import run_bass_kernel_spmd

    x = {n: np.ascontiguousarray(v) for n, v in inputs.items()}
    f = np.float32

    def rows_to_tiles(a, n):
        return np.ascontiguousarray(np.swapaxes(a.reshape(n, P, *a.shape[1:]), 0, 1))

    w_in, w_ssd, w_att, w_out = x["w_in"][0], x["w_ssd_br"][0], x["w_att_br"][0], x["w_out"][0]
    wpack = np.zeros((len(ITEMS), P, SLOT), f)
    for i, it in enumerate(ITEMS):
        kind, j = it[0], it[1]
        if kind == "rm":
            c = OFF[it[2]] + j * DATT
            a = w_in[512 * it[3]:512 * (it[3] + 1), c:c + DATT]
        elif kind == "dt":
            a = np.zeros((D, P), f)
            a[:, :HEADS] = w_in[:, OFF["dt"]:OFF["dt"] + HEADS]
        elif kind == "bc":
            a = np.concatenate([w_in[:, o + j * P:o + (j + 1) * P] for o in (OFF_B, OFF_C)], axis=1)
        elif kind == "bs":
            a = w_ssd[:, j * P:(j + 1) * P]
        elif kind == "ba":
            a = w_att[:, j * 512:(j + 1) * 512]
        elif kind == "wo":
            a = w_out[:, j * 2 * P:(j + 1) * 2 * P]
        else:
            c = {"x": OFF_X}.get(kind, OFF.get(kind)) + j * 2 * P
            a = w_in[:, c:c + 2 * P]
        k = a.shape[0] // P
        wpack[i, :, :k * a.shape[1]] = rows_to_tiles(a, k).reshape(P, -1)

    par = np.zeros((P, NPARAM), f)
    par[:, PW_NORM:PW_CONV] = x["norm_w"][0].reshape(KD, P).T
    par[:, PW_CONV:PW_CONVB] = x["conv_w"][0].reshape(TAPS, XU, P).transpose(2, 1, 0).reshape(P, -1)
    par[:, PW_CONVB:PW_SNORM] = x["conv_b"][0].reshape(XU, P).T
    par[:, PW_SNORM:PW_D] = x["ssd_norm_w"][0].reshape(UNITS, P).T
    par[:, PW_D:PW_DTB] = np.repeat(x["d_skip"][0], HD).reshape(UNITS, P).T
    par[:HEADS, PW_DTB] = x["dt_bias"][0]
    par[:HEADS, PW_ALOG] = x["a_log"][0]
    par[:, PW_QW:PW_KW] = x["q_norm_w"][0]
    par[:, PW_KW:NPARAM] = x["k_norm_w"][0]
    con, sel = _tables()

    rows = np.concatenate([x["x_sample"][:, 0], x["x_prompt"][0]], axis=0)
    arrays = {
        "in_xT": rows_to_tiles(np.ascontiguousarray(rows.T), KD),
        "in_weights": wpack,
        "in_params": par,
        "in_consts": con,
        "in_sel": sel,
        "in_state_conv": np.ascontiguousarray(x["state_conv"][0].reshape(B, TAPS - 1, XU, P).transpose(3, 2, 0, 1)),
        "in_state_ssm": np.ascontiguousarray(x["state_ssm"][0].reshape(B, UNITS, P, NSTATE).transpose(1, 2, 0, 3)),
    }
    for w in WINDOWS:
        arrays[f"in_cache{w}"] = x[f"cache_kv_w{w}"][0].reshape(B, w, 2 * DATT)
    outs = {"out_y": (P, KD, R), "out_tail": (P, XU, TAIL), "out_ssm_p": (UNITS, P, P), "out_ssm_s": (UNITS, P, B, P)}
    for w in WINDOWS:
        outs[f"out_kvp{w}"] = (min(w, T), 2 * DATT)
        outs[f"out_kvs{w}"] = (B, w, 2 * DATT)

    nc = bacc.Bacc("TRN2", target_bir_lowering=False, num_devices=1)
    ap = {n: nc.dram_tensor(n, a.shape, F32, kind="ExternalInput").ap() for n, a in arrays.items()}
    ap.update({n: nc.dram_tensor(n, s, F32, kind="ExternalOutput").ap() for n, s in outs.items()})
    hybrid_kernel(nc, ap["in_xT"], ap["in_weights"], ap["in_params"], ap["in_consts"], ap["in_sel"],
                  ap["in_state_conv"], ap["in_state_ssm"], [ap[f"in_cache{w}"] for w in WINDOWS],
                  ap["out_y"], ap["out_tail"], ap["out_ssm_p"], [ap[f"out_kvp{w}"] for w in WINDOWS],
                  ap["out_ssm_s"], [ap[f"out_kvs{w}"] for w in WINDOWS])
    r = run_bass_kernel_spmd(nc, [arrays], core_ids=[0]).results[0]

    y = np.swapaxes(r["out_y"], 0, 1).reshape(D, R).T
    tail = np.swapaxes(r["out_tail"], 0, 1).reshape(DXBC, TAIL)
    conv_p = tail[:, :TAPS - 1].T.reshape(1, 1, TAPS - 1, DXBC)
    conv_s = tail[:, TAPS - 1:].reshape(DXBC, B, TAPS - 1).transpose(1, 2, 0).reshape(1, B, TAPS - 1, DXBC)
    ssm_p = np.swapaxes(r["out_ssm_p"], 1, 2).reshape(1, 1, HEADS, HD, NSTATE)
    ssm_s = r["out_ssm_s"].transpose(2, 0, 1, 3).reshape(1, B, HEADS, HD, NSTATE)
    kvp = [r[f"out_kvp{w}"].reshape(1, 1, min(w, T), 2, SLOTS, HD) for w in WINDOWS]
    kvs = [r[f"out_kvs{w}"].reshape(1, B, w, 2, SLOTS, HD) for w in WINDOWS]
    out = [y[B:].reshape(1, T, D), y[:B].reshape(B, 1, D), conv_p, ssm_p, *kvp, conv_s, ssm_s, *kvs]
    return tuple(np.ascontiguousarray(o) for o in out)
```
